# Optimizing a Trainium2 kernel written in Bass

```python
import math
import jax, jax.numpy as jnp
from jax import lax
import numpy as np
import jax
import jax.numpy as jnp

D_MODEL = 1024
BATCH = 1
SEQ = 512
DEPTH = 1

MIX_WIDTH = D_MODEL
ATTN_WIDTH = MIX_WIDTH // 2
POOL_WIDTH = MIX_WIDTH - ATTN_WIDTH
N_DIFF_HEADS = 4
DIFF_HEAD_DIM = ATTN_WIDTH // (2 * N_DIFF_HEADS)
DIFF_VALUE_DIM = 2 * DIFF_HEAD_DIM
ROT_DIM = DIFF_HEAD_DIM // 4
ROPE_THETA = 500000.0
Q_BLOCK = 128
POOL_WINDOWS = (2, 4, 8, 16)
N_POOL_GROUPS = len(POOL_WINDOWS)
POOL_GROUP_DIM = POOL_WIDTH // N_POOL_GROUPS
IN_COLS = 3 * ATTN_WIDTH + POOL_WIDTH
N_EXPERT_GROUPS = 4
EXPERTS_PER_GROUP = 8
N_EXPERTS = N_EXPERT_GROUPS * EXPERTS_PER_GROUP
TOP_K_IN_GROUP = 2
D_EXPERT = D_MODEL // 2
MOE_BLOCK = 128
RMS_EPS = 1e-6
N_MOD = 6


def rms_norm(x, g):
    xf = x.astype(jnp.float32)
    y = xf * lax.rsqrt(jnp.mean(xf * xf, axis=-1, keepdims=True) + RMS_EPS)
    return (y * g.astype(jnp.float32)).astype(x.dtype)

def lambda_init_for(layer_idx):
    return 0.8 - 0.6 * math.exp(-0.3 * layer_idx)

def rope_tables(seq_len):
    pos = jnp.arange(seq_len, dtype=jnp.float32)
    inv_freq = ROPE_THETA ** (-jnp.arange(0, ROT_DIM, 2, dtype=jnp.float32) / ROT_DIM)
    ang = pos[:, None] * inv_freq[None, :]
    return jnp.cos(ang), jnp.sin(ang)

def apply_partial_rope(t, cos, sin):
    half = ROT_DIM // 2
    cs = cos[None, :, None, None, :].astype(t.dtype)
    sn = sin[None, :, None, None, :].astype(t.dtype)
    t1 = t[..., :half]
    t2 = t[..., half:ROT_DIM]
    return jnp.concatenate([t1 * cs - t2 * sn, t2 * cs + t1 * sn, t[..., ROT_DIM:]], axis=-1)

def diff_attention(q, k, v, lam, subln_g, lambda_init):
    B, S = q.shape[0], q.shape[1]
    cos, sin = rope_tables(S)
    q = apply_partial_rope(q, cos, sin) * (DIFF_HEAD_DIM ** -0.5)
    k = apply_partial_rope(k, cos, sin)
    nqb = S // Q_BLOCK
    qb = q.reshape(B, nqb, Q_BLOCK, N_DIFF_HEADS, 2, DIFF_HEAD_DIM).transpose(1, 0, 3, 4, 2, 5)
    kt = k.transpose(0, 2, 3, 1, 4)
    vt = v.transpose(0, 2, 1, 3)

    def block(qblk):
        s = jnp.einsum('bhcqd,bhckd->bhcqk', qblk, kt).astype(jnp.float32)
        a = jax.nn.softmax(s, axis=-1)
        w = a[:, :, 0] - lam * a[:, :, 1]
        return jnp.einsum('bhqk,bhkv->bhqv', w.astype(vt.dtype), vt)

    o = lax.map(block, qb)
    o = o.transpose(1, 0, 3, 2, 4).reshape(B, S, N_DIFF_HEADS, DIFF_VALUE_DIM)
    o = rms_norm(o, subln_g) * (1.0 - lambda_init)
    return o.reshape(B, S, N_DIFF_HEADS * DIFF_VALUE_DIM)

def multiscale_pool(u, w_pool, pool_scale):
    B, S = u.shape[0], u.shape[1]
    uf = u.astype(jnp.float32)
    cs = jnp.concatenate([jnp.zeros_like(uf[:, :1]), jnp.cumsum(uf, axis=1)], axis=1)
    pos = jnp.arange(S)
    outs = []
    for g, w in enumerate(POOL_WINDOWS):
        left = w // 2
        right = w - 1 - left
        lo = jnp.clip(pos - left, 0, S)
        hi = jnp.clip(pos + right + 1, 0, S)
        cnt = (hi - lo).astype(jnp.float32)
        mean = (cs[:, hi, g] - cs[:, lo, g]) / cnt[None, :, None]
        outs.append(mean - uf[:, :, g])
    d = jnp.stack(outs, axis=2).astype(u.dtype)
    y = jnp.einsum('bsgc,gcd->bsgd', d, w_pool) * pool_scale
    return y.reshape(B, S, N_POOL_GROUPS * POOL_GROUP_DIM)

def grouped_expert_ffn(xt, flat_e, flat_tok, flat_w, w_gate, w_up, w_down):
    N, D = xt.shape
    NK = flat_e.shape[0]
    order = jnp.argsort(flat_e)
    sorted_e = flat_e[order]
    counts = jax.ops.segment_sum(jnp.ones((NK,), jnp.int32), flat_e, num_segments=N_EXPERTS)
    starts = jnp.cumsum(counts) - counts
    padded = ((counts + MOE_BLOCK - 1) // MOE_BLOCK) * MOE_BLOCK
    pad_ends = jnp.cumsum(padded)
    pad_starts = pad_ends - padded
    rank = jnp.arange(NK, dtype=jnp.int32) - starts[sorted_e]
    dest = pad_starts[sorted_e] + rank
    n_blocks = -(-NK // MOE_BLOCK) + N_EXPERTS
    P = n_blocks * MOE_BLOCK
    row_tok = jnp.full((P,), N, jnp.int32).at[dest].set(flat_tok[order])
    row_w = jnp.zeros((P,), jnp.float32).at[dest].set(flat_w[order])
    block_e = jnp.minimum(
        jnp.searchsorted(pad_ends, jnp.arange(n_blocks, dtype=jnp.int32) * MOE_BLOCK, side='right'),
        N_EXPERTS - 1).astype(jnp.int32)
    x_pad = jnp.concatenate([xt, jnp.zeros((1, D), xt.dtype)], axis=0)
    xb = x_pad[row_tok].reshape(n_blocks, MOE_BLOCK, D)

    def expert_block(args):
        xblk, e = args
        hid = jax.nn.silu(xblk @ w_gate[e]) * (xblk @ w_up[e])
        return hid @ w_down[e]

    yb = lax.map(expert_block, (xb, block_e)).reshape(P, D)
    y = jnp.zeros((N + 1, D), jnp.float32).at[row_tok].add(yb.astype(jnp.float32) * row_w[:, None])
    return y[:N].astype(xt.dtype)

def hierarchical_moe(h, w_rg, b_rg, w_re, b_re, w_gate, w_up, w_down):
    B, S, D = h.shape
    N = B * S
    xt = h.reshape(N, D)
    g_logits = (xt @ w_rg).astype(jnp.float32) + b_rg.astype(jnp.float32)
    g_prob = jax.nn.softmax(g_logits, axis=-1)
    _, g_idx = lax.top_k(g_logits, 1)
    g_sel = g_idx[:, 0]
    tok = jnp.arange(N)
    g_p = g_prob[tok, g_sel]
    e_logits = ((xt @ w_re).astype(jnp.float32) + b_re.astype(jnp.float32)).reshape(N, N_EXPERT_GROUPS, EXPERTS_PER_GROUP)
    e_in = e_logits[tok, g_sel]
    e_prob = jax.nn.softmax(e_in, axis=-1)
    top_p, top_i = lax.top_k(e_prob, TOP_K_IN_GROUP)
    top_p = top_p / jnp.sum(top_p, axis=-1, keepdims=True)
    weights = g_p[:, None] * top_p
    expert_id = (g_sel[:, None] * EXPERTS_PER_GROUP + top_i).astype(jnp.int32)
    flat_tok = jnp.repeat(jnp.arange(N, dtype=jnp.int32), TOP_K_IN_GROUP)
    y = grouped_expert_ffn(xt, expert_id.reshape(-1), flat_tok, weights.reshape(-1), w_gate, w_up, w_down)
    return y.reshape(B, S, D)

def first_inputs(seed: int = 0) -> dict:
    key = jax.random.key(seed)
    ks = jax.random.split(key, 24)
    f32 = jnp.float32
    D = D_MODEL
    nrm = lambda k, shape, s: jax.random.normal(k, shape, f32) * s
    return {
        "x": nrm(ks[0], (BATCH, SEQ, D), 1.0),
        "c": nrm(ks[1], (BATCH, D), 1.0),
        "w_ada": nrm(ks[2], (DEPTH, D, N_MOD * D), 0.3 * D ** -0.5),
        "b_ada": nrm(ks[3], (DEPTH, N_MOD * D), 0.02),
        "norm1_g": 1.0 + nrm(ks[4], (DEPTH, D), 0.02),
        "w_in": nrm(ks[5], (DEPTH, D, IN_COLS), D ** -0.5),
        "lambda_q1": nrm(ks[6], (DEPTH, DIFF_HEAD_DIM), 0.1),
        "lambda_k1": nrm(ks[7], (DEPTH, DIFF_HEAD_DIM), 0.1),
        "lambda_q2": nrm(ks[8], (DEPTH, DIFF_HEAD_DIM), 0.1),
        "lambda_k2": nrm(ks[9], (DEPTH, DIFF_HEAD_DIM), 0.1),
        "subln_g": 1.0 + nrm(ks[10], (DEPTH, DIFF_VALUE_DIM), 0.02),
        "w_pool": nrm(ks[11], (DEPTH, N_POOL_GROUPS, POOL_GROUP_DIM, POOL_GROUP_DIM), POOL_GROUP_DIM ** -0.5),
        "pool_scale": 1.0 + nrm(ks[12], (DEPTH, N_POOL_GROUPS, POOL_GROUP_DIM), 0.1),
        "w_out": nrm(ks[13], (DEPTH, MIX_WIDTH, D), MIX_WIDTH ** -0.5),
        "norm2_g": 1.0 + nrm(ks[14], (DEPTH, D), 0.02),
        "w_router_group": nrm(ks[15], (DEPTH, D, N_EXPERT_GROUPS), D ** -0.5),
        "b_router_group": nrm(ks[16], (DEPTH, N_EXPERT_GROUPS), 0.01),
        "w_router_expert": nrm(ks[17], (DEPTH, D, N_EXPERTS), D ** -0.5),
        "b_router_expert": nrm(ks[18], (DEPTH, N_EXPERTS), 0.01),
        "w_gate": nrm(ks[19], (DEPTH, N_EXPERTS, D, D_EXPERT), D ** -0.5),
        "w_up": nrm(ks[20], (DEPTH, N_EXPERTS, D, D_EXPERT), D ** -0.5),
        "w_down": nrm(ks[21], (DEPTH, N_EXPERTS, D_EXPERT, D), D_EXPERT ** -0.5),
        "final_g": 1.0 + nrm(ks[22], (D,), 0.02),
    }

def first_block(x, c, w_ada, b_ada, norm1_g, w_in, lambda_q1, lambda_k1, lambda_q2, lambda_k2,
              subln_g, w_pool, pool_scale, w_out, norm2_g, w_router_group, b_router_group,
              w_router_expert, b_router_expert, w_gate, w_up, w_down, final_g):
    B, S, D = x.shape
    A = ATTN_WIDTH
    for l in range(DEPTH):
        lambda_init = lambda_init_for(l)
        mod = jax.nn.silu(c) @ w_ada[l] + b_ada[l]
        sh1, sc1, g1, sh2, sc2, g2 = jnp.split(mod, N_MOD, axis=-1)
        h = rms_norm(x, norm1_g[l]) * (1.0 + sc1[:, None]) + sh1[:, None]
        z = h @ w_in[l]
        q = z[..., :A].reshape(B, S, N_DIFF_HEADS, 2, DIFF_HEAD_DIM)
        k = z[..., A:2 * A].reshape(B, S, N_DIFF_HEADS, 2, DIFF_HEAD_DIM)
        v = z[..., 2 * A:3 * A].reshape(B, S, N_DIFF_HEADS, DIFF_VALUE_DIM)
        u = z[..., 3 * A:].reshape(B, S, N_POOL_GROUPS, POOL_GROUP_DIM)
        lam = (jnp.exp(jnp.sum(lambda_q1[l].astype(jnp.float32) * lambda_k1[l].astype(jnp.float32)))
               - jnp.exp(jnp.sum(lambda_q2[l].astype(jnp.float32) * lambda_k2[l].astype(jnp.float32)))
               + lambda_init)
        a_out = diff_attention(q, k, v, lam, subln_g[l], lambda_init)
        p_out = multiscale_pool(u, w_pool[l], pool_scale[l])
        mix = jnp.concatenate([a_out, p_out], axis=-1) @ w_out[l]
        x = x + g1[:, None] * mix
        h = rms_norm(x, norm2_g[l]) * (1.0 + sc2[:, None]) + sh2[:, None]
        y = hierarchical_moe(h, w_router_group[l], b_router_group[l], w_router_expert[l],
                             b_router_expert[l], w_gate[l], w_up[l], w_down[l])
        x = x + g2[:, None] * y
    return rms_norm(x, final_g)


DEPTH_2 = 2

F32 = jnp.float32

GDN_HEADS = 6
GDN_DK = 64
GDN_DV = 64
GDN_CONV = 5
GDN_CHUNK = 64
GDN_QK_W = GDN_HEADS * GDN_DK
GDN_W = GDN_HEADS * GDN_DV
GDN_QKV_W = 2 * GDN_QK_W + GDN_W

MLA_HEADS = 6
MLA_NOPE = 64
MLA_ROPE = 32
MLA_V = 64
MLA_Q_RANK = 192
MLA_KV_RANK = 128
MLA_QBLOCK = 128
ROPE_THETA_2 = 10000.0
MLA_W = MLA_HEADS * MLA_V

RWKV_HEADS = 4
RWKV_HD = 64
RWKV_DECAY_LORA = 64
RWKV_ICLR_LORA = 64
RWKV_W = RWKV_HEADS * RWKV_HD
RWKV_SHIFT_W = 3 * RWKV_W + RWKV_DECAY_LORA + RWKV_ICLR_LORA
RWKV_LN_EPS = 64e-5

D_MIX = GDN_W + MLA_W + RWKV_W
NORM_EPS = 1e-6

IN_LAYOUT = (
    ('gate', D_MIX),
    ('gdn_q', GDN_QK_W), ('gdn_k', GDN_QK_W), ('gdn_v', GDN_W),
    ('gdn_a', 2 * GDN_HEADS), ('gdn_b', 2 * GDN_HEADS),
    ('mla_cq', MLA_Q_RANK), ('mla_ckv', MLA_KV_RANK), ('mla_kr', MLA_ROPE),
    ('rw_r', RWKV_W), ('rw_k', RWKV_W), ('rw_v', RWKV_W),
    ('rw_wd', RWKV_DECAY_LORA), ('rw_ad', RWKV_ICLR_LORA),
)
N_IN = sum(width for _, width in IN_LAYOUT)


def split_columns(p):
    cols = {}
    off = 0
    for name, width in IN_LAYOUT:
        cols[name] = p[..., off:off + width]
        off += width
    return cols

def rms_norm_2(x, g, eps=NORM_EPS):
    xf = x.astype(F32)
    y = xf * lax.rsqrt(jnp.mean(xf * xf, axis=-1, keepdims=True) + eps)
    return (y * g.astype(F32)).astype(x.dtype)

def l2_normalize(x, eps=1e-6):
    xf = x.astype(F32)
    return xf * lax.rsqrt(jnp.sum(xf * xf, axis=-1, keepdims=True) + eps)

def centred_depthwise_conv(x, w):
    pad = w.shape[0] // 2
    return lax.conv_general_dilated(
        x, w[:, None, :].astype(x.dtype), window_strides=(1,), padding=[(pad, pad)],
        dimension_numbers=('NWC', 'WIO', 'NWC'), feature_group_count=x.shape[-1])

def centred_token_shift(x, mu):
    zeros = jnp.zeros_like(x[:, :1])
    x_prev = jnp.concatenate([zeros, x[:, :-1]], axis=1)
    x_next = jnp.concatenate([x[:, 1:], zeros], axis=1)
    return x + mu[0] * (x_prev - x) + mu[1] * (x_next - x)

def bidir_stack(t_fwd, t_bwd):
    return jnp.concatenate([t_fwd, jnp.flip(t_bwd, axis=1)], axis=0)

def bidir_merge(y):
    b = y.shape[0] // 2
    return y[:b] + jnp.flip(y[b:], axis=1)

def gated_delta_chunked(q, k, v, g, beta):
    n, l, h, dk = q.shape
    dv = v.shape[-1]
    c = GDN_CHUNK
    nc = l // c

    def chunks(t):
        return jnp.moveaxis(t.reshape((n, nc, c, h) + t.shape[3:]), 3, 1)

    q, k, v, g, beta = chunks(q), chunks(k), chunks(v), chunks(g), chunks(beta)
    cum = jnp.cumsum(g, axis=-1)
    diff = cum[..., :, None] - cum[..., None, :]
    idx = jnp.arange(c)
    incl = idx[:, None] >= idx[None, :]
    strict = idx[:, None] > idx[None, :]
    d_incl = jnp.exp(jnp.where(incl, diff, -jnp.inf))
    d_strict = jnp.where(strict, d_incl, 0.0)
    a_mat = beta[..., :, None] * jnp.einsum('nhcid,nhcjd->nhcij', k, k) * d_strict
    gam = jnp.exp(cum)
    rhs = jnp.concatenate([beta[..., None] * v, (beta * gam)[..., None] * k], axis=-1)
    sol = lax.linalg.triangular_solve(a_mat, rhs, left_side=True, lower=True, unit_diagonal=True)
    u0, w = sol[..., :dv], sol[..., dv:]
    p_intra = jnp.einsum('nhcid,nhcjd->nhcij', q, k) * d_incl
    q_g = q * gam[..., None]
    k_d = k * jnp.exp(cum[..., -1:] - cum)[..., None]
    g_end = jnp.exp(cum[..., -1])
    xs = tuple(jnp.moveaxis(t, 2, 0) for t in (w, u0, p_intra, q_g, k_d, g_end))

    def step(s, inp):
        w_c, u0_c, p_c, qg_c, kd_c, ge_c = inp
        u = u0_c - jnp.einsum('nhcd,nhde->nhce', w_c, s)
        o = jnp.einsum('nhcd,nhde->nhce', qg_c, s) + jnp.einsum('nhij,nhje->nhie', p_c, u)
        s = ge_c[..., None, None] * s + jnp.einsum('nhcd,nhce->nhde', kd_c, u)
        return s, o

    s0 = jnp.zeros((n, h, dk, dv), F32)
    _, o = lax.scan(step, s0, xs)
    return jnp.transpose(o, (1, 0, 3, 2, 4)).reshape(n, l, h, dv)

def gdn_branch(cols, conv_w, a_log, dt_bias, norm_g):
    b, l = cols['gdn_q'].shape[:2]
    qkv = jnp.concatenate([cols['gdn_q'], cols['gdn_k'], cols['gdn_v']], axis=-1)
    qkv = jax.nn.silu(centred_depthwise_conv(qkv, conv_w))
    q, k, v = jnp.split(qkv, [GDN_QK_W, 2 * GDN_QK_W], axis=-1)
    q = l2_normalize(q.reshape(b, l, GDN_HEADS, GDN_DK)) * (GDN_DK ** -0.5)
    k = l2_normalize(k.reshape(b, l, GDN_HEADS, GDN_DK))
    v = v.reshape(b, l, GDN_HEADS, GDN_DV).astype(F32)
    a = cols['gdn_a'].astype(F32).reshape(b, l, 2, GDN_HEADS)
    bt = cols['gdn_b'].astype(F32).reshape(b, l, 2, GDN_HEADS)
    g = -jnp.exp(a_log.astype(F32)) * jax.nn.softplus(a + dt_bias.astype(F32))
    beta = jax.nn.sigmoid(bt)
    o = gated_delta_chunked(
        bidir_stack(q, q), bidir_stack(k, k), bidir_stack(v, v),
        bidir_stack(g[:, :, 0], g[:, :, 1]), bidir_stack(beta[:, :, 0], beta[:, :, 1]))
    o = rms_norm_2(bidir_merge(o), norm_g)
    return o.reshape(b, l, GDN_W)

def apply_rope(x, cos, sin):
    xf = x.astype(F32)
    x1, x2 = jnp.split(xf, 2, axis=-1)
    return jnp.concatenate([x1 * cos - x2 * sin, x2 * cos + x1 * sin], axis=-1)

def mla_branch(cols, positions, q_norm_g, w_uq, kv_norm_g, w_ukv):
    b, l = cols['mla_cq'].shape[:2]
    q = (rms_norm_2(cols['mla_cq'], q_norm_g) @ w_uq).reshape(b, l, MLA_HEADS, MLA_NOPE + MLA_ROPE)
    kv = (rms_norm_2(cols['mla_ckv'], kv_norm_g) @ w_ukv).reshape(b, l, MLA_HEADS, MLA_NOPE + MLA_V)
    q_nope, q_rot = q[..., :MLA_NOPE], q[..., MLA_NOPE:]
    k_nope, v = kv[..., :MLA_NOPE], kv[..., MLA_NOPE:]
    half = MLA_ROPE // 2
    inv_freq = ROPE_THETA_2 ** (-jnp.arange(half, dtype=F32) / half)
    ang = positions.astype(F32)[..., None] * inv_freq
    cos, sin = jnp.cos(ang), jnp.sin(ang)
    q_rot = apply_rope(q_rot, cos[:, :, None], sin[:, :, None])
    k_rot = apply_rope(cols['mla_kr'], cos, sin)
    scale = (MLA_NOPE + MLA_ROPE) ** -0.5
    q = jnp.concatenate([q_nope.astype(F32), q_rot], axis=-1) * scale
    k = jnp.concatenate([k_nope.astype(F32),
                         jnp.broadcast_to(k_rot[:, :, None], (b, l, MLA_HEADS, MLA_ROPE))], axis=-1)
    v = v.astype(F32)
    nb = l // MLA_QBLOCK
    q_blocks = jnp.moveaxis(q.reshape(b, nb, MLA_QBLOCK, MLA_HEADS, MLA_NOPE + MLA_ROPE), 1, 0)

    def attend(q_blk):
        s = jnp.einsum('bqhd,bkhd->bhqk', q_blk, k)
        p = jax.nn.softmax(s, axis=-1)
        return jnp.einsum('bhqk,bkhd->bqhd', p, v)

    o = lax.map(attend, q_blocks)
    return jnp.moveaxis(o, 0, 1).reshape(b, l, MLA_W)

def to_heads(t):
    return t.reshape(t.shape[:-1] + (RWKV_HEADS, RWKV_HD))

def rwkv7_branch(cols, mu, w0, w2, a0, a2, k_k, k_a, r_k, ln_g, ln_b):
    b, l = cols['rw_r'].shape[:2]
    feats = jnp.concatenate([cols['rw_r'], cols['rw_k'], cols['rw_v'], cols['rw_wd'], cols['rw_ad']],
                            axis=-1).astype(F32)
    feats = centred_token_shift(feats, mu.astype(F32))
    r, k, v, wd, ad = jnp.split(feats, [RWKV_W, 2 * RWKV_W, 3 * RWKV_W, 3 * RWKV_W + RWKV_DECAY_LORA], axis=-1)
    w_log = -jax.nn.softplus(-(w0.astype(F32)[:, None, None]
                               + jnp.einsum('bld,edc->eblc', jnp.tanh(wd), w2.astype(F32)))) - 0.5
    decay = jnp.exp(-jnp.exp(w_log))
    a = jax.nn.sigmoid(a0.astype(F32)[:, None, None] + jnp.einsum('bld,edc->eblc', ad, a2.astype(F32)))
    kk = l2_normalize(to_heads(k * k_k.astype(F32)))
    k_mod = k[None] * (1.0 + (a - 1.0) * k_a.astype(F32))
    r_h, v_h = to_heads(r), to_heads(v)
    a_h = to_heads(a)
    xs = (
        bidir_stack(r_h, r_h),
        bidir_stack(to_heads(decay[0]), to_heads(decay[1])),
        bidir_stack(to_heads(k_mod[0]), to_heads(k_mod[1])),
        bidir_stack(v_h, v_h),
        bidir_stack(kk, kk),
        bidir_stack(a_h[0] * kk, a_h[1] * kk),
    )
    xs = tuple(jnp.moveaxis(t, 1, 0) for t in xs)

    def step(s, inp):
        r_t, w_t, k_t, v_t, kk_t, b_t = inp
        sa = jnp.einsum('nhij,nhj->nhi', s, -kk_t)
        s = s * w_t[:, :, None, :] + sa[..., None] * b_t[:, :, None, :] + v_t[..., None] * k_t[:, :, None, :]
        y = jnp.einsum('nhij,nhj->nhi', s, r_t)
        return s, y

    s0 = jnp.zeros((2 * b, RWKV_HEADS, RWKV_HD, RWKV_HD), F32)
    _, y = lax.scan(step, s0, xs)
    y = bidir_merge(jnp.moveaxis(y, 0, 1))
    mean = jnp.mean(y, axis=-1, keepdims=True)
    var = jnp.mean(jnp.square(y - mean), axis=-1, keepdims=True)
    y = ((y - mean) * lax.rsqrt(var + RWKV_LN_EPS)).reshape(b, l, RWKV_W) * ln_g.astype(F32) + ln_b.astype(F32)
    k_bonus = to_heads(0.5 * (k_mod[0] + k_mod[1]))
    bonus = jnp.sum(r_h * k_bonus * r_k.astype(F32), axis=-1, keepdims=True) * v_h
    return y + bonus.reshape(b, l, RWKV_W)

def second_inputs(seed: int = 0) -> dict:
    key = jax.random.key(seed)
    ks = jax.random.split(key, 24)

    def nrm(k, shape, scale):
        return jax.random.normal(k, shape, F32) * scale

    x = nrm(ks[0], (BATCH, SEQ, D_MODEL), 1.0)
    positions = (jnp.arange(SEQ, dtype=jnp.int32)[None, :]
                 + jax.random.randint(ks[1], (BATCH, 1), 0, 512, dtype=jnp.int32))
    norm_g = 1.0 + nrm(ks[2], (DEPTH_2, D_MODEL), 0.02)
    w_in = nrm(ks[3], (DEPTH_2, D_MODEL, N_IN), D_MODEL ** -0.5)
    gdn_conv = nrm(ks[4], (DEPTH_2, GDN_CONV, GDN_QKV_W), GDN_CONV ** -0.5)
    gdn_a_log = jnp.log(jax.random.uniform(ks[5], (DEPTH_2, 2, GDN_HEADS), F32, 1.0, 16.0))
    dt = jnp.exp(jax.random.uniform(ks[6], (DEPTH_2, 2, GDN_HEADS), F32, math.log(1e-3), math.log(1e-1)))
    gdn_dt_bias = dt + jnp.log(-jnp.expm1(-dt))
    gdn_norm_g = 1.0 + nrm(ks[7], (DEPTH_2, GDN_DV), 0.02)
    mla_q_norm_g = 1.0 + nrm(ks[8], (DEPTH_2, MLA_Q_RANK), 0.02)
    mla_w_uq = nrm(ks[9], (DEPTH_2, MLA_Q_RANK, MLA_HEADS * (MLA_NOPE + MLA_ROPE)), MLA_Q_RANK ** -0.5)
    mla_kv_norm_g = 1.0 + nrm(ks[10], (DEPTH_2, MLA_KV_RANK), 0.02)
    mla_w_ukv = nrm(ks[11], (DEPTH_2, MLA_KV_RANK, MLA_HEADS * (MLA_NOPE + MLA_V)), MLA_KV_RANK ** -0.5)
    rwkv_mu = jax.random.uniform(ks[12], (DEPTH_2, 2, RWKV_SHIFT_W), F32, 0.0, 0.5)
    rwkv_w0 = jax.random.uniform(ks[13], (DEPTH_2, 2, RWKV_W), F32, -6.0, -1.0)
    rwkv_w2 = nrm(ks[14], (DEPTH_2, 2, RWKV_DECAY_LORA, RWKV_W), 0.1)
    rwkv_a0 = nrm(ks[15], (DEPTH_2, 2, RWKV_W), 0.1)
    rwkv_a2 = nrm(ks[16], (DEPTH_2, 2, RWKV_ICLR_LORA, RWKV_W), 0.1)
    rwkv_k_k = 0.85 + nrm(ks[17], (DEPTH_2, RWKV_W), 0.02)
    rwkv_k_a = 1.0 + nrm(ks[18], (DEPTH_2, RWKV_W), 0.02)
    rwkv_r_k = nrm(ks[19], (DEPTH_2, RWKV_HEADS, RWKV_HD), 0.1)
    rwkv_ln_g = 1.0 + nrm(ks[20], (DEPTH_2, RWKV_W), 0.02)
    rwkv_ln_b = nrm(ks[21], (DEPTH_2, RWKV_W), 0.02)
    w_out = nrm(ks[22], (DEPTH_2, D_MIX, D_MODEL), D_MIX ** -0.5)
    final_norm_g = 1.0 + nrm(ks[23], (D_MODEL,), 0.02)
    return {
        'x': x, 'positions': positions, 'norm_g': norm_g, 'w_in': w_in,
        'gdn_conv': gdn_conv, 'gdn_a_log': gdn_a_log, 'gdn_dt_bias': gdn_dt_bias, 'gdn_norm_g': gdn_norm_g,
        'mla_q_norm_g': mla_q_norm_g, 'mla_w_uq': mla_w_uq, 'mla_kv_norm_g': mla_kv_norm_g, 'mla_w_ukv': mla_w_ukv,
        'rwkv_mu': rwkv_mu, 'rwkv_w0': rwkv_w0, 'rwkv_w2': rwkv_w2, 'rwkv_a0': rwkv_a0, 'rwkv_a2': rwkv_a2,
        'rwkv_k_k': rwkv_k_k, 'rwkv_k_a': rwkv_k_a, 'rwkv_r_k': rwkv_r_k,
        'rwkv_ln_g': rwkv_ln_g, 'rwkv_ln_b': rwkv_ln_b,
        'w_out': w_out, 'final_norm_g': final_norm_g,
    }

def second_block(x, positions, norm_g, w_in, gdn_conv, gdn_a_log, gdn_dt_bias, gdn_norm_g,
              mla_q_norm_g, mla_w_uq, mla_kv_norm_g, mla_w_ukv,
              rwkv_mu, rwkv_w0, rwkv_w2, rwkv_a0, rwkv_a2, rwkv_k_k, rwkv_k_a, rwkv_r_k,
              rwkv_ln_g, rwkv_ln_b, w_out, final_norm_g):
    for layer in range(DEPTH_2):
        h = rms_norm_2(x, norm_g[layer])
        cols = split_columns(h @ w_in[layer])
        y_gdn = gdn_branch(cols, gdn_conv[layer], gdn_a_log[layer], gdn_dt_bias[layer], gdn_norm_g[layer])
        y_mla = mla_branch(cols, positions, mla_q_norm_g[layer], mla_w_uq[layer],
                           mla_kv_norm_g[layer], mla_w_ukv[layer])
        y_rwkv = rwkv7_branch(cols, rwkv_mu[layer], rwkv_w0[layer], rwkv_w2[layer], rwkv_a0[layer],
                              rwkv_a2[layer], rwkv_k_k[layer], rwkv_k_a[layer], rwkv_r_k[layer],
                              rwkv_ln_g[layer], rwkv_ln_b[layer])
        mix = jnp.concatenate([y_gdn.astype(F32), y_mla.astype(F32), y_rwkv.astype(F32)], axis=-1)
        mix = mix * jax.nn.silu(cols['gate'].astype(F32))
        x = x + mix.astype(x.dtype) @ w_out[layer]
    return rms_norm_2(x, final_norm_g)


def setup_inputs(seed=0):
    out = dict(first_inputs(seed))
    for name, value in second_inputs(seed + 1).items():
        if name != "x":
            out[name + "_2"] = value
    return out


def reference(
    x, c, w_ada, b_ada, norm1_g, w_in, lambda_q1, lambda_k1, lambda_q2, lambda_k2, subln_g,
    w_pool, pool_scale, w_out, norm2_g, w_router_group, b_router_group, w_router_expert,
    b_router_expert, w_gate, w_up, w_down, final_g, positions_2, norm_g_2, w_in_2, gdn_conv_2,
    gdn_a_log_2, gdn_dt_bias_2, gdn_norm_g_2, mla_q_norm_g_2, mla_w_uq_2, mla_kv_norm_g_2,
    mla_w_ukv_2, rwkv_mu_2, rwkv_w0_2, rwkv_w2_2, rwkv_a0_2, rwkv_a2_2, rwkv_k_k_2, rwkv_k_a_2,
    rwkv_r_k_2, rwkv_ln_g_2, rwkv_ln_b_2, w_out_2, final_norm_g_2,
):
    x = first_block(
        x, c, w_ada, b_ada, norm1_g, w_in, lambda_q1, lambda_k1, lambda_q2, lambda_k2, subln_g,
        w_pool, pool_scale, w_out, norm2_g, w_router_group, b_router_group, w_router_expert,
        b_router_expert, w_gate, w_up, w_down, final_g,
    )
    return second_block(
        x, positions_2, norm_g_2, w_in_2, gdn_conv_2, gdn_a_log_2, gdn_dt_bias_2, gdn_norm_g_2,
        mla_q_norm_g_2, mla_w_uq_2, mla_kv_norm_g_2, mla_w_ukv_2, rwkv_mu_2, rwkv_w0_2,
        rwkv_w2_2, rwkv_a0_2, rwkv_a2_2, rwkv_k_k_2, rwkv_k_a_2, rwkv_r_k_2, rwkv_ln_g_2,
        rwkv_ln_b_2, w_out_2, final_norm_g_2,
    )


_drawn_inputs = setup_inputs


def setup_inputs(seed=0):
    import zlib

    import numpy as np

    out = dict(_drawn_inputs(seed))
    spreads = {}
    factors = {'norm1_g': 8.0,
     'lambda_q1': 64.0,
     'lambda_k1': 7.563,
     'lambda_q2': 5.569,
     'lambda_k2': 8.0,
     'subln_g': 8.0,
     'pool_scale': 3.464,
     'norm2_g': 7.787,
     'b_router_group': 8.0,
     'b_router_expert': 8.0,
     'gdn_norm_g_2': 6.115,
     'mla_q_norm_g_2': 8.0,
     'mla_kv_norm_g_2': 8.0,
     'rwkv_w2_2': 3.186,
     'rwkv_a0_2': 3.741,
     'rwkv_k_k_2': 6.19,
     'rwkv_k_a_2': 5.74,
     'rwkv_ln_g_2': 6.559,
     'rwkv_ln_b_2': 7.101,
     'final_norm_g_2': 8.146}
    for name, (base, spread) in spreads.items():
        noise = np.random.default_rng([zlib.crc32(name.encode()), seed]).standard_normal(out[name].shape)
        drawn = base * np.exp(spread * noise) if base else spread * noise
        out[name] = jnp.asarray(drawn.astype(out[name].dtype))
    for name, factor in factors.items():
        out[name] = (out[name] * factor).astype(out[name].dtype)
    return out
```

```python
from contextlib import ExitStack

import numpy as np
import concourse.bass as bass
from concourse import mybir

F32 = mybir.dt.float32
I32 = mybir.dt.int32
U32 = mybir.dt.uint32
ALU = mybir.AluOpType
ACT = mybir.ActivationFunctionType
AX = mybir.AxisListType

P = 128
T = 512
D = 1024
KD = D // P
TT = T // P
UNIT = 4096
SLOTS = 6
EPS = 1e-6
DEBUG = []
HEADS, HD = 4, 64
E_GROUPS, E_PER, N_EXP, FE = 4, 8, 32, 512
N_MORE = 7
N_BLK = N_EXP + N_MORE
NO_SLOT = 1 << 20
POOL_W = (2, 4, 8, 16)
POOL_PAD = 8

P1 = {}
def _cols(table, spec):
    at = 0
    for name, n in spec:
        table[name] = (at, at + n)
        at += n
    return at
N_P1 = _cols(P1, [("norm1_g", 8), ("b_ada", 48), ("norm2_g", 8), ("final_g", 8), ("pool_scale", 4),
                  ("subln_g", 1), ("c", 8), ("final2_g", 8)])
R1 = {}
N_R1 = _cols(R1, [("lambda", 256), ("b_router", 36)])

CN = {}
N_CN = _cols(CN, [("ident", 128), ("ones", 128), ("blk", 128), ("rotA", 128), ("cosA", 512), ("sinA", 512),
                  ("iota", 32), ("scal", 8), ("lt", 128), ("tok", 12)])


LAYERS = 2
GH, MH, RH, GD = 6, 6, 4, 64
NOPE, ROPE = 64, 32
QK_M = NOPE + ROPE
CHUNK = P
LEVELS = 7
N_IN2 = 3448
C_DECAY = float(np.exp(-0.5))
UNITS2 = [(1024, 384), (1408, 384), (1792, 408), (2552, 512), (3064, 384), (2200, 352), (0, 512), (512, 512)]
P2 = {}
N_P2 = _cols(P2, [("norm_g", 8), ("conv", 45), ("gdn_g", 1), ("qn_g", 2), ("kvn_g", 1), ("mu0", 7), ("mu1", 7),
                  ("k_k", 2), ("k_a", 2), ("r_k", 2), ("ln_g", 2), ("ln_b", 2), ("w0", 4), ("a0", 4)])
C2 = {}
N_C2 = _cols(C2, [("LE", 128), ("LT", 128), ("GE", 128), ("GT", 128), ("nLE", 128), ("nLT", 128), ("nGE", 128),
                  ("nGT", 128), ("lev0", LEVELS * 128), ("lev1", LEVELS * 128), ("reset", 512), ("rotM", 96),
                  ("invf", 1), ("ln8", 1), ("eps_ln", 1)])


def take(eng, sem, value=1):
    eng.wait_ge(sem, value)
    eng.sem_clear(sem)


class Chain:

    def __init__(self, eng, sem):
        self.eng, self.sem, self.n = eng, sem, 0

    def __call__(self, ins):
        self.n += 1
        ins.then_inc(self.sem, 1)
        self.eng.wait_ge(self.sem, self.n)

    def mark(self, ins):
        self.n += 1
        ins.then_inc(self.sem, 1)

    def wait(self):
        self.eng.wait_ge(self.sem, self.n)

    def reset(self):
        if self.n:
            self.eng.wait_ge(self.sem, self.n)
            self.eng.sem_clear(self.sem)
        self.n = 0


def build(nc, xT_d, par1, row1, cn, invcnt, w_ada, w_in, w_pool, w_out, w_rg, w_re, w_gate, w_up, w_down,
          w2, out, debug=None):
    ctx = ExitStack()
    with ctx:
        def sb(name, shape, dt=F32):
            return ctx.enter_context(nc.sbuf_tensor(name, shape, dt))

        sems = {}
        def sem(name):
            if name not in sems:
                sems[name] = ctx.enter_context(nc.semaphore(name))
            return sems[name]

        for late, early in (("xy_full0", "hid_full0"), ("xy_full1", "hid_full1"), ("v_full0", "hidT_full0"),
                            ("v_full1", "hidT_full1"), ("pad_free0", "wgt_free0"), ("pad_free1", "wgt_free1"),
                            ("pad_full0", "xt_full0"), ("pad_full1", "xt_full1"), ("R_full0", "y_full0"),
                            ("R_full1", "y_full1"),
                            ("d_args0", "max_full01"), ("d_args1", "max_full11"), ("d_full0", "slot_full2"),
                            ("d_full1", "slot_full3"), ("cb_full0", "slot_full4"), ("cb_full1", "slot_full5")):
            sems[late] = sem(early)

        h_d = nc.dram_tensor("h_scratch", (T, D), F32).ap()
        y_d = nc.dram_tensor("y_scratch", (2 * T, D), F32).ap()
        slot_d = nc.dram_tensor("slot_scratch", (N_BLK * P, 4), I32).ap()

        xT = sb("xT", [P, KD, T])
        hT = sb("hT", [P, KD, T])
        ARENA = 39300
        arena = sb("arena", [P, ARENA])
        ring = arena[:, 0:SLOTS * UNIT].rearrange("p (s n) -> p s n", s=SLOTS)
        c_sb = sb("c_sb", [P, N_CN])
        p1 = sb("p1", [P, N_P1])
        r1 = sb("r1", [P, N_R1])
        mod = sb("mod", [P, 48])
        small = sb("small", [P, 512])
        work = arena[:, SLOTS * UNIT:SLOTS * UNIT + 13000]
        bank = [ctx.enter_context(nc.psum_tensor(f"bank{i}", [P, 512], F32)) for i in range(8)]
        for_act = [sem(f"for_act{i}") for i in range(8)]
        for_dve = [sem(f"for_dve{i}") for i in range(8)]
        bank_free = [sem(f"bank_free{i}") for i in range(8)]
        slot_full = [sem(f"slot_full{i}") for i in range(SLOTS)]
        slot_free = [sem(f"slot_free{i}") for i in range(SLOTS)]

        def const(name, rows=P):
            a, b = CN[name]
            return c_sb[0:rows, a:b]
        def par(name, i=0, n=1):
            a = P1[name][0] + i
            return p1[:, a:a + n]
        ident, ones, blk = const("ident"), const("ones"), const("blk")
        eps_col = c_sb[:, CN["scal"][0]:CN["scal"][0] + 1]

        class Area:
            def __init__(self, at=0, base=work, end=13000):
                self.at, self.base, self.end = at, base, end
            def __call__(self, *shape):
                n = int(np.prod(shape))
                ap = self.base[:, self.at:self.at + n]
                self.at += n
                assert self.at <= self.end, self.at
                if len(shape) == 2:
                    ap = ap.rearrange("p (a b) -> p a b", a=shape[0])
                if len(shape) == 3:
                    ap = ap.rearrange("p (a b c) -> p a b c", a=shape[0], b=shape[1])
                return ap

        ar = Area()
        qkT = ar(8, T)
        v_tok = ar(TT, 512)
        u_pad = ar(4, T + 2 * POOL_PAD)
        att0 = ar.at
        raw = ar(2, T)
        rtmp = ar(2, T)
        ar.at = att0
        probs = ar(2, 2, T)
        wgt = ar(2, T)
        wTq = ar(2, T)
        inv_c = work[:, 0:4 * T].rearrange("p (a b) -> p a b", a=4)
        pool_a = work[:, 4 * T:4 * T + 2 * (T + 16)].rearrange("p (a b) -> p a b", a=2)
        sq = sb("sq", [P, 2, T])
        rs = sb("rs", [P, T])
        gs = sb("gs", [P, 2, 8])
        mixT = hT
        pool_w = sb("pool_w", [P, 4, P])
        w_router = sb("w_router", [P, KD, 36])
        stat = small[:, 32:48].rearrange("p (a b) -> p a b", a=2)
        subln = small[:, 24:25]
        rw = Area(att0)
        lg, ohg, m_g = rw(TT, 36), rw(TT, 4), rw(TT, 1)
        rt_t, rt_i, rt_big = rw(TT, 8), rw(TT, 1), rw(4, 8)
        e_in, e_in2, oh1, oh2, m_1, m_2 = rw(TT, 8), rw(TT, 8), rw(TT, 8), rw(TT, 8), rw(TT, 1), rw(TT, 1)
        rt_arg, rt_exp = rw(TT * 5), rw(TT * 5)
        rt_s = rw(3, TT, 1)

        am = Area()
        h_tok = am(4, D)
        am.at = 0
        X = [am(D) for _ in range(2)]
        XT = [am(KD, P) for _ in range(2)]
        sg = am(2, 512)
        hid = am(2, 512)
        hidT = am(2, 512)
        Yb = [am(D) for _ in range(2)]
        assert am.at <= 11000
        am.at = 11000
        info = am(N_BLK, 4).bitcast(I32)
        cur = [am(4).bitcast(I32) for _ in range(2)]
        rows = am(2, TT, 4).bitcast(I32)
        dest = am(2, TT).bitcast(U32)
        meta = am(8).bitcast(I32)
        M1, M2, Ms = am(TT, N_EXP), am(TT, N_EXP), am(TT, N_EXP)
        posn, prod = am(TT, N_EXP), am(TT, N_EXP)
        cnt, nblk, ends, base = am(N_EXP), am(N_EXP), am(N_EXP), am(N_EXP)
        dst_f, more_f = am(2, TT), am(8)
        more_t = am(N_MORE, N_EXP)
        y_tok = arena[:, 0:2 * TT * D].rearrange("p (t k d) -> p t k d", t=TT, k=2)

        def ada_unit(n):
            return w_ada[0, :, n * 512:(n + 1) * 512].rearrange("(k p) n -> p k n", p=P)
        def in_unit(n):
            return w_in[0, :, n * 512:(n + 1) * 512].rearrange("(k p) n -> p k n", p=P)
        def out_unit(n):
            return w_out[0, :, n * 512:(n + 1) * 512].rearrange("(k p) n -> p k n", p=P)
        units = ([ada_unit(n) for n in range(4)] + [in_unit(n) for n in range(4)]
                 + [ada_unit(n) for n in range(4, 12)] + [out_unit(n) for n in range(2)])
        N1 = len(units)
        assert N1 % SLOTS == 0

        def slot(n, k=8):
            return ring[:, n % SLOTS, :].rearrange("p (k n) -> p k n", k=k)

        w_in2, w_out2 = w2["w_in"], w2["w_out"]
        a2 = Area(2 * UNIT, arena, ARENA)
        mix = a2(KD, T)
        c2 = a2(N_C2)
        a2.at += N_C2 % 2
        cosM, sinM = a2(T), a2(T)
        p2, row2 = a2(N_P2), a2(24)
        a2.at += a2.at % 2
        W0 = a2.at

        def const2(name, rows=P):
            a, b = C2[name]
            return c2[0:rows, a:b]
        def par2(name, i=0, n=1):
            a = P2[name][0] + i
            return p2[:, a:a + n]
        def level(d, l):
            a = C2[f"lev{d}"][0] + l * P
            return over_tiles(c2[:, a:a + P])
        def over_tiles(m):
            return m.rearrange("p (a b) -> p a b", a=1).to_broadcast([P, TT, P])
        def tiles4(ap):
            return ap.rearrange("p (t n) -> p t n", t=TT)
        def along(col):
            return col.rearrange("p (t o) -> p t o", o=1).to_broadcast([P, TT, P])
        def slot2(n):
            w = UNITS2[n][1] if n < 8 else 512
            return arena[:, (n % 2) * UNIT:(n % 2) * UNIT + KD * w].rearrange("p (k n) -> p k n", k=KD)

        ga = Area(W0, arena, ARENA)
        g_qk = ga(6, T)
        g_ktok, g_vtok = ga(TT, 384), ga(TT, 384)
        g_PT = ga(GH, T)
        g_v = g_PT[:, 0:3, :]
        g_WT, g_qg = ga(3, T), ga(3, T)
        g_u0 = ga(TT, GH, GD)
        g_kd = ga(TT, GH, GD)
        g_TA = ga(10, T)
        g_y, g_neg, g_ln, g_g, g_beta, g_cum, g_tc, g_gam, g_dec, g_bg, g_ge = [ga(TT, 12) for _ in range(11)]
        g_ea = ga(12)
        g_ge2 = ga(2, 3, TT)
        g_S = ga(2, 3, GD)
        g_U = ga(GH, GD)
        pads = [g_TA[:, 2 * i:2 * i + 2, :].rearrange("p a b -> p (a b)")[:, 0:T + 4] for i in range(2)]
        R_v = [sq[:, s, 0:256].rearrange("p (t n) -> p t n", t=TT) for s in range(2)]
        R_k = [sq[:, s, 256:512].rearrange("p (t n) -> p t n", t=TT) for s in range(2)]

        ra = Area(W0, arena, ARENA)
        r_f = ra(6, T)
        r_wa = ra(1, T)
        r_kk, r_bon = ra(2, T), ra(2, T)
        r_kt, r_bt, r_kmt, r_rt = ra(2, T), ra(2, T), ra(2, T), ra(2, T)
        r_vtok = ra(TT, 256)
        r_PbT = ra(RH, T)
        r_PkT = ra(2, T)
        r_WT = ra(2, T)
        r_u0 = ra(TT, RH, GD)
        r_TA = ra(10, T)
        r_w = ra(2, 256)
        r_S = ra(2, 2, GD)
        r_U = ra(RH, GD)
        r_m, r_d, r_pm, r_pd, r_sc = ra(2, TT), ra(2, TT), ra(2, TT), ra(2, TT), ra(2, TT)
        r_c0, r_oka = ra(7), ra(2)
        r_ktok = mix[:, 3:5, :].rearrange("p a (b n) -> p (a b) n", n=256)
        r_nBV = mix[:, 5, :].rearrange("p (s t n) -> p s t n", s=2, t=TT)
        r_BT = [sq[:, s, :] for s in range(2)]
        r_btok = r_TA[:, 0:2, :].rearrange("p a (b n) -> p (a b) n", n=256)
        r_kmtok = r_TA[:, 2:4, :].rearrange("p a (b n) -> p (a b) n", n=256)
        r_pads = [r_TA[:, 2 * i:2 * i + 2, :].rearrange("p a b -> p (a b)")[:, 0:T + 2] for i in range(2)]

        la = Area(W0, arena, ARENA)
        m_cq, m_ckv, m_kr, m_tmp = la(2, T), la(1, T), la(1, T), la(2, T)
        m_q, m_k = la(MH, T), la(MH, T)
        m_vtok = la(TT, 384)
        m_pr, m_wT = la(2, T), la(2, T)
        m_st = la(2, 4)
        m_wuq, m_wukv = la(2, 576), la(768)
        m_gate = la(2, T)

        def sp_second(sp):
            take(sp, sem("go_sp"))
            sp.dma_start(c2, w2["cn"]).then_inc(sem("const2_full"), 16)
            pos = w2["positions"].to_broadcast([P, T])
            sp.dma_start(hT[:, 7, :].bitcast(I32), pos).then_inc(sem("const2_full"), 16)
            with sp.Fori(0, LAYERS) as l:
                def unit(n):
                    take(sp, slot_free[n % 2])
                    src, c, w = (w_in2, *UNITS2[n]) if n < 8 else (w_out2, 512 * (n - 8), 512)
                    src = src[bass.ds(l, 1), :, c:c + w].rearrange("a (k p) n -> p (a k) n", p=P)
                    sp.dma_start(slot2(n), src).then_inc(slot_full[n % 2], 16)
                take(sp, sem("par_free"))
                sp.dma_start(p2, w2["par"][bass.ds(l, 1)].rearrange("a p n -> p (a n)")).then_inc(sem("par_full"), 16)
                sp.dma_start(row2, w2["row"][bass.ds(l, 1), :].to_broadcast([P, 24])).then_inc(sem("par_full"), 16)
                for n in range(5):
                    unit(n)
                take(sp, sem("go_sp"))
                for lo, name in ((0, "rwkv_w2"), (64, "rwkv_a2")):
                    sp.dma_start(r_w[lo:lo + 64], w2[name][bass.ds(l, 1)].rearrange("a e k n -> k (a e) n"))\
                      .then_inc(sem("small_w_full"), 16)
                unit(5)
                take(sp, sem("go_sp"))
                uq = w2["mla_w_uq"][bass.ds(l, 1)]
                sp.dma_start(m_wuq[:, 0, :], uq[:, 0:P, :].rearrange("a k n -> k (a n)")).then_inc(sem("small_w_full"), 16)
                sp.dma_start(m_wuq[0:64, 1, :], uq[:, P:192, :].rearrange("a k n -> k (a n)")).then_inc(sem("small_w_full"), 16)
                sp.dma_start(m_wukv, w2["mla_w_ukv"][bass.ds(l, 1)].rearrange("a k n -> k (a n)")).then_inc(sem("small_w_full"), 16)
                for n in range(6, 10):
                    unit(n)
            sp.wait_ge(sem("done"), 1)
            sp.dma_start(out.rearrange("(k p) t -> p k t", p=P), hT[:]).then_inc(sem("out_stored"), 16)
            sp.wait_ge(sem("out_stored"), 16)

        def pe_second(pe, sumsq):
            def column(b, n, c, w, rows=None):
                lo = 0 if rows is None else rows
                for k in range(KD):
                    m = pe.matmul(bank[b][lo:lo + w, :], slot2(n)[:, k, c:c + w], hT[:, k, :], start=(k == 0), stop=(k == KD - 1))
                return m
            def grid(b, lhs, rhs, reader=for_dve):
                for t in range(TT):
                    m = pe.matmul(bank[b][:, t * P:(t + 1) * P], lhs(t), rhs(t), start=True, stop=True)
                m.then_inc(reader[b], 1)
            def ts(t):
                return slice(t * P, (t + 1) * P)
            def to_tokens(b, src):
                take(pe, bank_free[b])
                for t in range(TT):
                    m = pe.transpose(bank[b][:, ts(t)], src[:, ts(t)], ident)
                m.then_inc(for_act[b], 1)
            def invert(TA):
                Tm, Y, X, V = [[TA[:, 2 * i + s, :] for s in range(2)] for i in (1, 2, 3, 4)]
                for s in range(2):
                    take(pe, sem(f"xy_full{s}"))
                    take(pe, bank_free[s])
                    grid(s, lambda t: X[s][:, ts(t)], lambda t: ident)
                for l in range(1, LEVELS):
                    for s in range(2):
                        take(pe, sem(f"xy_full{s}"))
                        take(pe, bank_free[s])
                        grid(s, lambda t: X[s][:, ts(t)], lambda t: Y[s][:, ts(t)], for_act)
                    for s in range(2):
                        take(pe, sem(f"v_full{s}"))
                        take(pe, bank_free[2 + s])
                        take(pe, sem(f"t_full{s}"))
                        grid(2 + s, lambda t: Tm[s][:, ts(t)], lambda t: V[s][:, ts(t)])
                        if l < LEVELS - 1:
                            take(pe, bank_free[4 + s])
                            grid(4 + s, lambda t: V[s][:, ts(t)], lambda t: Tm[s][:, ts(t)])
                for s in range(2):
                    take(pe, sem(f"xy_full{s}"))
            def norm_over_heads():
                take(pe, bank_free[6])
                take(pe, sem("sq_full0"))
                pe.matmul(bank[6][:, :], blk, sq[:, 0, :], start=True, stop=True).then_inc(for_act[6], 1)
            def recurrence(d, n_heads, WT, S, q_in, U, PT, pairs, step0):
                for n in range(TT):
                    t = n if d == 0 else TT - 1 - n
                    if n > 0:
                        take(pe, sem("state_full"))
                        for s, b in ((0, 0), (1, 2)):
                            take(pe, bank_free[b])
                            for i in range(n_heads // 2):
                                m = pe.matmul(bank[b][:, i * 64:(i + 1) * 64], WT[64 * s:64 * s + 64, i, ts(t)],
                                              S[64 * s:64 * s + 64, n % 2, i, :], start=True, stop=True)
                            m.then_inc(for_dve[b], 1)
                    take(pe, sem("u_full"))
                    if n < TT - 1:
                        take(pe, bank_free[3])
                        for h in range(n_heads):
                            lo = 64 * (h % 2)
                            prods = pairs(h, t)
                            for i, (a, b) in enumerate(prods):
                                m = pe.matmul(bank[3][lo:lo + 64, (h // 2) * 64:(h // 2 + 1) * 64], a, b, start=(i == 0),
                                              stop=(i == len(prods) - 1))
                        m.then_inc(for_dve[3], 1)
                    take(pe, bank_free[1])
                    for h in range(n_heads):
                        lo = 64 * (h % 2)
                        o = bank[1][lo:lo + 64, (h // 2) * P:(h // 2 + 1) * P]
                        if n > 0:
                            pe.matmul(o, S[lo:lo + 64, n % 2, h // 2, :], q_in[lo:lo + 64, h // 2, ts(t)], start=True, stop=False)
                        m = pe.matmul(o, U[:, h, :], PT[:, h, ts(t)], start=(n == 0), stop=True)
                    m.then_inc(for_dve[1], 1)

            with pe.Fori(0, LAYERS) as l:
                sumsq(1, KD, 0)
                for i in range(9):
                    n, b = i // 3, i % 2
                    if i % 3 == 0:
                        take(pe, slot_full[n % 2], 16)
                    if i == 0:
                        take(pe, sem("tiles_full"), KD)
                    take(pe, bank_free[b])
                    column(b, n, (i % 3) * P, P).then_inc(for_act[b], 1)
                take(pe, bank_free[2])
                for t in range(TT):
                    for k in range(KD):
                        m = pe.matmul(bank[2][:, t * 24:(t + 1) * 24], hT[:, k, ts(t)], slot2(2)[:, k, 384:408],
                                      start=(k == 0), stop=(k == KD - 1))
                m.then_inc(for_dve[2], 1)
                for i in range(6):
                    norm_over_heads()
                for i in range(3):
                    take(pe, sem("v_ch_full"))
                    to_tokens(4 + i % 2, g_v[:, i, :])
                take(pe, sem("k_ch_full"))
                for i in range(3):
                    to_tokens(4 + i % 2, g_qk[:, 3 + i, :])
                take(pe, sem("g_full"))
                take(pe, bank_free[2])
                cum = bank[2][:, 0:48].rearrange("p (t c) -> p t c", t=TT)
                pe.matmul(cum[:, :, 0:6], const2("LE"), g_g[:, :, 0:6], start=True, stop=True)
                pe.matmul(cum[:, :, 6:12], const2("GE"), g_g[:, :, 6:12], start=True, stop=True)
                pe.matmul(bank[2][:, 64:112], ones, g_g.rearrange("p t c -> p (t c)"), start=True, stop=True)\
                  .then_inc(for_dve[2], 1)
                for d in range(2):
                    for ht in range(3):
                        for s in range(2):
                            c = 6 * d + 2 * ht + s
                            lo = 64 * s
                            take(pe, bank_free[s])
                            grid(s, lambda t: g_g[:, t, c:c + 1].to_broadcast([P, P]), lambda t: const2("LE" if d == 0 else "GE"))
                            kh, qh = g_qk[lo:lo + 64, 3 + ht, :], g_qk[lo:lo + 64, ht, :]
                            take(pe, bank_free[2 + s])
                            grid(2 + s, lambda t: kh[:, ts(t)], lambda t: kh[:, ts(t)])
                            take(pe, bank_free[4 + s])
                            grid(4 + s, lambda t: kh[:, ts(t)], lambda t: qh[:, ts(t)])
                        invert(g_TA)
                        take(pe, bank_free[6])
                        take(pe, bank_free[7])
                        for s in range(2):
                            take(pe, sem(f"R_full{s}"))
                            Y = g_TA[:, 4 + s, :]
                            for t in range(TT):
                                m6 = pe.matmul(bank[6][:, s * 256 + t * 64:s * 256 + (t + 1) * 64], Y[:, ts(t)], R_v[s][:, t, :],
                                               start=True, stop=True)
                        m6.then_inc(for_act[6], 1)
                        for s in range(2):
                            Y = g_TA[:, 4 + s, :]
                            for t in range(TT):
                                m7 = pe.matmul(bank[7][64 * s:64 * s + 64, ts(t)], R_k[s][:, t, :], Y[:, ts(t)], start=True, stop=True)
                        m7.then_inc(for_act[7], 1)
                    take(pe, sem("chunks_full"))
                    take(pe, sem("kd_full"))
                    recurrence(d, GH, g_WT, g_S, g_qg, g_U, g_PT, lambda h, t: [(g_kd[:, t, h, :], g_U[:, h, :])], None)
                for i in range(3):
                    norm_over_heads()
                for i in range(7):
                    n, b = 3 + i // 4, i % 2
                    if i % 4 == 0:
                        take(pe, slot_full[n % 2], 16)
                    take(pe, bank_free[b])
                    column(b, n, (i % 4) * P, P).then_inc(for_act[b], 1)
                for i in range(2):
                    norm_over_heads()
                for i in range(2):
                    take(pe, sem("v_ch_full"))
                    to_tokens(4 + i, r_f[:, 4 + i, :])
                take(pe, sem("small_w_full"), 32)
                take(pe, sem("wa_full"))
                for e in range(2):
                    for ct in range(2):
                        for b, lo in ((0, 0), (1, 64)):
                            take(pe, bank_free[b])
                            pe.matmul(bank[b][:, :], r_w[lo:lo + 64, e, ts(ct)], r_wa[lo:lo + 64, 0, :], start=True,
                                      stop=True).then_inc(for_act[b], 1)
                        take(pe, sem("kt_full"))
                        to_tokens(2 + ct, r_kt[:, ct, :])
                    for ct in range(2):
                        for s in range(2):
                            lo = 64 * s
                            kt, bt, kmt, rt = [x[lo:lo + 64, ct, :] for x in (r_kt, r_bt, r_kmt, r_rt)]
                            for b, x, y in ((s, kt, bt), (2 + s, kmt, kt), (4 + s, bt, rt), (6 + s, kmt, rt)):
                                take(pe, bank_free[b])
                                grid(b, lambda t: x[:, ts(t)], lambda t: y[:, ts(t)])
                        take(pe, sem("bp_full"))
                        take(pe, bank_free[6])
                        take(pe, bank_free[7])
                        for s in range(2):
                            h = 2 * ct + s
                            for t in range(TT):
                                pe.matmul(bank[6][:, s * 256 + t * 64:s * 256 + (t + 1) * 64], r_BT[s][:, ts(t)],
                                          r_vtok[:, t, h * 64:(h + 1) * 64], start=True, stop=True)
                                m7 = pe.matmul(bank[7][64 * s:64 * s + 64, ts(t)], r_vtok[:, t, h * 64:(h + 1) * 64],
                                               r_PkT[:, s, ts(t)], start=True, stop=True)
                        m7.then_inc(for_act[7], 1)
                        invert(r_TA)
                        take(pe, sem("nBV_full"))
                        take(pe, bank_free[6])
                        take(pe, bank_free[7])
                        for s in range(2):
                            Y = r_TA[:, 4 + s, :]
                            for t in range(TT):
                                m6 = pe.matmul(bank[6][:, s * 256 + t * 64:s * 256 + (t + 1) * 64], Y[:, ts(t)],
                                               r_nBV[:, s, t, :], start=True, stop=True)
                        m6.then_inc(for_act[6], 1)
                        for s in range(2):
                            h = 2 * ct + s
                            Y = r_TA[:, 4 + s, :]
                            for t in range(TT):
                                m7 = pe.matmul(bank[7][64 * s:64 * s + 64, ts(t)], r_ktok[:, t, h * 64:(h + 1) * 64],
                                               Y[:, ts(t)], start=True, stop=True)
                        m7.then_inc(for_act[7], 1)
                    for ct in range(2):
                        to_tokens(2 + ct, r_bt[:, ct, :])
                        to_tokens(4 + ct, r_kmt[:, ct, :])
                    take(pe, sem("chunks_full"))
                    recurrence(e, RH, r_WT, r_S, r_rt, r_U, r_PbT, lambda h, t: [
                        (r_btok[:, t, h * 64:(h + 1) * 64], r_U[:, h, :]),
                        (r_kmtok[:, t, h * 64:(h + 1) * 64], r_vtok[:, t, h * 64:(h + 1) * 64])], None)
                for i in range(2):
                    take(pe, bank_free[5])
                    take(pe, sem("y_full"))
                    pe.matmul(bank[5][:, :], blk, mix[:, 6 + i, :], start=True, stop=True).then_inc(for_dve[5], 1)
                    norm_over_heads()
                    take(pe, bank_free[7])
                    take(pe, sem("bonus_full"))
                    pe.matmul(bank[7][:, :], blk, r_bon[:, i, :], start=True, stop=True).then_inc(for_dve[7], 1)
                take(pe, slot_full[1], 16)
                for b, c, w, rows in ((0, 0, 128, 0), (1, 128, 64, 0), (2, 192, 128, 0), (3, 320, 32, 64)):
                    take(pe, bank_free[b])
                    column(b, 5, c, w, rows).then_inc(for_act[b], 1)
                sumsq(4, 2, 0, rows=[P, 64])
                sumsq(5, 1, 0)
                take(pe, sem("raw_full"))
                take(pe, bank_free[3])
                pe.matmul(bank[3][64:96, :], const2("rotM")[64:96, 64:96], m_kr[64:96, 0, :], start=True, stop=True)\
                  .then_inc(for_dve[3], 1)
                take(pe, sem("small_w_full"), 48)
                take(pe, sem("latent_in_full"), 2)
                for h in range(MH):
                    b = h % 2
                    take(pe, bank_free[b])
                    pe.matmul(bank[b][0:QK_M, :], m_wuq[:, 0, h * QK_M:(h + 1) * QK_M], m_cq[:, 0, :], start=True, stop=False)
                    pe.matmul(bank[b][0:QK_M, :], m_wuq[0:64, 1, h * QK_M:(h + 1) * QK_M], m_cq[0:64, 1, :], start=False,
                              stop=True).then_inc(for_act[b], 1)
                    take(pe, bank_free[4 + b])
                    pe.matmul(bank[4 + b][0:64, :], m_wukv[:, h * P:h * P + 64], m_ckv[:, 0, :], start=True,
                              stop=True).then_inc(for_act[4 + b], 1)
                    take(pe, sem("raw_full"))
                    take(pe, bank_free[2 + b])
                    pe.matmul(bank[2 + b][64:96, :], const2("rotM")[64:96, 64:96], m_q[64:96, h, :], start=True, stop=True)\
                      .then_inc(for_dve[2 + b], 1)
                for t in range(TT):
                    take(pe, bank_free[6 + t % 2])
                    pe.matmul(bank[6 + t % 2][:, 0:384], m_ckv[:, 0, ts(t)],
                              m_wukv.rearrange("p (h x) -> p h x", h=MH)[:, :, 64:128], start=True, stop=True)\
                      .then_inc(for_act[6 + t % 2], 1)
                take(pe, sem("mla_q_full"), MH)
                take(pe, sem("mla_k_full"), MH)
                steps = [(h, q) for h in range(MH) for q in range(TT)]
                for i in range(len(steps) + 2):
                    if i < len(steps):
                        h, q = steps[i]
                        take(pe, bank_free[i % 2])
                        pe.matmul(bank[i % 2][:, :], m_q[0:QK_M, h, ts(q)], m_k[0:QK_M, h, :], start=True,
                                  stop=True).then_inc(for_dve[i % 2], 1)
                    if 1 <= i <= len(steps):
                        j = (i - 1) % 2
                        take(pe, sem(f"wgt_full{j}"))
                        to_tokens(2 + j, m_pr[:, j, :])
                    if i >= 2:
                        h, q = steps[i - 2]
                        b = 4 + (h // 2) % 2
                        take(pe, sem(f"wT_full{i % 2}"))
                        if q == 0 and h % 2 == 0:
                            take(pe, bank_free[b])
                        lo = 64 * (h % 2)
                        for kt in range(TT):
                            m = pe.matmul(bank[b][lo:lo + 64, ts(q)], m_vtok[:, kt, h * 64:(h + 1) * 64], m_wT[:, i % 2, ts(kt)],
                                          start=(kt == 0), stop=(kt == TT - 1))
                        m.then_inc(for_act[b] if h % 2 == 1 and q == TT - 1 else sem(f"wT_free{i % 2}"), 1)
                for i in range(8):
                    n, b = 6 + i // 4, i % 2
                    if i % 4 == 0:
                        take(pe, slot_full[n % 2], 16)
                    take(pe, bank_free[b])
                    column(b, n, (i % 4) * P, P).then_inc(for_act[b], 1)
                take(pe, sem("tiles_full"), KD)
                for m_ in range(8):
                    n, b = 8 + m_ // 4, 4 + m_ % 4
                    if m_ % 4 == 0:
                        take(pe, slot_full[n % 2], 16)
                    take(pe, bank_free[b])
                    for k in range(KD):
                        m = pe.matmul(bank[b][:, :], slot2(n)[:, k, (m_ % 4) * P:(m_ % 4 + 1) * P], mix[:, k, :],
                                      start=(k == 0), stop=(k == KD - 1))
                    m.then_inc(for_dve[b], 1)
            sumsq(1, KD, 0)

        def act_second(act, chain):
            def move(b, dst, src, func=ACT.Copy, **kw):
                take(act, for_act[b])
                chain(act.activation(dst, src, func, **kw))
                act.sem_inc(bank_free[b], 1)
            def meet():
                act.sem_inc(sem("act_here"), 1)
                take(act, sem("go_act"))
            def square(src, j, rows=P):
                take(act, sem(f"sq_free{j}"))
                act.activation(sq[0:rows, j, :], src, ACT.Square).then_inc(sem(f"sq_full{j}"), 1)
            def root(b, scale, last=0, eps=eps_col, bias=None):
                take(act, for_act[b])
                take(act, sem("rs_free"))
                chain(act.activation(rs[:], bank[b][:, :], ACT.Ln, bias=eps, scale=scale))
                act.sem_inc(bank_free[b], 1)
                act.sem_inc(sem(f"sq_free{last}"), 1)
                kw = {} if bias is None else {"bias": bias}
                act.activation(rs[:], rs[:], ACT.Exp, scale=-0.5, **kw).then_inc(sem("rs_full"), 1)
            def to_tokens(b, dst):
                move(b, dst, tiles4(bank[b][:, :]))
            def invert(TA):
                V = [TA[:, 8 + s, :] for s in range(2)]
                for l in range(1, LEVELS):
                    for s in range(2):
                        move(s, V[s], bank[s][:, :])
                        act.sem_inc(sem(f"v_full{s}"), 1)
            meet()
            take(act, sem("args_full"))
            chain(act.activation(sinM[0:QK_M], sinM[0:QK_M], ACT.Sin))
            chain(act.activation(cosM[0:QK_M], cosM[0:QK_M], ACT.Sin))
            act.sem_inc(sem("func_full"), 1)
            chain.reset()
            with act.Fori(0, LAYERS) as l:
                take(act, sem("norm_in_full"))
                for i in range(KD):
                    square(xT[:, i, :], i % 2)
                root(1, 1.0 / D, last=1)
                for i in range(10):
                    if i < 9:
                        take(act, for_act[i % 2])
                        take(act, sem(f"pad_free{i % 2}"))
                        chain(act.activation(pads[i % 2][:, 2:2 + T], bank[i % 2][:, :], ACT.Copy))
                        act.sem_inc(bank_free[i % 2], 1)
                        act.sem_inc(sem(f"pad_full{i % 2}"), 1)
                        if i in (2, 5):
                            act.sem_inc(slot_free[(i // 3) % 2], 1)
                    if i >= 1:
                        j = i - 1
                        dst = g_qk[:, j, :] if j < 6 else g_v[:, j - 6, :]
                        take(act, sem(f"conv_full{j % 2}"))
                        chain(act.activation(dst, dst, ACT.Silu))
                for i in range(6):
                    square(g_qk[:, i, :], 0)
                    root(6, 1.0, bias=const2("ln8") if i < 3 else None)
                act.sem_inc(sem("v_ch_full"), 1)
                for i in range(3):
                    to_tokens(4 + i % 2, g_vtok[:, :, i * P:(i + 1) * P])
                    if i < 2:
                        act.sem_inc(sem("v_ch_full"), 1)
                for i in range(3):
                    to_tokens(4 + i % 2, g_ktok[:, :, i * P:(i + 1) * P])
                take(act, sem("args_full"))
                chain(act.activation(g_beta, g_beta, ACT.Sigmoid))
                chain(act.activation(g_ln, g_neg, ACT.Exp))
                chain(act.activation(g_ea, row2[:, 0:12], ACT.Exp))
                act.activation(g_ln, g_ln, ACT.Ln, bias=ones[:, 0:1]).then_inc(sem("func_full"), 1)
                take(act, sem("args_full"))
                chain(act.activation(g_gam, g_cum, ACT.Exp))
                chain(act.activation(g_dec, g_dec, ACT.Exp))
                act.activation(g_ge, g_ge, ACT.Exp).then_inc(sem("func_full"), 1)
                for d in range(2):
                    for ht in range(3):
                        TA = g_TA
                        for s in range(2):
                            lo = 64 * s
                            Y, X, V = TA[:, 4 + s, :], TA[:, 6 + s, :], TA[:, 8 + s, :]
                            take(act, sem(f"cb_full{s}"))
                            chain(act.activation(Y[lo:lo + 64, :], bank[s][lo:lo + 64, :], ACT.Exp))
                            act.sem_inc(bank_free[s], 1)
                            take(act, sem(f"d_args{s}"))
                            chain(act.activation(V, V, ACT.Exp))
                            chain(act.activation(X, X, ACT.Exp, scale=-1.0))
                            act.sem_inc(sem(f"d_full{s}"), 1)
                        invert(TA)
                        take(act, for_act[6])
                        u = bank[6][:, :].rearrange("p (s t n) -> p s t n", s=2, t=TT)
                        for s in range(2):
                            chain(act.activation(g_u0[:, :, 2 * ht + s, :], u[:, s], ACT.Copy))
                        act.sem_inc(bank_free[6], 1)
                        move(7, g_WT[:, ht, :], bank[7][:, :])
                        for s in range(2):
                            act.sem_inc(sem(f"R_free{s}"), 1)
                    act.sem_inc(sem("chunks_act"), 1)
                for i in range(3):
                    if i == 0:
                        take(act, sem("norm_in_full"))
                    square(mix[:, i, :], 0)
                    root(6, 1.0 / 64)
                meet()
                for i in range(7):
                    take(act, for_act[i % 2])
                    take(act, sem(f"pad_free{i % 2}"))
                    chain(act.activation(r_pads[i % 2][:, 1:1 + T], bank[i % 2][:, :], ACT.Copy))
                    act.sem_inc(bank_free[i % 2], 1)
                    act.sem_inc(sem(f"pad_full{i % 2}"), 1)
                    if i in (3, 6):
                        act.sem_inc(slot_free[(3 + i // 4) % 2], 1)
                take(act, sem("norm_in_full"))
                chain(act.activation(r_wa[0:64, 0, :], r_wa[0:64, 0, :], ACT.Tanh))
                act.sem_inc(sem("wa_full"), 1)
                for i in range(2):
                    square(r_kk[:, i, :], 0)
                    root(6, 1.0)
                for i in range(2):
                    act.sem_inc(sem("v_ch_full"), 1)
                    to_tokens(4 + i, r_vtok[:, :, i * P:(i + 1) * P])
                for e in range(2):
                    TA = r_TA
                    for ct in range(2):
                        take(act, sem("ta_free"))
                        move(0, TA[:, 0, :], bank[0][:, :], ACT.Sigmoid, bias=par2("w0", 2 * e + ct))
                        move(1, TA[:, 1, :], bank[1][:, :], ACT.Sigmoid, bias=par2("a0", 2 * e + ct))
                        act.sem_inc(sem("sig_full"), 1)
                        take(act, sem("args_full"))
                        A1, A2 = TA[:, 3, :], TA[:, 4, :]
                        for dst, src, sign in (((5, A1, -1), (6, A1, 1), (7, A2, -1)) if e == 0 else
                                               ((5, A2, 1), (6, A2, -1), (7, A1, 1))):
                            chain(act.activation(TA[:, dst, :], src, ACT.Exp, scale=sign * C_DECAY))
                        chain(act.activation(r_pm[:, ct, :], r_m[:, ct, :], ACT.Exp, scale=-C_DECAY))
                        chain(act.activation(r_pd[:, ct, :], r_d[:, ct, :], ACT.Exp, scale=-C_DECAY))
                        act.sem_inc(sem("func_full"), 1)
                        to_tokens(2 + ct, r_ktok[:, :, ct * P:(ct + 1) * P])
                    for ct in range(2):
                        take(act, for_act[7])
                        chain(act.activation(r_nBV.rearrange("p s t n -> p (s t n)"), bank[6][:, :], ACT.Copy, scale=-1.0))
                        act.sem_inc(bank_free[6], 1)
                        act.sem_inc(sem("nBV_full"), 1)
                        act.sem_inc(sem("direct_full"), 1)
                        invert(TA)
                        take(act, for_act[6])
                        u = bank[6][:, :].rearrange("p (s t n) -> p s t n", s=2, t=TT)
                        for s in range(2):
                            chain(act.activation(r_u0[:, :, 2 * ct + s, :], u[:, s], ACT.Copy))
                        act.sem_inc(bank_free[6], 1)
                        move(7, r_WT[:, ct, :], bank[7][:, :])
                    for ct in range(2):
                        to_tokens(2 + ct, r_btok[:, :, ct * P:(ct + 1) * P])
                        to_tokens(4 + ct, r_kmtok[:, :, ct * P:(ct + 1) * P])
                    act.sem_inc(sem("chunks_act"), 1)
                for i in range(2):
                    take(act, sem("norm_in_full"))
                    square(mix[:, 6 + i, :], 0)
                    root(6, 1.0 / 64, eps=const2("eps_ln"))
                meet()
                move(0, m_cq[:, 0, :], bank[0][:, :])
                move(1, m_cq[0:64, 1, :], bank[1][0:64, :])
                move(2, m_ckv[:, 0, :], bank[2][:, :])
                move(3, m_kr[64:96, 0, :], bank[3][64:96, :])
                act.sem_inc(slot_free[1], 1)
                act.sem_inc(sem("raw_full"), 1)
                square(m_cq[:, 0, :], 0)
                square(m_cq[0:64, 1, :], 1, 64)
                root(4, 1.0 / 192, last=1)
                square(m_ckv[:, 0, :], 0)
                root(5, 1.0 / 128)
                for h in range(MH):
                    b = h % 2
                    move(b, m_q[0:QK_M, h, :], bank[b][0:QK_M, :])
                    act.sem_inc(sem("raw_full"), 1)
                    move(4 + b, m_k[0:64, h, :], bank[4 + b][0:64, :])
                    act.sem_inc(sem("mla_k_full"), 1)
                for t in range(TT):
                    move(6 + t % 2, m_vtok[:, t, :], bank[6 + t % 2][:, 0:384])
                n = MH * TT
                for i in range(n + 3):
                    if i < n:
                        take(act, sem(f"probs_free{i % 2}"))
                        take(act, sem(f"max_full{i % 2}0"))
                        chain(act.activation(m_pr[:, i % 2, :], bank[i % 2][:, :], ACT.Exp, bias=m_st[:, i % 2, 0:1],
                                             scale=QK_M ** -0.5, accum_out=m_st[:, i % 2, 1:2]))
                        act.sem_inc(bank_free[i % 2], 1)
                        act.sem_inc(sem(f"probs_full{i % 2}"), 1)
                    if i >= 3 and (i - 3) % 8 == 7:
                        hp = (i - 3) // 8
                        move(4 + hp % 2, mix[:, 3 + hp, :], bank[4 + hp % 2][:, :])
                        act.sem_inc(sem("wT_free1"), 1)
                    if 1 <= i <= n:
                        j = (i - 1) % 2
                        take(act, for_act[2 + j])
                        act.sem_inc(sem(f"probs_free{j}"), 1)
                        take(act, sem(f"wT_free{j}"))
                        chain(act.activation(m_wT[:, j, :], bank[2 + j][:, :], ACT.Copy))
                        act.sem_inc(bank_free[2 + j], 1)
                        act.sem_inc(sem(f"wT_full{j}"), 1)
                for i in range(8):
                    take(act, sem(f"sg_free{i % 2}"))
                    move(i % 2, m_gate[:, i % 2, :], bank[i % 2][:, :], ACT.Silu)
                    act.sem_inc(sem(f"sg_full{i % 2}"), 1)
                    if i % 4 == 3:
                        act.sem_inc(slot_free[(6 + i // 4) % 2], 1)
                chain.reset()
            take(act, sem("norm_in_full"))
            for i in range(KD):
                square(xT[:, i, :], i % 2)
            root(1, 1.0 / D, last=1)

        def pool_second(pool):
            for name in ("par_free", "R_free0", "R_free1", "ta_free"):
                pool.sem_inc(sem(name), 1)
            chain = Chain(pool, sem("pool_chain"))
            def meet():
                pool.sem_inc(sem("pool_here"), 1)
                take(pool, sem("go_pool"))
            meet()
            with pool.Fori(0, LAYERS) as l:
                take(pool, sem("tok_full"))
                for d in range(2):
                    if d == 1:
                        take(pool, sem("dir_done"))
                    for h in range(GH):
                        s = h % 2
                        c = 6 * d + h
                        def scaled(dst, src, col):
                            chain(pool.tensor_tensor(dst, src[:, :, h * 64:(h + 1) * 64],
                                                     col[:, :, c:c + 1].to_broadcast([P, TT, 64]), ALU.mult))
                        take(pool, sem(f"R_free{s}"))
                        scaled(R_v[s], g_vtok, g_beta)
                        scaled(R_k[s], g_ktok, g_bg)
                        pool.sem_inc(sem(f"R_full{s}"), 1)
                        scaled(g_kd[:, :, h, :], g_ktok, g_dec)
                    pool.sem_inc(sem("kd_full"), 1)
                meet()
                meet()
                take(pool, sem("kr_full"))
                for h in range(MH):
                    chain(pool.tensor_copy(m_k[64:96, h, :], m_kr[64:96, 0, :]))
                pool.sem_inc(sem("k_rot_full"), 1)
                chain.reset()

        def dve_second(dve, chain):
            def meet(sp=True):
                chain.wait()
                take(dve, sem("act_here"))
                take(dve, sem("pool_here"))
                for name in ("go_act", "go_pool") + (("go_sp",) if sp else ()):
                    dve.sem_inc(sem(name), 1)
            def times_rs(dst, src, col=None):
                take(dve, sem("rs_full"))
                if col is None:
                    chain(dve.tensor_tensor(dst, src, rs[:], ALU.mult))
                else:
                    chain(dve.scalar_tensor_tensor(dst, src, col, rs[:], ALU.mult, ALU.mult))
                dve.sem_inc(sem("rs_free"), 1)
            def invert(TA, d):
                A, Tm, Y, X, _ = [[tiles4(TA[:, 2 * i + s, :]) for s in range(2)] for i in range(5)]
                I4 = over_tiles(ident)
                for s in range(2):
                    chain(dve.tensor_tensor(X[s], A[s], level(d, 0), ALU.mult))
                    dve.sem_inc(sem(f"xy_full{s}"), 1)
                    chain(dve.tensor_tensor(Tm[s], I4, X[s], ALU.subtract))
                    dve.sem_inc(sem(f"t_full{s}"), 1)
                for s in range(2):
                    take(dve, for_dve[s])
                    chain.mark(dve.tensor_tensor(X[s], A[s], level(d, 1), ALU.mult))
                    chain(dve.tensor_tensor(Y[s], I4, tiles4(bank[s][:, :]), ALU.subtract))
                    dve.sem_inc(bank_free[s], 1)
                    dve.sem_inc(sem(f"xy_full{s}"), 1)
                for l in range(1, LEVELS):
                    for s in range(2):
                        take(dve, for_dve[2 + s])
                        if l < LEVELS - 1:
                            chain.mark(dve.tensor_tensor(X[s], A[s], level(d, l + 1), ALU.mult))
                        chain(dve.tensor_tensor(Y[s], Y[s], tiles4(bank[2 + s][:, :]), ALU.subtract))
                        dve.sem_inc(bank_free[2 + s], 1)
                        dve.sem_inc(sem(f"xy_full{s}"), 1)
                        if l < LEVELS - 1:
                            take(dve, for_dve[4 + s])
                            chain(dve.tensor_tensor(Tm[s], Tm[s], tiles4(bank[4 + s][:, :]), ALU.subtract))
                            dve.sem_inc(bank_free[4 + s], 1)
                            dve.sem_inc(sem(f"t_full{s}"), 1)
            def recurrence(d, n_heads, u0, U, S, next_state, first_tile, add):
                nt = n_heads // 2
                for n in range(TT):
                    t = n if d == 0 else TT - 1 - n
                    if n == 0:
                        chain(dve.tensor_copy(U, u0[:, t]))
                    else:
                        for s, b in ((0, 0), (1, 2)):
                            take(dve, for_dve[b])
                            chain(dve.tensor_tensor(U[:, s:n_heads:2], u0[:, t, s:n_heads:2],
                                                    bank[b][:, 0:nt * 64].rearrange("p (h n) -> p h n", h=nt), ALU.subtract))
                            dve.sem_inc(bank_free[b], 1)
                    dve.sem_inc(sem("u_full"), 1)
                    if n < TT - 1:
                        take(dve, for_dve[3])
                        next_state(n, t, bank[3][:, 0:nt * 64].rearrange("p (h n) -> p h n", h=nt))
                        dve.sem_inc(bank_free[3], 1)
                        dve.sem_inc(sem("state_full"), 1)
                    take(dve, for_dve[1])
                    dst = mix[:, first_tile:first_tile + nt, t * P:(t + 1) * P]
                    src = bank[1][:, 0:nt * P].rearrange("p (h n) -> p h n", h=nt)
                    if add:
                        chain(dve.tensor_tensor(dst, dst, src, ALU.add))
                    else:
                        chain(dve.tensor_copy(dst, src))
                    dve.sem_inc(bank_free[1], 1)
            meet()
            dve.wait_ge(sem("const2_full"), 32)
            R96 = slice(0, QK_M)
            ang, turns = hT[R96, 0, :], hT[R96, 1, :]
            chain(dve.tensor_copy(ang, hT[R96, 7, :].bitcast(I32)))
            chain(dve.tensor_scalar(ang, ang, const2("invf")[R96], None, ALU.mult))
            MAGIC = 1.5 * 2.0 ** 23
            for dst, shift in ((sinM, 0.0), (cosM, 0.25)):
                chain(dve.tensor_scalar(turns, ang, float(1 / (2 * np.pi)), shift, ALU.mult, ALU.add))
                chain(dve.tensor_scalar(turns, turns, MAGIC, None, ALU.add))
                chain(dve.tensor_scalar(turns, turns, MAGIC, None, ALU.subtract))
                chain(dve.scalar_tensor_tensor(dst[R96], turns, -6.28125, ang, ALU.mult, ALU.add))
                chain(dve.scalar_tensor_tensor(dst[R96], turns, -0.00193500518798828125, dst[R96], ALU.mult, ALU.add))
                chain(dve.scalar_tensor_tensor(dst[R96], turns, -float(2 * np.pi - 6.28125 - 0.00193500518798828125), dst[R96], ALU.mult, ALU.add))
                if shift:
                    chain(dve.tensor_scalar(dst[R96], dst[R96], float(np.pi / 2), None, ALU.add))
                chain(dve.tensor_scalar(dst[R96], dst[R96], 3.1415925, -3.1415925, ALU.min, ALU.max))
            dve.sem_inc(sem("args_full"), 1)
            take(dve, sem("func_full"))
            dve.sem_inc(sem("norm_in_full"), 1)
            chain.reset()
            with dve.Fori(0, LAYERS) as l:
                take(dve, sem("par_full"), 32)
                take(dve, sem("rs_full"))
                for k in range(KD):
                    dve.scalar_tensor_tensor(hT[:, k, :], xT[:, k, :], par2("norm_g", k), rs[:], ALU.mult,
                                             ALU.mult).then_inc(sem("tiles_full"), 1)
                for i in range(2):
                    chain(dve.memset(pads[i][:, 0:2], 0.0))
                    chain(dve.memset(pads[i][:, 2 + T:4 + T], 0.0))
                dve.sem_inc(sem("rs_free"), 1)
                for i in range(9):
                    dst = g_qk[:, i, :] if i < 6 else g_v[:, i - 6, :]
                    pad = pads[i % 2]
                    take(dve, sem(f"pad_full{i % 2}"))
                    chain(dve.tensor_scalar(dst, pad[:, 0:T], par2("conv", 5 * i), None, ALU.mult))
                    for j in range(1, 5):
                        chain(dve.scalar_tensor_tensor(dst, pad[:, j:j + T], par2("conv", 5 * i + j), dst, ALU.mult, ALU.add))
                    dve.sem_inc(sem(f"pad_free{i % 2}"), 1)
                    dve.sem_inc(sem(f"conv_full{i % 2}"), 1)
                take(dve, for_dve[2])
                ab = bank[2][:, 0:96].rearrange("p (t c) -> p t c", t=TT)
                bias = row2[:, 12:24].rearrange("p (o c) -> p o c", o=1).to_broadcast([P, TT, 12])
                chain(dve.tensor_tensor(g_y, ab[:, :, 0:12], bias, ALU.add))
                chain(dve.tensor_copy(g_beta, ab[:, :, 12:24]))
                dve.sem_inc(bank_free[2], 1)
                dve.sem_inc(slot_free[0], 1)
                chain(dve.scalar_tensor_tensor(g_neg, g_y, -1.0, g_y, ALU.mult, ALU.min))
                for i in range(6):
                    times_rs(g_qk[:, i, :], g_qk[:, i, :])
                dve.sem_inc(sem("k_ch_full"), 1)
                dve.sem_inc(sem("args_full"), 1)
                take(dve, sem("func_full"))
                chain(dve.scalar_tensor_tensor(g_g, g_y, 0.0, g_ln, ALU.max, ALU.add))
                ea = g_ea.rearrange("p (o c) -> p o c", o=1).to_broadcast([P, TT, 12])
                chain(dve.scalar_tensor_tensor(g_g, g_g, -1.0, ea, ALU.mult, ALU.mult))
                dve.sem_inc(sem("g_full"), 1)
                take(dve, for_dve[2])
                chain(dve.tensor_copy(g_cum, bank[2][:, 0:48].rearrange("p (t c) -> p t c", t=TT)))
                chain(dve.tensor_copy(g_ge, bank[2][:, 64:112].rearrange("p (t c) -> p t c", t=TT)))
                chain(dve.tensor_tensor(g_dec, g_ge, g_cum, ALU.subtract))
                dve.sem_inc(bank_free[2], 1)
                dve.sem_inc(sem("args_full"), 1)
                take(dve, sem("func_full"))
                chain(dve.tensor_tensor(g_bg, g_beta, g_gam, ALU.mult))
                for s in range(2):
                    for d in range(2):
                        chain(dve.tensor_copy(g_ge2[64 * s:64 * s + 64, d], g_ge[64 * s:64 * s + 64, :, 6 * d + s:6 * d + 6:2]
                                              .rearrange("p t h -> p h t")))
                dve.sem_inc(sem("tok_full"), 1)
                for d in range(2):
                    for ht in range(3):
                        TA = g_TA
                        for s in range(2):
                            c = 6 * d + 2 * ht + s
                            XD, X, V = TA[:, 2 + s, :], TA[:, 6 + s, :], TA[:, 8 + s, :]
                            take(dve, for_dve[s])
                            chain(dve.tensor_tensor(tiles4(XD), tiles4(bank[s][:, :]), along(g_cum[:, :, c]), ALU.subtract))
                            dve.sem_inc(sem(f"cb_full{s}"), 1)
                            keep1, keep2 = ("nLE", "nGT") if d == 0 else ("nGE", "nLT")
                            chain(dve.scalar_tensor_tensor(tiles4(V), tiles4(XD), 0.0, over_tiles(const2(keep1)), ALU.min, ALU.add))
                            chain(dve.scalar_tensor_tensor(tiles4(X), tiles4(XD), 0.0, over_tiles(const2(keep2)), ALU.max, ALU.subtract))
                            dve.sem_inc(sem(f"d_args{s}"), 1)
                        for s in range(2):
                            c = 6 * d + 2 * ht + s
                            lo = 64 * s
                            A, Y, X, V = [TA[:, i + s, :] for i in (0, 4, 6, 8)]
                            take(dve, sem(f"d_full{s}"))
                            take(dve, for_dve[4 + s])
                            chain(dve.tensor_tensor(g_PT[:, 2 * ht + s, :], bank[4 + s][:, :], V, ALU.mult))
                            dve.sem_inc(bank_free[4 + s], 1)
                            take(dve, for_dve[2 + s])
                            chain(dve.tensor_tensor(A, bank[2 + s][:, :], X, ALU.mult))
                            dve.sem_inc(bank_free[2 + s], 1)
                            chain(dve.tensor_tensor(tiles4(A), tiles4(A), along(g_beta[:, :, c]), ALU.mult))
                            chain(dve.tensor_tensor(g_qg[lo:lo + 64, ht, :], g_qk[lo:lo + 64, ht, :], Y[lo:lo + 64, :], ALU.mult))
                        invert(TA, d)
                    take(dve, sem("chunks_act"))
                    dve.sem_inc(sem("chunks_full"), 1)
                    def next_state(n, t, inc):
                        new, old = g_S[:, (n + 1) % 2], g_S[:, n % 2]
                        if n == 0:
                            chain(dve.tensor_copy(new, inc))
                        else:
                            ge = g_ge2[:, d, :, t:t + 1].to_broadcast([P, 3, 64])
                            chain(dve.tensor_tensor(new, old, ge, ALU.mult))
                            chain(dve.tensor_tensor(new, new, inc, ALU.add))
                    recurrence(d, GH, g_u0, g_U, g_S, next_state, 0, d == 1)
                    if d == 0:
                        dve.sem_inc(sem("dir_done"), 1)
                dve.sem_inc(sem("norm_in_full"), 1)
                for i in range(3):
                    times_rs(mix[:, i, :], mix[:, i, :], par2("gdn_g"))
                meet()
                for i in range(2):
                    chain(dve.memset(r_pads[i][:, 0:1], 0.0))
                    chain(dve.memset(r_pads[i][:, 1 + T:2 + T], 0.0))
                chain(dve.tensor_tensor(r_c0, par2("mu0", 0, 7), par2("mu1", 0, 7), ALU.add))
                chain(dve.tensor_scalar(r_c0, r_c0, -1.0, 1.0, ALU.mult, ALU.add))
                chain(dve.tensor_scalar(r_oka, par2("k_a", 0, 2), -1.0, 1.0, ALU.mult, ALU.add))
                for i in range(7):
                    dst = r_f[:, i, :] if i < 6 else r_wa[:, 0, :]
                    pad = r_pads[i % 2]
                    take(dve, sem(f"pad_full{i % 2}"))
                    chain(dve.tensor_scalar(dst, pad[:, 1:1 + T], r_c0[:, i:i + 1], None, ALU.mult))
                    chain(dve.scalar_tensor_tensor(dst, pad[:, 0:T], par2("mu0", i), dst, ALU.mult, ALU.add))
                    chain(dve.scalar_tensor_tensor(dst, pad[:, 2:2 + T], par2("mu1", i), dst, ALU.mult, ALU.add))
                    dve.sem_inc(sem(f"pad_free{i % 2}"), 1)
                for i in range(2):
                    chain(dve.tensor_scalar(r_kk[:, i, :], r_f[:, 2 + i, :], par2("k_k", i), None, ALU.mult))
                dve.sem_inc(sem("norm_in_full"), 1)
                for i in range(2):
                    times_rs(r_kk[:, i, :], r_kk[:, i, :])
                for e in range(2):
                    TA = r_TA
                    for ct in range(2):
                        SG, AV, L, A1, A2, E_up, E_dn, E_pr, KM = [TA[:, i, :] for i in range(9)]
                        take(dve, sem("sig_full"))
                        chain(dve.tensor_tensor_scan(L, const2("reset"), SG, 0.0, ALU.mult, ALU.add))
                        mid, tot = tiles4(L)[:, :, CHUNK // 2 - 1], tiles4(L)[:, :, CHUNK - 1]
                        chain(dve.tensor_copy(r_m[:, ct, :], mid))
                        chain(dve.tensor_tensor(r_d[:, ct, :], tot, r_m[:, ct, :], ALU.subtract))
                        chain(dve.tensor_tensor(tiles4(A1), tiles4(L), along(r_m[:, ct, :]), ALU.subtract))
                        chain(dve.tensor_tensor(A2, A1, SG, ALU.subtract))
                        dve.sem_inc(sem("args_full"), 1)
                        chain(dve.tensor_scalar(KM, AV, par2("k_a", ct), r_oka[:, ct:ct + 1], ALU.mult, ALU.add))
                        chain(dve.tensor_tensor(KM, KM, r_f[:, 2 + ct, :], ALU.mult))
                        if e == 0:
                            chain(dve.tensor_copy(r_bon[:, ct, :], KM))
                        else:
                            chain(dve.tensor_tensor(r_bon[:, ct, :], r_bon[:, ct, :], KM, ALU.add))
                        chain(dve.tensor_tensor(AV, AV, r_kk[:, ct, :], ALU.mult))
                        take(dve, sem("func_full"))
                        chain(dve.tensor_tensor(r_kt[:, ct, :], r_kk[:, ct, :], E_pr, ALU.mult))
                        dve.sem_inc(sem("kt_full"), 1)
                        chain(dve.tensor_tensor(r_bt[:, ct, :], AV, E_dn, ALU.mult))
                        chain(dve.tensor_tensor(r_kmt[:, ct, :], KM, E_dn, ALU.mult))
                        chain(dve.tensor_tensor(r_rt[:, ct, :], r_f[:, ct, :], E_up, ALU.mult))
                        if ct == 0:
                            dve.sem_inc(sem("ta_free"), 1)
                    pre, post = (r_pm, r_pd) if e == 0 else (r_pd, r_pm)
                    for t in range(TT):
                        nx = t + 1 if e == 0 else t - 1
                        if 0 <= nx < TT:
                            chain(dve.tensor_tensor(r_sc[:, :, t:t + 1], post[:, :, t:t + 1], pre[:, :, nx:nx + 1], ALU.mult))
                    for ct in range(2):
                        for s in range(2):
                            h = 2 * ct + s
                            after, incl, A_keep = ("LT", "LE", "GT") if e == 0 else ("GT", "GE", "LT")
                            for b, dst, m in ((s, TA[:, s, :], A_keep), (2 + s, r_BT[s], after),
                                              (4 + s, r_PbT[:, h, :], incl), (6 + s, r_PkT[:, s, :], incl)):
                                take(dve, for_dve[b])
                                chain(dve.tensor_tensor(tiles4(dst), tiles4(bank[b][:, :]), over_tiles(const2(m)), ALU.mult))
                                dve.sem_inc(bank_free[b], 1)
                        dve.sem_inc(sem("bp_full"), 1)
                        take(dve, sem("direct_full"))
                        if e == 0:
                            chain(dve.tensor_copy(mix[:, 6 + ct, :], bank[7][:, :]))
                        else:
                            chain(dve.tensor_tensor(mix[:, 6 + ct, :], mix[:, 6 + ct, :], bank[7][:, :], ALU.add))
                        dve.sem_inc(bank_free[7], 1)
                        invert(TA, e)
                    take(dve, sem("chunks_act"))
                    dve.sem_inc(sem("chunks_full"), 1)
                    def next_state(n, t, inc):
                        new, old = r_S[:, (n + 1) % 2], r_S[:, n % 2]
                        sc = r_sc[:, :, t:t + 1].to_broadcast([P, 2, 64])
                        if n == 0:
                            chain(dve.tensor_tensor(new, inc, sc, ALU.mult))
                        else:
                            chain(dve.tensor_tensor(new, old, inc, ALU.add))
                            chain(dve.tensor_tensor(new, new, sc, ALU.mult))
                    recurrence(e, RH, r_u0, r_U, r_S, next_state, 6, True)
                    if e == 0:
                        dve.sem_inc(sem("ta_free"), 1)
                dve.sem_inc(sem("ta_free"), 1)
                for i in range(2):
                    y = mix[:, 6 + i, :]
                    dve.sem_inc(sem("y_full"), 1)
                    take(dve, for_dve[5])
                    chain(dve.scalar_tensor_tensor(y, bank[5][:, :], -1.0 / 64, y, ALU.mult, ALU.add))
                    dve.sem_inc(bank_free[5], 1)
                    dve.sem_inc(sem("norm_in_full"), 1)
                    chain(dve.scalar_tensor_tensor(r_bon[:, i, :], r_bon[:, i, :], par2("r_k", i), r_f[:, i, :], ALU.mult, ALU.mult))
                    dve.sem_inc(sem("bonus_full"), 1)
                    times_rs(y, y)
                    chain(dve.tensor_scalar(y, y, par2("ln_g", i), par2("ln_b", i), ALU.mult, ALU.add))
                    take(dve, for_dve[7])
                    chain(dve.tensor_tensor(r_kt[:, i, :], bank[7][:, :], r_f[:, 4 + i, :], ALU.mult))
                    dve.sem_inc(bank_free[7], 1)
                    chain(dve.scalar_tensor_tensor(y, r_kt[:, i, :], 0.5, y, ALU.mult, ALU.add))
                meet()
                take(dve, sem("rs_full"))
                chain(dve.scalar_tensor_tensor(m_cq[:, 0, :], m_cq[:, 0, :], par2("qn_g"), rs[:], ALU.mult, ALU.mult))
                chain(dve.scalar_tensor_tensor(m_cq[0:64, 1, :], m_cq[0:64, 1, :], par2("qn_g", 1)[0:64], rs[0:64, :], ALU.mult, ALU.mult))
                dve.sem_inc(sem("rs_free"), 1)
                dve.sem_inc(sem("latent_in_full"), 1)
                times_rs(m_ckv[:, 0, :], m_ckv[:, 0, :], par2("kvn_g"))
                dve.sem_inc(sem("latent_in_full"), 1)
                rot = slice(64, 96)
                def rotate(x, b, j):
                    take(dve, for_dve[b])
                    chain(dve.tensor_tensor(m_tmp[rot, j, :], bank[b][rot, :], sinM[rot, :], ALU.mult))
                    dve.sem_inc(bank_free[b], 1)
                    chain(dve.tensor_tensor(x, x, cosM[rot, :], ALU.mult))
                    chain(dve.tensor_tensor(x, x, m_tmp[rot, j, :], ALU.add))
                rotate(m_kr[rot, 0, :], 3, 0)
                dve.sem_inc(sem("kr_full"), 1)
                for h in range(MH):
                    rotate(m_q[rot, h, :], 2 + h % 2, h % 2)
                    if h == MH - 1:
                        take(dve, sem("k_rot_full"))
                    dve.sem_inc(sem("mla_q_full"), 1)
                n = MH * TT
                for i in range(n + 1):
                    if i < n:
                        st = m_st[:, i % 2]
                        take(dve, for_dve[i % 2])
                        chain(dve.tensor_reduce(st[:, 2:3], bank[i % 2][:, :], AX.X, ALU.max))
                        chain(dve.tensor_scalar(st[:, 0:1], st[:, 2:3], -QK_M ** -0.5, None, ALU.mult))
                        dve.sem_inc(sem(f"max_full{i % 2}0"), 1)
                    if i >= 1:
                        j = (i - 1) % 2
                        st = m_st[:, j]
                        take(dve, sem(f"probs_full{j}"))
                        chain(dve.reciprocal(st[:, 3:4], st[:, 1:2]))
                        chain(dve.tensor_scalar(m_pr[:, j, :], m_pr[:, j, :], st[:, 3:4], None, ALU.mult))
                        dve.sem_inc(sem(f"wgt_full{j}"), 1)
                for i in range(8):
                    take(dve, sem(f"sg_full{i % 2}"))
                    chain(dve.tensor_tensor(mix[:, i, :], mix[:, i, :], m_gate[:, i % 2, :], ALU.mult))
                    dve.sem_inc(sem(f"sg_free{i % 2}"), 1)
                    dve.sem_inc(sem("tiles_full"), 1)
                for m_ in range(8):
                    b = 4 + m_ % 4
                    take(dve, for_dve[b])
                    chain(dve.tensor_tensor(xT[:, m_, :], xT[:, m_, :], bank[b][:, :], ALU.add))
                    dve.sem_inc(bank_free[b], 1)
                    if m_ % 4 == 3:
                        dve.sem_inc(slot_free[(8 + m_ // 4) % 2], 1)
                dve.sem_inc(sem("par_free"), 1)
                dve.sem_inc(sem("norm_in_full"), 1)
                chain.reset()
            take(dve, sem("rs_full"))
            for k in range(KD):
                chain(dve.scalar_tensor_tensor(hT[:, k, :], xT[:, k, :], par("final2_g", k), rs[:], ALU.mult, ALU.mult))
            dve.sem_inc(sem("done"), 1)

        block = ctx.enter_context(nc.Block())

        @block.sync
        def _(sp):
            for n, u in enumerate(units):
                take(sp, slot_free[n % SLOTS])
                sp.dma_start(slot(n), u).then_inc(slot_full[n % SLOTS], 16)
                if n == 0:
                    sp.dma_start(xT[:], xT_d.rearrange("(k p) t -> p k t", p=P)).then_inc(sem("x_loaded"), 16)
            def expert_weights(e_j, e, ring_at):
                for i, (w, k) in enumerate(((w_gate, 8), (w_up, 8), (w_down, 4))):
                    take(sp, slot_free[ring_at + i])
                    src = w[0].rearrange("(i j) d n -> i j d n", j=1 if e_j is None else 2)
                    src = src[bass.ds(e, 1), 0 if e_j is None else e_j].rearrange("a (k p) n -> p (a k) n", p=P)
                    sp.dma_start(slot(ring_at + i, k), src).then_inc(slot_full[ring_at + i], 16)
            with sp.Fori(0, N_EXP // 2) as pair:
                for j in range(2):
                    expert_weights(j, pair, 3 * j)
            sp.wait_ge(sem("routed"), 2)
            n_more = sp.value_load(meta[0:1, 7:8], min_val=0, max_val=N_MORE)
            with sp.Fori(0, N_MORE) as m:
                with sp.If(m < n_more):
                    expert = sp.value_load(meta[0:1, bass.ds(m, 1)], min_val=0, max_val=N_EXP - 1)
                    expert_weights(None, expert, 0)
            sp.wait_ge(sem("y_stored"), 1)
            for t in range(TT):
                sp.dma_start(y_tok[:, t], y_d[2 * t * P:2 * (t + 1) * P, :].rearrange("(p k) d -> p k d", k=2))\
                  .then_inc(sem("y_loaded"), 16)
            sp_second(sp)

        @block.gpsimd
        def _(pool):
            for b in range(8):
                pool.sem_inc(bank_free[b], 1)
            for s in range(SLOTS):
                pool.sem_inc(slot_free[s], 1)
            for name in ("rs_free",):
                pool.sem_inc(sem(name), 1)
            for j in range(2):
                pool.sem_inc(sem(f"sg_free{j}"), 1)
                pool.sem_inc(sem(f"x_free{j}"), 2)
                pool.sem_inc(sem(f"sq_free{j}"), 1)
                pool.sem_inc(sem(f"probs_free{j}"), 1)
                pool.sem_inc(sem(f"wgt_free{j}"), 1)
                pool.sem_inc(sem(f"wT_free{j}"), 1)
            pool.memset(u_pad, 0.0).then_inc(sem("pad_zero"), 1)
            pool.wait_ge(sem("scores_done"), 1)
            for g in range(4):
                pool.dma_start(inv_c[:, g, :], invcnt[g:g + 1, :].to_broadcast([P, T])).then_inc(sem("inv_loaded"), 16)
            pchain = Chain(pool, sem("pool_chain"))
            pool.wait_ge(sem("pooled"), 1)
            pchain(pool.memset(info, NO_SLOT))
            pool.dma_start(slot_d.rearrange("(s b) c -> s b c", s=P), info).then_inc(sem("slot_table"), 16)
            pool.wait_ge(sem("slot_table"), 16)
            pool.wait_ge(sem("routed"), 1)
            for k in range(2):
                for t in range(TT):
                    pool.indirect_dma_start(
                        slot_d, bass.IndirectOffsetOnAxis(ap=dest[:, k, t:t + 1], axis=0), rows[:, k, t, :], None,
                        bounds_check=N_BLK * P - 1, oob_is_err=False).then_inc(sem("slot_table"), 16)
            pool.wait_ge(sem("slot_table"), 16 + 16 * 2 * TT)
            pool.dma_start(info, slot_d.rearrange("(b s) c -> s b c", s=P)).then_inc(sem("slot_table"), 16)
            pool.wait_ge(sem("slot_table"), 32 + 16 * 2 * TT)
            pool.wait_ge(sem("h_stored"), 16 * TT)
            for j in range(2):
                pchain(pool.memset(X[j], 0.0))
            def gather(j, block, number, stored=None):
                if stored is not None:
                    pool.wait_ge(sem("rows_stored"), stored * 16)
                pool.sem_inc(sem(f"yb_free{j}"), 1)
                take(pool, sem(f"x_free{j}"), 2)
                pchain(pool.tensor_copy(cur[j], info[:, block, :].rearrange("p a c -> p (a c)") if not isinstance(block, int)
                                        else info[:, block, :]))
                pool.indirect_dma_start(
                    X[j], None, h_d, bass.IndirectOffsetOnAxis(ap=cur[j][:, 0:1].bitcast(U32), axis=0),
                    bounds_check=T - 1, oob_is_err=False).then_inc(sem("rows_loaded"), 16)
                pool.wait_ge(sem("rows_loaded"), number * 16)
                pool.sem_inc(sem(f"x_full{j}"), 1)
            def scatter(j):
                take(pool, sem(f"y_full{j}"))
                pool.indirect_dma_start(
                    y_d, bass.IndirectOffsetOnAxis(ap=cur[j][:, 1:2].bitcast(U32), axis=0), Yb[j], None,
                    bounds_check=2 * T - 1, oob_is_err=False).then_inc(sem("rows_stored"), 16)
            gather(0, 0, 1)
            gather(1, 1, 2)
            scatter(0)
            pchain.reset()
            with pool.Fori(0, N_EXP // 2 - 1) as pair:
                for j in range(2):
                    gather(j, bass.ds(2 * pair + 2 + j, 1), 2 * pair + 3 + j, 2 * pair + 1 + j)
                    scatter(1 - j)
                pchain.reset()
            scatter(1)
            pool.wait_ge(sem("routed"), 2)
            n_more = pool.value_load(meta[0:1, 7:8], min_val=0, max_val=N_MORE)
            with pool.Fori(0, N_MORE) as m:
                with pool.If(m < n_more):
                    gather(0, bass.ds(m + N_EXP, 1), m + N_EXP + 1, m + N_EXP)
                    scatter(0)
                    pchain.reset()
            pool.wait_ge(sem("rows_stored"), (n_more + N_EXP) * 16)
            pool.sem_inc(sem("y_stored"), 1)
            pool_second(pool)

        @block.tensor
        def _(pe):
            def sumsq(b, tiles, n0, mat=ones, rows=None):
                take(pe, bank_free[b])
                for i in range(tiles):
                    take(pe, sem(f"sq_full{(n0 + i) % 2}"))
                    r = P if rows is None else rows[i]
                    m = pe.matmul(bank[b][:, :], mat[0:r, :], sq[0:r, (n0 + i) % 2, :], start=(i == 0), stop=(i == tiles - 1))
                    if i < tiles - 1:
                        m.then_inc(sem(f"sq_free{(n0 + i) % 2}"), 1)
                m.then_inc(for_act[b], 1)

            pe.wait_ge(sem("params_loaded"), 16 * 3)
            pe.wait_ge(sem("silu_c"), 1)

            def modulation(first, n_units, b, ring_at):
                take(pe, bank_free[b])
                for n in range(n_units):
                    s = (ring_at + n) % SLOTS
                    take(pe, slot_full[s], 16)
                    for m in range(4):
                        col = (n * 4 + m)
                        for k in range(KD):
                            mm = pe.matmul(bank[b][:, col:col + 1], slot(s)[:, k, m * P:(m + 1) * P],
                                           small[:, k:k + 1], start=(k == 0), stop=(k == KD - 1))
                    if n < n_units - 1:
                        mm.then_inc(slot_free[s], 1)
                mm.then_inc(for_dve[b], 1)
                pe.wait_ge(sem("mod_ready"), first // 16 + 1)
                pe.sem_inc(slot_free[s], 1)

            modulation(0, 4, 0, 0)
            sumsq(1, KD, 0)
            for n in range(2):
                s = (4 + n) % SLOTS
                take(pe, slot_full[s], 16)
                for m in range(4):
                    i = n * 4 + m
                    b = 2 + i % 2
                    take(pe, bank_free[b])
                    for k in range(KD):
                        if n == 0 and m == 0:
                            pe.wait_ge(sem("h_ready"), k + 1)
                        mm = pe.matmul(bank[b][:, :], slot(s)[:, k, m * P:(m + 1) * P], hT[:, k, :],
                                       start=(k == 0), stop=(k == KD - 1))
                    mm.then_inc(for_act[b], 1)
                    if i > 0:
                        j = i - 1
                        pe.wait_ge(sem("raw_ready"), j + 1)
                        take(pe, bank_free[4 + j % 2])
                        pe.matmul(bank[4 + j % 2][:, :], const("rotA"), raw[:, j % 2, :], start=True,
                                  stop=True).then_inc(for_dve[4 + j % 2], 1)
                pe.wait_ge(sem("raw_ready"), n * 4 + 4)
                pe.sem_inc(slot_free[s], 1)
            take(pe, bank_free[5])
            pe.matmul(bank[5][:, :], const("rotA"), raw[:, 1, :], start=True, stop=True).then_inc(for_dve[5], 1)
            s = 6 % SLOTS
            take(pe, slot_full[s], 16)
            for t in range(TT):
                b = 2 + t % 2
                take(pe, bank_free[b])
                for k in range(KD):
                    mm = pe.matmul(bank[b][:, :], hT[:, k, t * P:(t + 1) * P], slot(s)[:, k, :],
                                   start=(k == 0), stop=(k == KD - 1))
                mm.then_inc(for_act[b], 1)
            pe.wait_ge(sem("v_ready"), TT)
            pe.sem_inc(slot_free[s], 1)
            s = 7 % SLOTS
            take(pe, slot_full[s], 16)
            for m in range(4):
                b = 2 + m % 2
                take(pe, bank_free[b])
                for k in range(KD):
                    mm = pe.matmul(bank[b][:, :], slot(s)[:, k, m * P:(m + 1) * P], hT[:, k, :],
                                   start=(k == 0), stop=(k == KD - 1))
                mm.then_inc(for_act[b], 1)
            pe.wait_ge(sem("u_ready"), 4)
            pe.sem_inc(slot_free[s], 1)
            modulation(16, 4, 0, 8)
            modulation(32, 4, 0, 12)

            steps = [(h, q) for h in range(HEADS) for q in range(TT)]
            def scores(i):
                h, q = steps[i]
                for c in range(2):
                    b = 2 * (i % 2) + c
                    take(pe, bank_free[b])
                    lo = c * HD
                    pe.matmul(bank[b][:, :], qkT[lo:lo + HD, h, q * P:(q + 1) * P], qkT[lo:lo + HD, 4 + h, :],
                              start=True, stop=True).then_inc(for_dve[b], 1)
            def weights(i):
                h, q = steps[i]
                take(pe, sem(f"wgt_full{i % 2}"))
                b = 4 + i % 2
                take(pe, bank_free[b])
                for kt in range(TT):
                    mm = pe.transpose(bank[b][:, kt * P:(kt + 1) * P], wgt[:, i % 2, kt * P:(kt + 1) * P], ident)
                mm.then_inc(for_act[b], 1)
            def values(i):
                h, q = steps[i]
                take(pe, sem(f"wT_full{i % 2}"))
                b = 6 + h % 2
                if q == 0:
                    take(pe, bank_free[b])
                for kt in range(TT):
                    mm = pe.matmul(bank[b][:, q * P:(q + 1) * P], v_tok[:, kt, h * P:(h + 1) * P],
                                   wTq[:, i % 2, kt * P:(kt + 1) * P], start=(kt == 0), stop=(kt == TT - 1))
                if q == TT - 1:
                    mm.then_inc(for_act[b], 1)
                else:
                    mm.then_inc(sem(f"wT_free{i % 2}"), 1)
            pe.wait_ge(sem("qk_ready"), 8)
            for i in range(len(steps) + 2):
                if i < len(steps):
                    scores(i)
                if 1 <= i <= len(steps):
                    weights(i - 1)
                if i >= 2:
                    values(i - 2)
            for h in range(HEADS):
                sumsq(h % 2, 1, h)
            pe.wait_ge(sem("pool_w_loaded"), 16)
            for g in range(4):
                b = 2 + g % 2
                take(pe, bank_free[b])
                pe.wait_ge(sem("pooled"), g + 1)
                pe.matmul(bank[b][:, :], pool_w[:, g, :], u_pad[:, g, 0:T], start=True,
                          stop=True).then_inc(for_act[b], 1)
            pe.wait_ge(sem("mix_ready"), 8)
            for n in range(2):
                s = (16 + n) % SLOTS
                take(pe, slot_full[s], 16)
                for m in range(4):
                    b = 4 + m
                    take(pe, bank_free[b])
                    for k in range(KD):
                        mm = pe.matmul(bank[b][:, :], slot(s)[:, k, m * P:(m + 1) * P], mixT[:, k, :],
                                       start=(k == 0), stop=(k == KD - 1))
                    mm.then_inc(for_dve[b], 1)
                pe.wait_ge(sem("x_mixed"), 4 * n + 4)
                pe.sem_inc(slot_free[s], 1)
            sumsq(1, KD, 0)
            pe.wait_ge(sem("router_loaded"), 32)
            pe.wait_ge(sem("h_ready"), 2 * KD)
            take(pe, bank_free[0])
            for t in range(TT):
                for k in range(KD):
                    mm = pe.matmul(bank[0][:, t * 36:(t + 1) * 36], hT[:, k, t * P:(t + 1) * P], w_router[:, k, :],
                                   start=(k == 0), stop=(k == KD - 1))
            mm.then_inc(for_dve[0], 1)
            for t in range(TT):
                for c in range(2):
                    b = 1 + c
                    take(pe, bank_free[b])
                    for k in range(4):
                        mm = pe.transpose(bank[b][:, k * P:(k + 1) * P], hT[:, 4 * c + k, t * P:(t + 1) * P], ident)
                    mm.then_inc(for_act[b], 1)
            pe.wait_ge(sem("choices_full"), 1)
            take(pe, bank_free[0])
            for t in range(TT):
                for i in range(t):
                    pe.matmul(bank[0][:, t * N_EXP:(t + 1) * N_EXP], ones, Ms[:, i, :], start=(i == 0), stop=False)
                pe.matmul(bank[0][:, t * N_EXP:(t + 1) * N_EXP], const("lt"), Ms[:, t, :], start=(t == 0), stop=True)
            for t in range(TT):
                mm = pe.matmul(bank[0][:, TT * N_EXP:(TT + 1) * N_EXP], ones, Ms[:, t, :], start=(t == 0), stop=(t == TT - 1))
            mm.then_inc(for_dve[0], 1)

            def turn_inputs(j):
                take(pe, sem(f"x_full{j}"))
                for c, reader in ((0, for_act), (1, for_dve)):
                    take(pe, bank_free[c])
                    for k in range(4):
                        mm = pe.transpose(bank[c][:, k * P:(k + 1) * P], X[j][:, (4 * c + k) * P:(4 * c + k + 1) * P], ident)
                    mm.then_inc(reader[c], 1)
            def gate_up(j, ring_at):
                take(pe, sem(f"xt_full{j}"), 2)
                for i, reader in ((0, for_act), (1, for_dve)):
                    take(pe, slot_full[ring_at + i], 16)
                    take(pe, bank_free[2 + i])
                    for k in range(KD):
                        mm = pe.matmul(bank[2 + i][:, :], XT[j][:, k, :], slot(ring_at + i)[:, k, :], start=(k == 0),
                                       stop=(k == KD - 1))
                    mm.then_inc(reader[2 + i], 1)
            def down(j, ring_at):
                take(pe, sem(f"hid_full{j}"))
                take(pe, bank_free[4])
                for f in range(4):
                    mm = pe.transpose(bank[4][:, f * P:(f + 1) * P], hid[:, j, f * P:(f + 1) * P], ident)
                mm.then_inc(for_act[4], 1)
                take(pe, slot_full[ring_at + 2], 16)
                take(pe, sem(f"hidT_full{j}"))
                for c in range(2):
                    take(pe, bank_free[5 + c])
                    for f in range(4):
                        mm = pe.matmul(bank[5 + c][:, :], hidT[:, j, f * P:(f + 1) * P],
                                       slot(ring_at + 2, 4)[:, f, c * 512:(c + 1) * 512], start=(f == 0), stop=(f == 3))
                    mm.then_inc(for_act[5 + c], 1)
            turn_inputs(0)
            with pe.Fori(0, N_EXP // 2 - 1) as pair:
                for j in range(2):
                    gate_up(j, 3 * j)
                    turn_inputs(1 - j)
                    down(j, 3 * j)
            gate_up(0, 0)
            turn_inputs(1)
            down(0, 0)
            gate_up(1, 3)
            down(1, 3)
            pe.wait_ge(sem("routed"), 2)
            n_more = pe.value_load(meta[0:1, 7:8], min_val=0, max_val=N_MORE)
            with pe.Fori(0, N_MORE) as m:
                with pe.If(m < n_more):
                    turn_inputs(0)
                    gate_up(0, 0)
                    down(0, 0)
            pe.wait_ge(sem("y_summed"), TT)
            for d in range(KD):
                b = d % 4
                take(pe, bank_free[b])
                for t in range(TT):
                    mm = pe.transpose(bank[b][:, t * P:(t + 1) * P], y_tok[:, t, 0, d * P:(d + 1) * P], ident)
                mm.then_inc(for_dve[b], 1)
            sumsq(1, KD, 0)
            pe_second(pe, sumsq)

        @block.scalar
        def _(act):
            chain = Chain(act, sem("act_chain"))
            act.dma_start(p1[:], par1).then_inc(sem("params_loaded"), 16)
            act.dma_start(c_sb[:], cn).then_inc(sem("params_loaded"), 16)
            act.dma_start(r1[:], row1.to_broadcast([P, N_R1])).then_inc(sem("params_loaded"), 16)
            act.dma_start(pool_w[:], w_pool[0].rearrange("g c d -> c g d")).then_inc(sem("pool_w_loaded"), 16)
            act.dma_start(w_router[:, :, 0:4], w_rg[0].rearrange("(k p) n -> p k n", p=P)).then_inc(sem("router_loaded"), 16)
            act.dma_start(w_router[:, :, 4:36], w_re[0].rearrange("(k p) n -> p k n", p=P)).then_inc(sem("router_loaded"), 16)
            act.wait_ge(sem("params_loaded"), 48)
            act.activation(small[:, 0:8], par("c", 0, 8), ACT.Silu).then_inc(sem("silu_c"), 1)
            take(act, sem("args_full"))
            act.activation(small[:, 18:20], small[:, 16:18], ACT.Exp).then_inc(sem("func_full"), 1)

            def squares(src, tiles, n0=0):
                for i in range(tiles):
                    j = (n0 + i) % 2
                    take(act, sem(f"sq_free{j}"))
                    act.activation(sq[:, j, :], src(i), ACT.Square).then_inc(sem(f"sq_full{j}"), 1)

            def inverse_root(b, scale, last=1):
                take(act, for_act[b])
                chain(act.activation(rs[:], bank[b][:, :], ACT.Ln, bias=eps_col, scale=scale))
                act.sem_inc(bank_free[b], 1)
                act.sem_inc(sem(f"sq_free{last}"), 1)
                act.activation(rs[:], rs[:], ACT.Exp, scale=-0.5).then_inc(sem("rs_ready"), 1)

            act.wait_ge(sem("x_loaded"), 16)
            squares(lambda i: xT[:, i, :], KD)
            inverse_root(1, 1.0 / D)
            act.wait_ge(sem("mod_ready"), 1)
            for k in range(KD):
                act.wait_ge(sem("scaled"), k + 1)
                act.activation(hT[:, k, :], hT[:, k, :], ACT.Identity, bias=mod[:, k:k + 1]).then_inc(sem("h_ready"), 1)
            for i in range(8):
                b = 2 + i % 2
                take(act, for_act[b])
                if i >= 2:
                    act.wait_ge(sem("qk_ready"), i - 1)
                chain(act.activation(raw[:, i % 2, :], bank[b][:, :], ACT.Copy))
                act.sem_inc(bank_free[b], 1)
                act.sem_inc(sem("raw_ready"), 1)
            for t in range(TT):
                b = 2 + t % 2
                take(act, for_act[b])
                chain(act.activation(v_tok[:, t, :], bank[b][:, :], ACT.Copy))
                act.sem_inc(bank_free[b], 1)
                act.sem_inc(sem("v_ready"), 1)
            act.wait_ge(sem("pad_zero"), 1)
            for m in range(4):
                b = 2 + m % 2
                take(act, for_act[b])
                chain(act.activation(u_pad[:, m, POOL_PAD:POOL_PAD + T], bank[b][:, :], ACT.Copy))
                act.sem_inc(bank_free[b], 1)
                act.sem_inc(sem("u_ready"), 1)

            steps = [(h, q) for h in range(HEADS) for q in range(TT)]
            def exps(i):
                take(act, sem(f"probs_free{i % 2}"))
                for c in range(2):
                    b = 2 * (i % 2) + c
                    take(act, sem(f"max_full{i % 2}{c}"))
                    chain(act.activation(probs[:, i % 2, c, :], bank[b][:, :], ACT.Exp,
                                         bias=stat[:, i % 2, c:c + 1], scale=HD ** -0.5,
                                         accum_out=stat[:, i % 2, 2 + c:3 + c]))
                    act.sem_inc(bank_free[b], 1)
                act.sem_inc(sem(f"probs_full{i % 2}"), 1)
            def move(i):
                h, q = steps[i]
                b = 4 + i % 2
                take(act, for_act[b])
                act.sem_inc(sem(f"wgt_free{i % 2}"), 1)
                take(act, sem(f"wT_free{i % 2}"))
                chain(act.activation(wTq[:, i % 2, :], bank[b][:, :], ACT.Copy))
                act.sem_inc(bank_free[b], 1)
                act.sem_inc(sem(f"wT_full{i % 2}"), 1)
            def head_out(h):
                b = 6 + h % 2
                take(act, for_act[b])
                chain(act.activation(mixT[:, h, :], bank[b][:, :], ACT.Copy))
                act.sem_inc(bank_free[b], 1)
                act.sem_inc(sem("wT_free1"), 1)
            for i in range(len(steps) + 3):
                if i < len(steps):
                    exps(i)
                if i >= 3 and steps[i - 3][1] == TT - 1:
                    head_out(steps[i - 3][0])
                if 1 <= i <= len(steps):
                    move(i - 1)
                if i == len(steps):
                    act.sem_inc(sem("scores_done"), 1)
            for h in range(HEADS):
                take(act, sem(f"sq_free{h % 2}"))
                if h >= 1:
                    act.wait_ge(sem("mix_ready"), h)
                act.activation(sq[:, h % 2, :], mixT[:, h, :], ACT.Square).then_inc(sem(f"sq_full{h % 2}"), 1)
                take(act, for_act[h % 2])
                chain(act.activation(rs[:], bank[h % 2][:, :], ACT.Ln, bias=eps_col, scale=1.0 / P))
                act.sem_inc(bank_free[h % 2], 1)
                act.sem_inc(sem(f"sq_free{h % 2}"), 1)
                act.activation(rs[:], rs[:], ACT.Exp, scale=-0.5).then_inc(sem("rs_ready"), 1)
            for g in range(4):
                take(act, for_act[2 + g % 2])
                chain(act.activation(mixT[:, 4 + g, :], bank[2 + g % 2][:, :], ACT.Copy, scale=par("pool_scale", g)))
                act.sem_inc(bank_free[2 + g % 2], 1)
                act.sem_inc(sem("mix_ready"), 1)
            act.wait_ge(sem("x_mixed"), 8)
            squares(lambda i: xT[:, i, :], KD)
            inverse_root(1, 1.0 / D)
            for k in range(KD):
                act.wait_ge(sem("scaled"), KD + k + 1)
                act.activation(hT[:, k, :], hT[:, k, :], ACT.Identity, bias=mod[:, 24 + k:25 + k]).then_inc(sem("h_ready"), 1)
            take(act, sem("args_full"))
            act.activation(rt_exp, rt_arg, ACT.Exp).then_inc(sem("func_full"), 1)
            for t in range(TT):
                for c in range(2):
                    b = 1 + c
                    take(act, for_act[b])
                    chain(act.activation(h_tok[:, t, c * 512:(c + 1) * 512], bank[b][:, :], ACT.Copy))
                    act.sem_inc(bank_free[b], 1)
                act.dma_start(h_d[t * P:(t + 1) * P, :], h_tok[:, t, :]).then_inc(sem("h_stored"), 16)
            act.wait_ge(sem("h_stored"), 16 * TT)

            def turned(j):
                take(act, for_act[0])
                chain(act.activation(XT[j][:, 0:4, :].rearrange("p k n -> p (k n)"), bank[0][:, :], ACT.Copy))
                act.sem_inc(bank_free[0], 1)
                act.sem_inc(sem(f"xt_full{j}"), 1)
                act.sem_inc(sem(f"x_free{j}"), 1)
            def gated(j, ring_at):
                take(act, for_act[2])
                take(act, sem(f"sg_free{j}"))
                chain(act.activation(sg[:, j, :], bank[2][:, :], ACT.Silu))
                act.sem_inc(bank_free[2], 1)
                act.sem_inc(slot_free[ring_at], 1)
                act.sem_inc(sem(f"sg_full{j}"), 1)
            def downed(j, ring_at):
                take(act, for_act[4])
                chain(act.activation(hidT[:, j, :], bank[4][:, :], ACT.Copy))
                act.sem_inc(bank_free[4], 1)
                act.sem_inc(sem(f"hidT_full{j}"), 1)
                take(act, sem(f"yb_free{j}"))
                for c in range(2):
                    take(act, for_act[5 + c])
                    chain(act.activation(Yb[j][:, c * 512:(c + 1) * 512], bank[5 + c][:, :], ACT.Copy))
                    act.sem_inc(bank_free[5 + c], 1)
                act.sem_inc(slot_free[ring_at + 2], 1)
                act.sem_inc(sem(f"y_full{j}"), 1)
            turned(0)
            chain.reset()
            with act.Fori(0, N_EXP // 2 - 1) as pair:
                for j in range(2):
                    gated(j, 3 * j)
                    turned(1 - j)
                    downed(j, 3 * j)
                chain.reset()
            gated(0, 0)
            turned(1)
            downed(0, 0)
            gated(1, 3)
            downed(1, 3)
            chain.reset()
            act.wait_ge(sem("routed"), 2)
            n_more = act.value_load(meta[0:1, 7:8], min_val=0, max_val=N_MORE)
            with act.Fori(0, N_MORE) as m:
                with act.If(m < n_more):
                    turned(0)
                    gated(0, 0)
                    downed(0, 0)
                    chain.reset()
            act.wait_ge(sem("x_moe"), 8)
            squares(lambda i: xT[:, i, :], KD)
            inverse_root(1, 1.0 / D)
            act_second(act, chain)

        @block.vector
        def _(dve):
            chain = Chain(dve, sem("dve_chain"))
            dve.wait_ge(sem("params_loaded"), 48)
            lam = r1[:, 0:256].rearrange("p (a b c) -> p a b c", a=2, b=2)
            lam_p = small[:, 128:256].rearrange("p (a c) -> p a c", a=2)
            chain(dve.tensor_tensor(lam_p, lam[:, :, 0, :], lam[:, :, 1, :], ALU.mult))
            dve.tensor_reduce(small[:, 16:18], lam_p, AX.X, ALU.add).then_inc(sem("args_full"), 1)
            take(dve, sem("func_full"))
            chain(dve.tensor_tensor(small[:, 20:21], small[:, 18:19], small[:, 19:20], ALU.subtract))
            chain(dve.tensor_scalar(small[:, 21:22], small[:, 20:21], 0.2, None, ALU.add))
            chain(dve.tensor_scalar(subln, par("subln_g"), 0.8, None, ALU.mult))

            def modulation(first, n_units, b):
                take(dve, for_dve[b])
                c0 = first
                chain(dve.tensor_tensor(mod[:, c0:c0 + 16], bank[b][:, 0:16], par("b_ada", c0, 16), ALU.add))
                dve.sem_inc(bank_free[b], 1)
                dve.sem_inc(sem("mod_ready"), 1)

            def gains(which, g):
                sc = mod[:, 24 * which + 8:24 * which + 16]
                chain(dve.tensor_scalar(gs[:, which, :], sc, 1.0, None, ALU.add))
                chain(dve.tensor_tensor(gs[:, which, :], gs[:, which, :], g, ALU.mult))

            def normed(which, n):
                dve.wait_ge(sem("rs_ready"), n)
                for k in range(KD):
                    dve.scalar_tensor_tensor(hT[:, k, :], xT[:, k, :], gs[:, which, k:k + 1], rs[:],
                                             ALU.mult, ALU.mult).then_inc(sem("scaled"), 1)

            modulation(0, 4, 0)
            gains(0, par("norm1_g", 0, 8))
            normed(0, 1)
            for i in range(8):
                b = 4 + i % 2
                dve.wait_ge(sem("raw_ready"), i + 1)
                chain(dve.tensor_tensor(qkT[:, i, :], raw[:, i % 2, :], const("cosA"), ALU.mult))
                take(dve, for_dve[b])
                chain(dve.tensor_tensor(rtmp[:, i % 2, :], bank[b][:, :], const("sinA"), ALU.mult))
                dve.sem_inc(bank_free[b], 1)
                dve.tensor_tensor(qkT[:, i, :], qkT[:, i, :], rtmp[:, i % 2, :], ALU.add).then_inc(sem("qk_ready"), 1)
            modulation(16, 4, 0)
            modulation(32, 4, 0)
            gains(1, par("norm2_g", 0, 8))
            dve.wait_ge(sem("qk_ready"), 8)
            steps = [(h, q) for h in range(HEADS) for q in range(TT)]
            def maxima(i):
                for c in range(2):
                    b = 2 * (i % 2) + c
                    take(dve, for_dve[b])
                    st = stat[:, i % 2, :]
                    chain(dve.tensor_reduce(st[:, 4 + c:5 + c], bank[b][:, :], AX.X, ALU.max))
                    dve.tensor_scalar(st[:, c:c + 1], st[:, 4 + c:5 + c], -HD ** -0.5, None,
                                      ALU.mult).then_inc(sem(f"max_full{i % 2}{c}"), 1)
            def combine(i):
                take(dve, sem(f"probs_full{i % 2}"))
                st = stat[:, i % 2, :]
                pr = probs[:, i % 2]
                chain(dve.reciprocal(st[:, 6:8], st[:, 2:4]))
                chain(dve.tensor_tensor(st[:, 7:8], st[:, 7:8], small[:, 21:22], ALU.mult))
                chain(dve.tensor_scalar(pr[:, 1, :], pr[:, 1, :], st[:, 7:8], None, ALU.mult))
                take(dve, sem(f"wgt_free{i % 2}"))
                chain(dve.scalar_tensor_tensor(wgt[:, i % 2, :], pr[:, 0, :], st[:, 6:7], pr[:, 1, :],
                                               ALU.mult, ALU.subtract))
                dve.sem_inc(sem(f"wgt_full{i % 2}"), 1)
                dve.sem_inc(sem(f"probs_free{i % 2}"), 1)
            for i in range(len(steps) + 1):
                if i < len(steps):
                    maxima(i)
                if i >= 1:
                    combine(i - 1)
            for h in range(HEADS):
                dve.wait_ge(sem("rs_ready"), 2 + h)
                dve.scalar_tensor_tensor(mixT[:, h, :], mixT[:, h, :], subln, rs[:], ALU.mult,
                                         ALU.mult).then_inc(sem("mix_ready"), 1)
            dve.wait_ge(sem("inv_loaded"), 64)
            for g, w in enumerate(POOL_W):
                n = T + 2 * POOL_PAD
                src, k, into = u_pad[:, g, :], 1, 0
                while k < w:
                    n -= k
                    chain(dve.tensor_tensor(pool_a[:, into, 0:n], src[:, 0:n], src[:, k:k + n], ALU.add))
                    src, k, into = pool_a[:, into, :], 2 * k, 1 - into
                lo = POOL_PAD - w // 2
                chain(dve.tensor_tensor(pool_a[:, into, 0:T], src[:, lo:lo + T], inv_c[:, g, :], ALU.mult))
                chain(dve.tensor_tensor(pool_a[:, into, 0:T], pool_a[:, into, 0:T],
                                        u_pad[:, g, POOL_PAD:POOL_PAD + T], ALU.subtract))
                dve.tensor_copy(u_pad[:, g, 0:T], pool_a[:, into, 0:T]).then_inc(sem("pooled"), 1)
                dve.wait_ge(sem("pooled"), g + 1)
            for m in range(8):
                take(dve, for_dve[4 + m % 4])
                chain(dve.scalar_tensor_tensor(xT[:, m, :], bank[4 + m % 4][:, :], mod[:, 16 + m:17 + m], xT[:, m, :],
                                               ALU.mult, ALU.add))
                dve.sem_inc(bank_free[4 + m % 4], 1)
                dve.sem_inc(sem("x_mixed"), 1)
            normed(1, 6)
            take(dve, for_dve[0])
            bias = r1[:, 256:292].rearrange("p (a b) -> p a b", a=1).to_broadcast([P, TT, 36])
            chain(dve.tensor_tensor(lg, bank[0][:, 0:TT * 36].rearrange("p (a b) -> p a b", a=TT), bias, ALU.add))
            dve.sem_inc(bank_free[0], 1)
            iota = const("iota").rearrange("p (a b) -> p a b", a=1)

            def first_max(vals, n, hot, mx):
                chain(dve.tensor_reduce(mx, vals, AX.X, ALU.max))
                chain(dve.tensor_tensor(rt_t[:, :, 0:n], vals, mx.to_broadcast([P, TT, n]), ALU.is_lt))
                chain(dve.scalar_tensor_tensor(rt_t[:, :, 0:n], rt_t[:, :, 0:n], 100.0,
                                               iota[:, :, 0:n].to_broadcast([P, TT, n]), ALU.mult, ALU.add))
                chain(dve.tensor_reduce(rt_i, rt_t[:, :, 0:n], AX.X, ALU.min))
                chain(dve.tensor_tensor(hot, iota[:, :, 0:n].to_broadcast([P, TT, n]),
                                        rt_i.to_broadcast([P, TT, n]), ALU.is_equal))
            gl = lg[:, :, 0:4]
            first_max(gl, 4, ohg, m_g)
            el = lg[:, :, 4:36].rearrange("p t (g e) -> p t g e", g=4)
            for t in range(TT):
                chain(dve.tensor_tensor(rt_big, el[:, t], ohg[:, t, :].rearrange("p (g o) -> p g o", o=1).to_broadcast([P, 4, 8]), ALU.mult))
                chain(dve.tensor_reduce(e_in[:, t, :], rt_big.rearrange("p g e -> p e g"), AX.X, ALU.add))
            first_max(e_in, 8, oh1, m_1)
            chain(dve.scalar_tensor_tensor(e_in2, oh1, -1e30, e_in, ALU.mult, ALU.add))
            first_max(e_in2, 8, oh2, m_2)
            chain(dve.tensor_tensor(rt_arg.rearrange("p (t n) -> p t n", t=TT)[:, :, 0:4], gl, m_g.to_broadcast([P, TT, 4]), ALU.subtract))
            dve.tensor_tensor(rt_arg.rearrange("p (t n) -> p t n", t=TT)[:, :, 4:5], m_2, m_1, ALU.subtract).then_inc(sem("args_full"), 1)
            take(dve, sem("func_full"))
            ex = rt_exp.rearrange("p (t n) -> p t n", t=TT)
            den, w1, w2_ = rt_s[:, 0], rt_s[:, 1], rt_s[:, 2]
            chain(dve.tensor_reduce(den, ex[:, :, 0:4], AX.X, ALU.add))
            chain(dve.tensor_scalar(w1, ex[:, :, 4:5], 1.0, None, ALU.add))
            chain(dve.tensor_tensor(w1, w1, den, ALU.mult))
            chain(dve.reciprocal(w1, w1))
            chain(dve.tensor_tensor(w2_, w1, ex[:, :, 4:5], ALU.mult))
            for M, oh in ((M1, oh1), (M2, oh2)):
                for g in range(4):
                    chain(dve.tensor_tensor(M[:, :, 8 * g:8 * g + 8], oh, ohg[:, :, g:g + 1].to_broadcast([P, TT, 8]), ALU.mult))
            chain(dve.tensor_tensor(Ms, M1, M2, ALU.add))
            dve.sem_inc(sem("choices_full"), 1)
            take(dve, for_dve[0])
            chain(dve.tensor_copy(posn, bank[0][:, 0:TT * N_EXP].rearrange("p (t e) -> p t e", t=TT)))
            chain(dve.tensor_copy(cnt, bank[0][:, TT * N_EXP:(TT + 1) * N_EXP]))
            dve.sem_inc(bank_free[0], 1)
            chain(dve.tensor_scalar(nblk, cnt, 128.0, None, ALU.is_gt))
            for full in (256.0, 384.0):
                chain(dve.scalar_tensor_tensor(nblk, cnt, full, nblk, ALU.is_gt, ALU.add))
            chain(dve.tensor_tensor_scan(ends, ones[:, 0:N_EXP], nblk, 0.0, ALU.mult, ALU.add))
            ex32 = const("iota")
            chain(dve.tensor_tensor(base, ends, nblk, ALU.subtract))
            chain(dve.tensor_tensor(base, base, ex32, ALU.subtract))
            chain(dve.tensor_scalar(base, base, 128.0, float((N_EXP - 1) * P), ALU.mult, ALU.add))
            over_t = lambda v: v.rearrange("p (o e) -> p o e", o=1).to_broadcast([P, TT, N_EXP])
            chain(dve.scalar_tensor_tensor(prod, posn, 128.0, over_t(base), ALU.is_ge, ALU.mult))
            chain(dve.tensor_tensor(prod, prod, posn, ALU.add))
            chain(dve.scalar_tensor_tensor(posn, over_t(ex32), 128.0, prod, ALU.mult, ALU.add))
            tok0 = CN["tok"][0]
            for k, (M, w) in enumerate(((M1, w1), (M2, w2_))):
                chain(dve.tensor_tensor(prod, M, posn, ALU.mult))
                chain(dve.tensor_reduce(dst_f[:, k, :].rearrange("p (t o) -> p t o", o=1), prod, AX.X, ALU.add))
                chain(dve.tensor_copy(rows[:, k, :, 0], c_sb[:, tok0:tok0 + TT]))
                chain(dve.tensor_copy(rows[:, k, :, 1], c_sb[:, tok0 + (1 + k) * TT:tok0 + (2 + k) * TT]))
                chain(dve.tensor_copy(rows[:, k, :, 2:3].bitcast(F32), w))
                chain(dve.tensor_copy(rows[:, k, :, 3:4].bitcast(F32), w))
            chain(dve.tensor_copy(dest.rearrange("p k t -> p (k t)"), dst_f.rearrange("p k t -> p (k t)")))
            dve.sem_inc(sem("routed"), 1)
            m_iota = const("iota")[:, 0:N_MORE].rearrange("p (m o) -> p m o", o=1).to_broadcast([P, N_MORE, N_EXP])
            m_ends = ends.rearrange("p (o e) -> p o e", o=1).to_broadcast([P, N_MORE, N_EXP])
            chain(dve.tensor_tensor(more_t, m_ends, m_iota, ALU.is_le))
            chain(dve.tensor_reduce(more_f[:, 0:N_MORE].rearrange("p (m o) -> p m o", o=1), more_t, AX.X, ALU.add))
            chain(dve.tensor_scalar(more_f[:, 0:N_MORE], more_f[:, 0:N_MORE], float(N_EXP - 1), None, ALU.min))
            chain(dve.tensor_copy(more_f[:, 7:8], ends[:, N_EXP - 1:N_EXP]))
            chain(dve.tensor_copy(meta, more_f))
            dve.sem_inc(sem("routed"), 1)
            dve.wait_ge(sem("h_stored"), 16 * TT)

            def turned(j):
                take(dve, for_dve[1])
                chain(dve.tensor_copy(XT[j][:, 4:8, :].rearrange("p k n -> p (k n)"), bank[1][:, :]))
                dve.sem_inc(bank_free[1], 1)
                dve.sem_inc(sem(f"xt_full{j}"), 1)
                dve.sem_inc(sem(f"x_free{j}"), 1)
            def hidden(j, ring_at):
                take(dve, sem(f"sg_full{j}"))
                take(dve, for_dve[3])
                chain(dve.scalar_tensor_tensor(hid[:, j, :], bank[3][:, :], cur[j][:, 2:3].bitcast(F32), sg[:, j, :],
                                               ALU.mult, ALU.mult))
                dve.sem_inc(bank_free[3], 1)
                dve.sem_inc(slot_free[ring_at + 1], 1)
                dve.sem_inc(sem(f"sg_free{j}"), 1)
                dve.sem_inc(sem(f"hid_full{j}"), 1)
            turned(0)
            chain.reset()
            with dve.Fori(0, N_EXP // 2 - 1) as pair:
                for j in range(2):
                    hidden(j, 3 * j)
                    turned(1 - j)
                chain.reset()
            hidden(0, 0)
            turned(1)
            hidden(1, 3)
            chain.reset()
            n_more = dve.value_load(meta[0:1, 7:8], min_val=0, max_val=N_MORE)
            with dve.Fori(0, N_MORE) as m:
                with dve.If(m < n_more):
                    turned(0)
                    hidden(0, 0)
                    chain.reset()
            for t in range(TT):
                if t == 0:
                    dve.wait_ge(sem("y_loaded"), 16 * TT)
                chain(dve.tensor_tensor(y_tok[:, t, 0, :], y_tok[:, t, 0, :], y_tok[:, t, 1, :], ALU.add))
                dve.sem_inc(sem("y_summed"), 1)
            for m in range(8):
                take(dve, for_dve[m % 4])
                chain(dve.scalar_tensor_tensor(xT[:, m, :], bank[m % 4][:, :], mod[:, 40 + m:41 + m], xT[:, m, :],
                                               ALU.mult, ALU.add))
                dve.sem_inc(bank_free[m % 4], 1)
                dve.sem_inc(sem("x_moe"), 1)
            dve.wait_ge(sem("rs_ready"), 7)
            for k in range(KD):
                chain(dve.scalar_tensor_tensor(xT[:, k, :], xT[:, k, :], par("final_g", k), rs[:], ALU.mult, ALU.mult))
            dve_second(dve, chain)


def constants():
    c = np.zeros((P, N_CN), np.float32)
    def put(name, a):
        c[:a.shape[0], CN[name][0]:CN[name][0] + a.shape[1]] = a
    put("ident", np.eye(P, dtype=np.float32))
    put("ones", np.ones((P, P), np.float32))
    b = np.zeros((P, P), np.float32); b[:64, :64] = 1; b[64:, 64:] = 1
    put("blk", b)
    rot = HD // 4
    half = rot // 2
    inv = np.float32(500000.0) ** (-np.arange(0, rot, 2, dtype=np.float32) / np.float32(rot))
    ang = np.arange(T, dtype=np.float32)[:, None] * inv[None]
    cos, sin = np.ones((P, T), np.float32), np.zeros((P, T), np.float32)
    R = np.zeros((P, P), np.float32)
    for o in (0, 64):
        cos[o:o + half] = np.cos(ang).T; cos[o + half:o + rot] = np.cos(ang).T
        sin[o:o + half] = np.sin(ang).T; sin[o + half:o + rot] = np.sin(ang).T
        for i in range(half):
            R[o + half + i, o + i] = -1.0
            R[o + i, o + half + i] = 1.0
    put("cosA", cos); put("sinA", sin); put("rotA", R)
    put("iota", np.tile(np.arange(32, dtype=np.float32), (P, 1)))
    put("lt", (np.arange(P)[:, None] < np.arange(P)[None]).astype(np.float32))
    tok = np.arange(P)[:, None] + P * np.arange(TT)[None]
    put("tok", np.concatenate([tok, 2 * tok, 2 * tok + 1], axis=1).astype(np.float32))
    s = np.zeros((P, 8), np.float32); s[:, 0] = EPS
    put("scal", s)
    pos = np.arange(T)
    ic = np.stack([1.0 / (np.clip(pos + w - 1 - w // 2 + 1, 0, T) - np.clip(pos - w // 2, 0, T)) for w in POOL_W])
    return c, ic.astype(np.float32)


def constants2():
    c = np.zeros((P, N_C2), np.float32)
    def put(name, a):
        c[:a.shape[0], C2[name][0]:C2[name][0] + a.shape[1]] = a
    p, f = np.arange(P)[:, None], np.arange(P)[None]
    for name, m in (("LE", p <= f), ("LT", p < f), ("GE", p >= f), ("GT", p > f)):
        put(name, m.astype(np.float32))
        put("n" + name, np.where(m, 0.0, -30000.0).astype(np.float32))
    lev = []
    for l in range(LEVELS):
        s = 1 << l
        lev.append((p // (2 * s) == f // (2 * s)) & ((p // s) % 2 == 1) & ((f // s) % 2 == 0))
    put("lev0", np.concatenate([m.astype(np.float32) for m in lev], axis=1))
    put("lev1", np.concatenate([m.T.astype(np.float32) for m in lev], axis=1))
    put("reset", np.tile((np.arange(T) % CHUNK != 0).astype(np.float32), (P, 1)))
    half = ROPE // 2
    R = np.zeros((QK_M, QK_M), np.float32)
    for i in range(half):
        R[NOPE + half + i, NOPE + i] = -1.0
        R[NOPE + i, NOPE + half + i] = 1.0
    put("rotM", R)
    inv = np.float32(10000.0) ** (-np.arange(half, dtype=np.float32) / np.float32(half))
    put("invf", np.concatenate([np.zeros(NOPE, np.float32), inv, inv])[:, None])
    put("ln8", np.full((P, 1), np.log(GD ** -0.5), np.float32))
    put("eps_ln", np.full((P, 1), 64e-5, np.float32))
    return c


def second_inputs(a, put):
    def col(v, n):
        v = np.asarray(v).reshape(-1)
        if v.size < n * P:
            v = np.concatenate([v, np.zeros(n * P - v.size, v.dtype)])
        return v.reshape(n, P).T
    par, row = [], []
    for l in range(LAYERS):
        g = lambda n: np.asarray(a[n + "_2"])[l]
        conv = g("gdn_conv").reshape(5, 9, P).transpose(2, 1, 0).reshape(P, 45)
        par.append(np.concatenate([
            col(g("norm_g"), 8), conv, col(np.tile(g("gdn_norm_g"), 2), 1), col(g("mla_q_norm_g"), 2),
            col(g("mla_kv_norm_g"), 1), col(g("rwkv_mu")[0], 7), col(g("rwkv_mu")[1], 7), col(g("rwkv_k_k"), 2),
            col(g("rwkv_k_a"), 2), col(g("rwkv_r_k"), 2), col(g("rwkv_ln_g"), 2), col(g("rwkv_ln_b"), 2),
            col(g("rwkv_w0"), 4), col(g("rwkv_a0"), 4)], axis=1))
        row.append(np.concatenate([g("gdn_a_log").reshape(-1), g("gdn_dt_bias").reshape(-1)]))
    w = {n: put(n + "_2", a[n + "_2"]) for n in ("w_in", "w_out", "mla_w_uq", "mla_w_ukv", "rwkv_w2", "rwkv_a2", "positions")}
    w["par"] = put("par2", np.stack(par))
    w["row"] = put("row2", np.stack(row))
    w["cn"] = put("cn2", constants2())
    return w


def kernel(x, c, w_ada, b_ada, norm1_g, w_in, lambda_q1, lambda_k1, lambda_q2, lambda_k2, subln_g, w_pool,
           pool_scale, w_out, norm2_g, w_router_group, b_router_group, w_router_expert, b_router_expert,
           w_gate, w_up, w_down, final_g, final_norm_g_2, **rest):
    import concourse.bacc as bacc
    from concourse.bass_utils import run_bass_kernel_spmd
    nc = bacc.Bacc("TRN2", target_bir_lowering=False, num_devices=1)
    arrays = {}
    def put(name, a):
        a = np.ascontiguousarray(a)
        arrays[name] = a
        return nc.dram_tensor(name, a.shape, mybir.dt.from_np(a.dtype), kind="ExternalInput").ap()
    def col(a):
        return np.asarray(a).reshape(-1, P).T
    par1 = np.concatenate([col(norm1_g), col(b_ada), col(norm2_g), col(final_g), col(pool_scale), col(subln_g), col(c),
                           col(final_norm_g_2)], axis=1)
    row1 = np.concatenate([np.asarray(a).reshape(1, -1) for a in (lambda_q1, lambda_k1, lambda_q2, lambda_k2,
                           b_router_group, b_router_expert)], axis=1)
    cn, ic = constants()
    out = nc.dram_tensor("out", (D, T), F32, kind="ExternalOutput").ap()
    debug = {n: nc.dram_tensor(n, (D, T), F32, kind="ExternalOutput").ap() for n in DEBUG}
    build(nc, put("xT_in", np.asarray(x)[0].T), put("par1", par1), put("row1", row1), put("cn", cn), put("invcnt", ic),
          put("w_ada", w_ada), put("w_in", w_in), put("w_pool", w_pool), put("w_out", w_out), put("w_rg", w_router_group),
          put("w_re", w_router_expert), put("w_gate", w_gate), put("w_up", w_up), put("w_down", w_down), second_inputs(rest, put), out, debug)
    r = run_bass_kernel_spmd(nc, [arrays], core_ids=[0])
    return np.ascontiguousarray(np.asarray(r.results[0]["out"]).T)[None]
```

```python
from contextlib import ExitStack

import numpy as np
import concourse.bass as bass
from concourse import mybir

F32 = mybir.dt.float32
I32 = mybir.dt.int32
U32 = mybir.dt.uint32
ALU = mybir.AluOpType
ACT = mybir.ActivationFunctionType
AX = mybir.AxisListType

P = 128
T = 512
D = 1024
KD = D // P
TT = T // P
UNIT = 4096
SLOTS = 6
EPS = 1e-6
HEADS, HD = 4, 64
N_EXP, FE = 32, 512
CAP = 64
HALF = D // 2
N_MORE = 2 * T // CAP - 1
MORE = N_MORE + 1
N_BLK = N_EXP + N_MORE
NO_SLOT = 1 << 20
POOL_W = (2, 4, 8, 16)
POOL_PAD = 8

P1 = {}
def _cols(table, spec):
    at = 0
    for name, n in spec:
        table[name] = (at, at + n)
        at += n
    return at
N_P1 = _cols(P1, [("norm1_g", 8), ("b_ada", 48), ("norm2_g", 8), ("final_g", 8), ("pool_scale", 4),
                  ("subln_g", 1), ("c", 8), ("final2_g", 8)])
R1 = {}
N_R1 = _cols(R1, [("lambda", 256), ("b_router", 36)])

CN = {}
N_CN = _cols(CN, [("ident", 128), ("ones", 128), ("blk", 128), ("rotA", 128), ("cosA", 512), ("sinA", 512),
                  ("iota", 32), ("scal", 8), ("lt", 128), ("tok", 24)])


LAYERS = 2
GH, MH, RH, GD = 6, 6, 4, 64
NOPE, ROPE = 64, 32
QK_M = NOPE + ROPE
CHUNK = P
LEVELS = 7
N_IN2 = 3448
C_DECAY = float(np.exp(-0.5))
UNITS2 = [(1024, 384), (1408, 384), (1792, 408), (2552, 512), (3064, 384), (2200, 352), (0, 512), (512, 512)]
P2 = {}
N_P2 = _cols(P2, [("norm_g", 8), ("conv", 45), ("gdn_g", 1), ("qn_g", 2), ("kvn_g", 1), ("mu0", 7), ("mu1", 7),
                  ("k_k", 2), ("k_a", 2), ("r_k", 2), ("ln_g", 2), ("ln_b", 2), ("w0", 4), ("a0", 4)])
C2 = {}
N_C2 = _cols(C2, [("LE", 128), ("LT", 128), ("GE", 128), ("GT", 128), ("nLE", 128), ("nLT", 128), ("nGE", 128),
                  ("nGT", 128), ("lev0", LEVELS * 128), ("lev1", LEVELS * 128), ("reset", 512), ("rotM", 96),
                  ("invf", 1), ("ln8", 1), ("eps_ln", 1)])


def take(eng, sem, value=1):
    eng.wait_ge(sem, value)
    eng.sem_clear(sem)


class Chain:

    def __init__(self, eng, sem):
        self.eng, self.sem, self.n = eng, sem, 0

    def __call__(self, ins):
        self.n += 1
        ins.then_inc(self.sem, 1)
        self.eng.wait_ge(self.sem, self.n)

    def mark(self, ins):
        self.n += 1
        ins.then_inc(self.sem, 1)

    def wait(self):
        self.eng.wait_ge(self.sem, self.n)

    def reset(self):
        if self.n:
            self.eng.wait_ge(self.sem, self.n)
            self.eng.sem_clear(self.sem)
        self.n = 0


def build(nc, xT_d, par1, row1, cn, invcnt, w_ada, w_in, w_pool, w_out, w_rg, w_re, w_gate, w_up, w_down,
          w2, out):
    ctx = ExitStack()
    with ctx:
        def sb(name, shape, dt=F32):
            return ctx.enter_context(nc.sbuf_tensor(name, shape, dt))

        sems = {}
        def sem(name):
            if name not in sems:
                sems[name] = ctx.enter_context(nc.semaphore(name))
            return sems[name]

        for late, early in (("xy_full0", "hid_full0"), ("xy_full1", "hid_full1"), ("v_full0", "hidT_full0"),
                            ("v_full1", "hidT_full1"), ("pad_free0", "wgt_free0"), ("pad_free1", "wgt_free1"),
                            ("pad_full0", "xt_full0"), ("pad_full1", "xt_full1"), ("R_full0", "y_full0"),
                            ("R_full1", "y_full1"), ("maxima_ready", "max_full00"), ("exps_ready", "probs_full0"),
                            ("probs_ready", "wgt_full0"), ("turned_ready", "wT_full0"), ("turned_used", "probs_full1"),
                            ("d_args0", "max_full01"), ("d_args1", "max_full11"), ("d_full0", "slot_full2"),
                            ("d_full1", "slot_full3"), ("cb_full0", "slot_full4"), ("cb_full1", "slot_full5")):
            sems[late] = sem(early)

        h_d = nc.dram_tensor("h_scratch", (T, D), F32).ap()
        y_d = nc.dram_tensor("y_scratch", (2 * T, D), F32).ap()
        slot_d = nc.dram_tensor("slot_scratch", (N_BLK * CAP, 8), I32).ap()

        xT = sb("xT", [P, KD, T])
        hT = sb("hT", [P, KD, T])
        ARENA = 39300
        arena = sb("arena", [P, ARENA])
        ring = arena[:, 0:SLOTS * UNIT].rearrange("p (s n) -> p s n", s=SLOTS)
        c_sb = sb("c_sb", [P, N_CN])
        p1 = sb("p1", [P, N_P1])
        r1 = sb("r1", [P, N_R1])
        mod = sb("mod", [P, 48])
        small = sb("small", [P, 512])
        work = arena[:, SLOTS * UNIT:SLOTS * UNIT + 13000]
        bank = [ctx.enter_context(nc.psum_tensor(f"bank{i}", [P, 512], F32)) for i in range(8)]
        for_act = [sem(f"for_act{i}") for i in range(8)]
        for_dve = [sem(f"for_dve{i}") for i in range(8)]
        bank_free = [sem(f"bank_free{i}") for i in range(8)]
        slot_full = [sem(f"slot_full{i}") for i in range(SLOTS)]
        slot_free = [sem(f"slot_free{i}") for i in range(SLOTS)]

        def const(name, rows=P):
            a, b = CN[name]
            return c_sb[0:rows, a:b]
        def par(name, i=0, n=1):
            a = P1[name][0] + i
            return p1[:, a:a + n]
        ident, ones, blk = const("ident"), const("ones"), const("blk")
        quarters = c_sb[:, CN["scal"][0] + 1:CN["scal"][0] + 2]
        eps_col = c_sb[:, CN["scal"][0]:CN["scal"][0] + 1]

        class Area:
            def __init__(self, at=0, base=work, end=13000):
                self.at, self.base, self.end = at, base, end
            def __call__(self, *shape):
                n = int(np.prod(shape))
                ap = self.base[:, self.at:self.at + n]
                self.at += n
                assert self.at <= self.end, self.at
                if len(shape) == 2:
                    ap = ap.rearrange("p (a b) -> p a b", a=shape[0])
                if len(shape) == 3:
                    ap = ap.rearrange("p (a b c) -> p a b c", a=shape[0], b=shape[1])
                if len(shape) == 4:
                    ap = ap.rearrange("p (a b c d) -> p a b c d", a=shape[0], b=shape[1], c=shape[2])
                return ap

        ar = Area()
        qkT = ar(8, T)
        v_tok = ar(TT, 512)
        u_pad = ar(4, T + 2 * POOL_PAD)
        att0 = ar.at
        raw = ar(2, T)
        rtmp = ar(2, T)
        ar.at = att0
        probs = ar(2, 2, T)
        wgt = ar(2, T)
        wTq = ar(2, T)
        mod_rows = wTq
        inv_c = work[:, 0:4 * T].rearrange("p (a b) -> p a b", a=4)
        pool_a = work[:, 4 * T:4 * T + 2 * (T + 16)].rearrange("p (a b) -> p a b", a=2)
        sq = sb("sq", [P, 2, T])
        rs = sb("rs", [P, T])
        gs = sb("gs", [P, 2, 8])
        mixT = hT
        pool_w = sb("pool_w", [P, 4, P])
        w_router = sb("w_router", [P, KD, 36])
        stat = small[:, 32:48].rearrange("p (a b) -> p a b", a=2)
        subln = small[:, 24:25]
        rw = Area(att0)
        lg, ohg, m_g = rw(TT, 36), rw(TT, 4), rw(TT, 1)
        rt_t, rt_i, rt_big = rw(TT, 8), rw(TT, 1), rw(4, 8)
        e_in, e_in2, oh1, oh2, m_1, m_2 = rw(TT, 8), rw(TT, 8), rw(TT, 8), rw(TT, 8), rw(TT, 1), rw(TT, 1)
        rt_arg, rt_exp = rw(TT * 5), rw(TT * 5)
        rt_s = rw(3, TT, 1)

        am = Area()
        h_tok = am(4, D)
        am.at = 0
        X = [am(HALF) for _ in range(2)]
        XT = [am(4, 2, CAP) for _ in range(2)]
        sg = am(2, FE // 2)
        hid = am(2, FE // 2)
        hidT = am(2, 2, 2, CAP)
        Yb = [am(HALF) for _ in range(2)]
        assert am.at <= 11000
        am.at = 11000
        info = am(N_BLK, 4).bitcast(I32)
        cur = [am(4).bitcast(I32) for _ in range(2)]
        cur_y = [am(4).bitcast(I32) for _ in range(2)]
        cur_w = am(4).bitcast(I32)
        rows = am(2, TT, 8).bitcast(I32)
        dest = am(2, TT).bitcast(U32)
        meta = am(MORE).bitcast(I32)
        M1, M2, Ms = am(TT, N_EXP), am(TT, N_EXP), am(TT, N_EXP)
        posn, prod = am(TT, N_EXP), am(TT, N_EXP)
        cnt, nblk, ends, base = am(N_EXP), am(N_EXP), am(N_EXP), am(N_EXP)
        dst_f, more_f = am(2, TT), am(MORE)
        more_t = am(N_MORE, N_EXP)
        y_tok = arena[:, 0:2 * TT * D].rearrange("p (t k d) -> p t k d", t=TT, k=2)

        def ada_unit(n):
            return w_ada[0, :, n * 512:(n + 1) * 512].rearrange("(k p) n -> p k n", p=P)
        def in_unit(n):
            return w_in[0, :, n * 512:(n + 1) * 512].rearrange("(k p) n -> p k n", p=P)
        def out_unit(n):
            return w_out[0, :, n * 512:(n + 1) * 512].rearrange("(k p) n -> p k n", p=P)
        units = [ada_unit(n) for n in range(4)]
        ada_at, in_at = list(range(4)), []
        for n in range(4):
            in_at.append(len(units))
            ada_at += [len(units) + 1, len(units) + 2]
            units += [in_unit(n), ada_unit(4 + 2 * n), ada_unit(5 + 2 * n)]
        units += [out_unit(n) for n in range(2)]
        out_at = len(units) - 2
        N1 = len(units)
        assert N1 % SLOTS == 0

        def slot(n, k=8):
            return ring[:, n % SLOTS, :].rearrange("p (k n) -> p k n", k=k)

        w_in2, w_out2 = w2["w_in"], w2["w_out"]
        a2 = Area(2 * UNIT, arena, ARENA)
        mix = a2(KD, T)
        c2 = a2(N_C2)
        a2.at += N_C2 % 2
        cosM, sinM = a2(T), a2(T)
        p2, row2 = a2(N_P2), a2(24)
        a2.at += a2.at % 2
        W0 = a2.at

        def const2(name, rows=P):
            a, b = C2[name]
            return c2[0:rows, a:b]
        def par2(name, i=0, n=1):
            a = P2[name][0] + i
            return p2[:, a:a + n]
        def level(d, l):
            a = C2[f"lev{d}"][0] + l * P
            return over_tiles(c2[:, a:a + P])
        def over_tiles(m):
            return m.rearrange("p (a b) -> p a b", a=1).to_broadcast([P, TT, P])
        def tiles4(ap):
            return ap.rearrange("p (t n) -> p t n", t=TT)
        def along(col):
            return col.rearrange("p (t o) -> p t o", o=1).to_broadcast([P, TT, P])
        def slot2(n):
            w = UNITS2[n][1] if n < 8 else 512
            return arena[:, (n % 2) * UNIT:(n % 2) * UNIT + KD * w].rearrange("p (k n) -> p k n", k=KD)

        ga = Area(W0, arena, ARENA)
        g_qk = ga(6, T)
        g_ktok, g_vtok = ga(TT, 384), ga(TT, 384)
        g_PT = ga(GH, T)
        g_v = g_PT[:, 0:3, :]
        g_WT, g_qg = ga(3, T), ga(3, T)
        g_u0 = ga(TT, GH, GD)
        g_kd = ga(TT, GH, GD)
        g_TA = ga(10, T)
        g_y, g_neg, g_ln, g_g, g_beta, g_cum, g_tc, g_gam, g_dec, g_bg, g_ge = [ga(TT, 12) for _ in range(11)]
        g_ea = ga(12)
        g_ge2 = ga(2, 3, TT)
        g_S = ga(2, 3, GD)
        g_U = ga(GH, GD)
        pads = [g_TA[:, 2 * i:2 * i + 2, :].rearrange("p a b -> p (a b)")[:, 0:T + 4] for i in range(2)]
        R_v = [sq[:, s, 0:256].rearrange("p (t n) -> p t n", t=TT) for s in range(2)]
        R_k = [sq[:, s, 256:512].rearrange("p (t n) -> p t n", t=TT) for s in range(2)]

        ra = Area(W0, arena, ARENA)
        r_f = ra(6, T)
        r_wa = ra(1, T)
        r_kk, r_bon = ra(2, T), ra(2, T)
        r_kt, r_bt, r_kmt, r_rt = ra(2, T), ra(2, T), ra(2, T), ra(2, T)
        r_vtok = ra(TT, 256)
        r_PbT = ra(RH, T)
        r_PkT = ra(2, T)
        r_WT = ra(2, T)
        r_u0 = ra(TT, RH, GD)
        r_TA = ra(10, T)
        r_w = ra(2, 256)
        r_S = ra(2, 2, GD)
        r_U = ra(RH, GD)
        r_m, r_d, r_pm, r_pd, r_sc = ra(2, TT), ra(2, TT), ra(2, TT), ra(2, TT), ra(2, TT)
        r_c0, r_oka = ra(7), ra(2)
        r_ktok = mix[:, 3:5, :].rearrange("p a (b n) -> p (a b) n", n=256)
        r_nBV = mix[:, 5, :].rearrange("p (s t n) -> p s t n", s=2, t=TT)
        r_BT = [sq[:, s, :] for s in range(2)]
        r_btok = r_TA[:, 0:2, :].rearrange("p a (b n) -> p (a b) n", n=256)
        r_kmtok = r_TA[:, 2:4, :].rearrange("p a (b n) -> p (a b) n", n=256)
        r_pads = [r_TA[:, 2 * i:2 * i + 2, :].rearrange("p a b -> p (a b)")[:, 0:T + 2] for i in range(2)]

        la = Area(W0, arena, ARENA)
        m_cq, m_ckv, m_kr, m_tmp = la(2, T), la(1, T), la(1, T), la(2, T)
        m_q, m_k = la(MH, T), la(MH, T)
        m_vtok = la(TT, 384)
        m_pr = la(4, T)
        m_wT = la(2, 2, T)
        m_st = la(4, 4)
        m_wuq, m_wukv = la(2, 576), la(768)
        m_gate = la(2, T)

        def sp_second(sp):
            take(sp, sem("go_sp"))
            with sp.Fori(0, LAYERS) as l:
                def unit(n):
                    take(sp, slot_free[n % 2])
                    src, c, w = (w_in2, *UNITS2[n]) if n < 8 else (w_out2, 512 * (n - 8), 512)
                    src = src[bass.ds(l, 1), :, c:c + w].rearrange("a (k p) n -> p (a k) n", p=P)
                    sp.dma_start(slot2(n), src).then_inc(slot_full[n % 2], 16)
                take(sp, sem("par_free"))
                sp.dma_start(p2, w2["par"][bass.ds(l, 1)].rearrange("a p n -> p (a n)")).then_inc(sem("par_full"), 16)
                sp.dma_start(row2, w2["row"][bass.ds(l, 1), :].to_broadcast([P, 24])).then_inc(sem("par_full"), 16)
                for n in range(5):
                    unit(n)
                take(sp, sem("go_sp"))
                for lo, name in ((0, "rwkv_w2"), (64, "rwkv_a2")):
                    sp.dma_start(r_w[lo:lo + 64], w2[name][bass.ds(l, 1)].rearrange("a e k n -> k (a e) n"))\
                      .then_inc(sem("small_w_full"), 16)
                unit(5)
                take(sp, sem("go_sp"))
                uq = w2["mla_w_uq"][bass.ds(l, 1)]
                sp.dma_start(m_wuq[:, 0, :], uq[:, 0:P, :].rearrange("a k n -> k (a n)")).then_inc(sem("small_w_full"), 16)
                sp.dma_start(m_wuq[0:64, 1, :], uq[:, P:192, :].rearrange("a k n -> k (a n)")).then_inc(sem("small_w_full"), 16)
                sp.dma_start(m_wukv, w2["mla_w_ukv"][bass.ds(l, 1)].rearrange("a k n -> k (a n)")).then_inc(sem("small_w_full"), 16)
                for n in range(6, 10):
                    unit(n)
            sp.wait_ge(sem("done"), 1)
            sp.dma_start(out.rearrange("(k p) t -> p k t", p=P), hT[:]).then_inc(sem("out_stored"), 16)
            sp.wait_ge(sem("out_stored"), 16)

        def pe_second(pe, sumsq):
            def column(b, n, c, w, rows=None):
                lo = 0 if rows is None else rows
                for k in range(KD):
                    m = pe.matmul(bank[b][lo:lo + w, :], slot2(n)[:, k, c:c + w], hT[:, k, :], start=(k == 0), stop=(k == KD - 1))
                return m
            def grid(b, lhs, rhs, reader=for_dve):
                for t in range(TT):
                    m = pe.matmul(bank[b][:, t * P:(t + 1) * P], lhs(t), rhs(t), start=True, stop=True)
                m.then_inc(reader[b], 1)
            def ts(t):
                return slice(t * P, (t + 1) * P)
            def to_tokens(b, src):
                take(pe, bank_free[b])
                for t in range(TT):
                    m = pe.transpose(bank[b][:, ts(t)], src[:, ts(t)], ident)
                m.then_inc(for_act[b], 1)
            def invert(TA):
                Tm, Y, X, V = [[TA[:, 2 * i + s, :] for s in range(2)] for i in (1, 2, 3, 4)]
                for s in range(2):
                    take(pe, sem(f"xy_full{s}"))
                    take(pe, bank_free[s])
                    grid(s, lambda t: X[s][:, ts(t)], lambda t: ident)
                for l in range(1, LEVELS):
                    for s in range(2):
                        take(pe, sem(f"xy_full{s}"))
                        take(pe, bank_free[s])
                        grid(s, lambda t: X[s][:, ts(t)], lambda t: Y[s][:, ts(t)], for_act)
                    for s in range(2):
                        take(pe, sem(f"v_full{s}"))
                        take(pe, bank_free[2 + s])
                        take(pe, sem(f"t_full{s}"))
                        grid(2 + s, lambda t: Tm[s][:, ts(t)], lambda t: V[s][:, ts(t)])
                        if l < LEVELS - 1:
                            take(pe, bank_free[4 + s])
                            grid(4 + s, lambda t: V[s][:, ts(t)], lambda t: Tm[s][:, ts(t)])
                for s in range(2):
                    take(pe, sem(f"xy_full{s}"))
            def norm_over_heads(i=0):
                j = i % 2
                take(pe, bank_free[6 + j])
                take(pe, sem(f"sq_full{j}"))
                pe.matmul(bank[6 + j][:, :], blk, sq[:, j, :], start=True, stop=True).then_inc(for_act[6 + j], 1)
            def recurrence(d, n_heads, WT, S, q_in, U, PT, pairs):
                for n in range(TT):
                    t = n if d == 0 else TT - 1 - n
                    if n > 0:
                        take(pe, sem("state_full"))
                        for s, b in ((0, 0), (1, 2)):
                            take(pe, bank_free[b])
                            for i in range(n_heads // 2):
                                m = pe.matmul(bank[b][:, i * 64:(i + 1) * 64], WT[64 * s:64 * s + 64, i, ts(t)],
                                              S[64 * s:64 * s + 64, n % 2, i, :], start=True, stop=True)
                            m.then_inc(for_dve[b], 1)
                    take(pe, sem("u_full"))
                    if n < TT - 1:
                        take(pe, bank_free[3])
                        for h in range(n_heads):
                            lo = 64 * (h % 2)
                            prods = pairs(h, t)
                            for i, (a, b) in enumerate(prods):
                                m = pe.matmul(bank[3][lo:lo + 64, (h // 2) * 64:(h // 2 + 1) * 64], a, b, start=(i == 0),
                                              stop=(i == len(prods) - 1))
                        m.then_inc(for_dve[3], 1)
                    take(pe, bank_free[1])
                    for h in range(n_heads):
                        lo = 64 * (h % 2)
                        o = bank[1][lo:lo + 64, (h // 2) * P:(h // 2 + 1) * P]
                        if n > 0:
                            pe.matmul(o, S[lo:lo + 64, n % 2, h // 2, :], q_in[lo:lo + 64, h // 2, ts(t)], start=True, stop=False)
                        m = pe.matmul(o, U[:, h, :], PT[:, h, ts(t)], start=(n == 0), stop=True)
                    m.then_inc(for_dve[1], 1)

            with pe.Fori(0, LAYERS) as l:
                sumsq(1, KD, 0)
                for i in range(9):
                    n, b = i // 3, i % 2
                    if i % 3 == 0:
                        take(pe, slot_full[n % 2], 16)
                    if i == 0:
                        take(pe, sem("tiles_full"), KD)
                    if i == 6:
                        take(pe, bank_free[2])
                        for t in range(TT):
                            for k in range(KD):
                                m = pe.matmul(bank[2][:, t * 24:(t + 1) * 24], hT[:, k, ts(t)], slot2(2)[:, k, 384:408],
                                              start=(k == 0), stop=(k == KD - 1))
                        m.then_inc(for_dve[2], 1)
                    take(pe, bank_free[b])
                    column(b, n, (i % 3) * P, P).then_inc(for_act[b], 1)
                take(pe, sem("g_full"))
                take(pe, bank_free[2])
                cum = bank[2][:, 0:48].rearrange("p (t c) -> p t c", t=TT)
                pe.matmul(cum[:, :, 0:6], const2("LE"), g_g[:, :, 0:6], start=True, stop=True)
                pe.matmul(cum[:, :, 6:12], const2("GE"), g_g[:, :, 6:12], start=True, stop=True)
                pe.matmul(bank[2][:, 64:112], ones, g_g.rearrange("p t c -> p (t c)"), start=True, stop=True)\
                  .then_inc(for_dve[2], 1)
                for i in range(6):
                    norm_over_heads(i)
                for i in range(3):
                    take(pe, sem("v_ch_full"))
                    to_tokens(4 + i % 2, g_v[:, i, :])
                take(pe, sem("k_ch_full"))
                for i in range(3):
                    to_tokens(4 + i % 2, g_qk[:, 3 + i, :])
                for d in range(2):
                    for ht in range(3):
                        for s in range(2):
                            c = 6 * d + 2 * ht + s
                            lo = 64 * s
                            take(pe, bank_free[s])
                            grid(s, lambda t: g_g[:, t, c:c + 1].to_broadcast([P, P]), lambda t: const2("LE" if d == 0 else "GE"))
                            kh, qh = g_qk[lo:lo + 64, 3 + ht, :], g_qk[lo:lo + 64, ht, :]
                            take(pe, bank_free[2 + s])
                            grid(2 + s, lambda t: kh[:, ts(t)], lambda t: kh[:, ts(t)])
                            take(pe, bank_free[4 + s])
                            grid(4 + s, lambda t: kh[:, ts(t)], lambda t: qh[:, ts(t)])
                        invert(g_TA)
                        take(pe, bank_free[6])
                        take(pe, bank_free[7])
                        for s in range(2):
                            take(pe, sem(f"R_full{s}"))
                            Y = g_TA[:, 4 + s, :]
                            for t in range(TT):
                                m6 = pe.matmul(bank[6][:, s * 256 + t * 64:s * 256 + (t + 1) * 64], Y[:, ts(t)], R_v[s][:, t, :],
                                               start=True, stop=True)
                        m6.then_inc(for_act[6], 1)
                        for t in range(TT):
                            for s in range(2):
                                m7 = pe.matmul(bank[7][64 * s:64 * s + 64, ts(t)], R_k[s][:, t, :], g_TA[:, 4 + s, ts(t)],
                                               start=True, stop=True)
                        m7.then_inc(for_act[7], 1)
                    take(pe, sem("chunks_full"))
                    take(pe, sem("kd_full"))
                    recurrence(d, GH, g_WT, g_S, g_qg, g_U, g_PT, lambda h, t: [(g_kd[:, t, h, :], g_U[:, h, :])])
                for i in range(3):
                    norm_over_heads(i)
                for i in range(7):
                    n, b = 3 + i // 4, i % 2
                    if i % 4 == 0:
                        take(pe, slot_full[n % 2], 16)
                    take(pe, bank_free[b])
                    column(b, n, (i % 4) * P, P).then_inc(for_act[b], 1)
                for i in range(2):
                    norm_over_heads(i)
                for i in range(2):
                    take(pe, sem("v_ch_full"))
                    to_tokens(4 + i, r_f[:, 4 + i, :])
                take(pe, sem("small_w_full"), 32)
                take(pe, sem("wa_full"))
                for e in range(2):
                    for ct in range(2):
                        for b, lo in ((0, 0), (1, 64)):
                            take(pe, bank_free[b])
                            pe.matmul(bank[b][:, :], r_w[lo:lo + 64, e, ts(ct)], r_wa[lo:lo + 64, 0, :], start=True,
                                      stop=True).then_inc(for_act[b], 1)
                        take(pe, sem("kt_full"))
                        to_tokens(2 + ct, r_kt[:, ct, :])
                    for ct in range(2):
                        for first in range(2):
                            for s in range(2):
                                lo = 64 * s
                                kt, bt, kmt, rt = [x[lo:lo + 64, ct, :] for x in (r_kt, r_bt, r_kmt, r_rt)]
                                for b, x, y in (((2 + s, kmt, kt), (6 + s, kmt, rt)) if first == 0 else
                                                ((s, kt, bt), (4 + s, bt, rt))):
                                    take(pe, bank_free[b])
                                    grid(b, lambda t: x[:, ts(t)], lambda t: y[:, ts(t)])
                        take(pe, sem("bp_full"))
                        take(pe, bank_free[6])
                        take(pe, bank_free[7])
                        for s in range(2):
                            h = 2 * ct + s
                            for t in range(TT):
                                pe.matmul(bank[6][:, s * 256 + t * 64:s * 256 + (t + 1) * 64], r_BT[s][:, ts(t)],
                                          r_vtok[:, t, h * 64:(h + 1) * 64], start=True, stop=True)
                        for t in range(TT):
                            for s in range(2):
                                h = 2 * ct + s
                                m7 = pe.matmul(bank[7][64 * s:64 * s + 64, ts(t)], r_vtok[:, t, h * 64:(h + 1) * 64],
                                               r_PkT[:, s, ts(t)], start=True, stop=True)
                        m7.then_inc(for_act[7], 1)
                        invert(r_TA)
                        take(pe, sem("nBV_full"))
                        take(pe, bank_free[6])
                        take(pe, bank_free[7])
                        for s in range(2):
                            Y = r_TA[:, 4 + s, :]
                            for t in range(TT):
                                m6 = pe.matmul(bank[6][:, s * 256 + t * 64:s * 256 + (t + 1) * 64], Y[:, ts(t)],
                                               r_nBV[:, s, t, :], start=True, stop=True)
                        m6.then_inc(for_act[6], 1)
                        for t in range(TT):
                            for s in range(2):
                                h = 2 * ct + s
                                Y = r_TA[:, 4 + s, :]
                                m7 = pe.matmul(bank[7][64 * s:64 * s + 64, ts(t)], r_ktok[:, t, h * 64:(h + 1) * 64],
                                               Y[:, ts(t)], start=True, stop=True)
                        m7.then_inc(for_act[7], 1)
                    for ct in range(2):
                        to_tokens(2 + ct, r_bt[:, ct, :])
                        to_tokens(4 + ct, r_kmt[:, ct, :])
                    take(pe, sem("chunks_full"))
                    recurrence(e, RH, r_WT, r_S, r_rt, r_U, r_PbT, lambda h, t: [
                        (r_btok[:, t, h * 64:(h + 1) * 64], r_U[:, h, :]),
                        (r_kmtok[:, t, h * 64:(h + 1) * 64], r_vtok[:, t, h * 64:(h + 1) * 64])])
                for i in range(2):
                    take(pe, bank_free[5])
                    take(pe, sem("y_full"))
                    pe.matmul(bank[5][:, :], blk, mix[:, 6 + i, :], start=True, stop=True).then_inc(for_dve[5], 1)
                    norm_over_heads()
                    take(pe, bank_free[7])
                    take(pe, sem("bonus_full"))
                    pe.matmul(bank[7][:, :], blk, r_bon[:, i, :], start=True, stop=True).then_inc(for_dve[7], 1)
                take(pe, slot_full[1], 16)
                for b, c, w, rows in ((0, 0, 128, 0), (1, 128, 64, 0), (2, 192, 128, 0), (3, 320, 32, 64)):
                    take(pe, bank_free[b])
                    column(b, 5, c, w, rows).then_inc(for_act[b], 1)
                sumsq(4, 2, 0, rows=[P, 64])
                sumsq(5, 1, 0)
                take(pe, sem("raw_full"))
                take(pe, bank_free[3])
                pe.matmul(bank[3][64:96, :], const2("rotM")[64:96, 64:96], m_kr[64:96, 0, :], start=True, stop=True)\
                  .then_inc(for_dve[3], 1)
                take(pe, sem("small_w_full"), 48)
                take(pe, sem("latent_in_full"), 2)
                for h in range(MH):
                    b = h % 2
                    take(pe, bank_free[b])
                    pe.matmul(bank[b][0:QK_M, :], m_wuq[:, 0, h * QK_M:(h + 1) * QK_M], m_cq[:, 0, :], start=True, stop=False)
                    pe.matmul(bank[b][0:QK_M, :], m_wuq[0:64, 1, h * QK_M:(h + 1) * QK_M], m_cq[0:64, 1, :], start=False,
                              stop=True).then_inc(for_act[b], 1)
                    take(pe, bank_free[4 + b])
                    pe.matmul(bank[4 + b][0:64, :], m_wukv[:, h * P:h * P + 64], m_ckv[:, 0, :], start=True,
                              stop=True).then_inc(for_act[4 + b], 1)
                    take(pe, sem("raw_full"))
                    take(pe, bank_free[2 + b])
                    pe.matmul(bank[2 + b][64:96, :], const2("rotM")[64:96, 64:96], m_q[64:96, h, :], start=True, stop=True)\
                      .then_inc(for_dve[2 + b], 1)
                for t in range(TT):
                    take(pe, bank_free[6 + t % 2])
                    pe.matmul(bank[6 + t % 2][:, 0:384], m_ckv[:, 0, ts(t)],
                              m_wukv.rearrange("p (h x) -> p h x", h=MH)[:, :, 64:128], start=True, stop=True)\
                      .then_inc(for_act[6 + t % 2], 1)
                take(pe, sem("mla_q_full"), MH)
                take(pe, sem("mla_k_full"), MH)
                n = MH * TT
                for i in range(n + 3):
                    if i < n:
                        h, q = 2 * (i // 8) + i % 2, (i % 8) // 2
                        take(pe, bank_free[i % 4])
                        pe.matmul(bank[i % 4][:, :], m_q[0:QK_M, h, ts(q)], m_k[0:QK_M, h, :], start=True,
                                  stop=True).then_inc(for_dve[i % 4], 1)
                    if 2 <= i < n + 2:
                        j = i - 2
                        pe.wait_ge(sem("probs_ready"), j + 1)
                        to_tokens(4 + j % 2, m_pr[:, j % 4, :])
                    if i >= 4 and i % 2 == 0:
                        p = (i - 4) // 2
                        hp, q = p // TT, p % TT
                        pe.wait_ge(sem("turned_ready"), 2 * p + 2)
                        if q == 0:
                            take(pe, bank_free[6 + hp % 2])
                        for kt in range(TT):
                            for e in range(2):
                                m = pe.matmul(bank[6 + hp % 2][64 * e:64 * e + 64, ts(q)],
                                              m_vtok[:, kt, (2 * hp + e) * 64:(2 * hp + e + 1) * 64], m_wT[:, p % 2, e, ts(kt)],
                                              start=(kt == 0), stop=(kt == TT - 1))
                        m.then_inc(for_act[6 + hp % 2] if q == TT - 1 else sem("turned_used"), 1)
                pe.sem_clear(sem("probs_ready"))
                pe.sem_clear(sem("turned_ready"))
                for i in range(8):
                    n, b = 6 + i // 4, i % 2
                    if i % 4 == 0:
                        take(pe, slot_full[n % 2], 16)
                    take(pe, bank_free[b])
                    column(b, n, (i % 4) * P, P).then_inc(for_act[b], 1)
                take(pe, sem("tiles_full"), KD)
                for m_ in range(8):
                    n, b = 8 + m_ // 4, 4 + m_ % 4
                    if m_ % 4 == 0:
                        take(pe, slot_full[n % 2], 16)
                    take(pe, bank_free[b])
                    for k in range(KD):
                        m = pe.matmul(bank[b][:, :], slot2(n)[:, k, (m_ % 4) * P:(m_ % 4 + 1) * P], mix[:, k, :],
                                      start=(k == 0), stop=(k == KD - 1))
                    m.then_inc(for_dve[b], 1)
            sumsq(1, KD, 0)

        def act_second(act, chain):
            def move(b, dst, src, func=ACT.Copy, **kw):
                take(act, for_act[b])
                chain(act.activation(dst, src, func, **kw))
                act.sem_inc(bank_free[b], 1)
            def meet():
                act.sem_inc(sem("act_here"), 1)
                take(act, sem("go_act"))
            def square(src, j, rows=P):
                take(act, sem(f"sq_free{j}"))
                act.activation(sq[0:rows, j, :], src, ACT.Square).then_inc(sem(f"sq_full{j}"), 1)
            def root(b, scale, last=0, eps=eps_col, bias=None):
                take(act, for_act[b])
                take(act, sem("rs_free"))
                chain(act.activation(rs[:], bank[b][:, :], ACT.Ln, bias=eps, scale=scale))
                act.sem_inc(bank_free[b], 1)
                act.sem_inc(sem(f"sq_free{last}"), 1)
                kw = {} if bias is None else {"bias": bias}
                act.activation(rs[:], rs[:], ACT.Exp, scale=-0.5, **kw).then_inc(sem("rs_full"), 1)
            def roots(n, src, buf, scale, bias=lambda i: None):
                def logarithm(i):
                    move(6 + i % 2, buf(i), bank[6 + i % 2][:, :], ACT.Ln, bias=eps_col, scale=scale)
                    act.sem_inc(sem(f"sq_free{i % 2}"), 1)
                for i in range(n):
                    square(src(i), i % 2)
                    if i > 0:
                        logarithm(i - 1)
                logarithm(n - 1)
                exponentials(n, buf, bias)
            def exponentials(n, buf, bias=lambda i: None):
                for i in range(n):
                    kw = {} if bias(i) is None else {"bias": bias(i)}
                    act.activation(buf(i), buf(i), ACT.Exp, scale=-0.5, **kw).then_inc(sem("rs_full"), 1)
            def to_tokens(b, dst):
                move(b, dst, tiles4(bank[b][:, :]))
            def invert(TA):
                V = [TA[:, 8 + s, :] for s in range(2)]
                for l in range(1, LEVELS):
                    for s in range(2):
                        move(s, V[s], bank[s][:, :])
                        act.sem_inc(sem(f"v_full{s}"), 1)
            meet()
            chain.reset()
            with act.Fori(0, LAYERS) as l:
                take(act, sem("norm_in_full"))
                for i in range(KD):
                    square(xT[:, i, :], i % 2)
                root(1, 1.0 / D, last=1)
                for i in range(10):
                    if i < 9:
                        take(act, for_act[i % 2])
                        take(act, sem(f"pad_free{i % 2}"))
                        chain(act.activation(pads[i % 2][:, 2:2 + T], bank[i % 2][:, :], ACT.Copy))
                        act.sem_inc(bank_free[i % 2], 1)
                        act.sem_inc(sem(f"pad_full{i % 2}"), 1)
                        if i % 3 == 2:
                            act.sem_inc(slot_free[(i // 3) % 2], 1)
                    if i >= 1:
                        j = i - 1
                        dst = g_qk[:, j, :] if j < 6 else g_v[:, j - 6, :]
                        take(act, sem(f"conv_full{j % 2}"))
                        chain(act.activation(dst, dst, ACT.Silu))
                    if i == 6:
                        take(act, sem("args_full"))
                        chain(act.activation(g_beta, g_beta, ACT.Sigmoid))
                        chain(act.activation(g_ln, g_neg, ACT.Exp))
                        chain(act.activation(g_ea, row2[:, 0:12], ACT.Exp))
                        act.activation(g_ln, g_ln, ACT.Ln, bias=ones[:, 0:1]).then_inc(sem("func_full"), 1)
                take(act, sem("args_full"))
                chain(act.activation(g_gam, g_cum, ACT.Exp))
                chain(act.activation(g_dec, g_dec, ACT.Exp))
                act.activation(g_ge, g_ge, ACT.Exp).then_inc(sem("func_full"), 1)
                roots(6, lambda i: g_qk[:, i, :], lambda i: g_TA[:, i, :], 1.0, lambda i: const2("ln8") if i < 3 else None)
                act.sem_inc(sem("v_ch_full"), 1)
                for i in range(3):
                    to_tokens(4 + i % 2, g_vtok[:, :, i * P:(i + 1) * P])
                    if i < 2:
                        act.sem_inc(sem("v_ch_full"), 1)
                for i in range(3):
                    to_tokens(4 + i % 2, g_ktok[:, :, i * P:(i + 1) * P])
                act.sem_inc(sem("tok_full"), 1)
                for d in range(2):
                    for ht in range(3):
                        TA = g_TA
                        for s in range(2):
                            lo = 64 * s
                            Y, X, V = TA[:, 4 + s, :], TA[:, 6 + s, :], TA[:, 8 + s, :]
                            take(act, sem(f"cb_full{s}"))
                            chain(act.activation(Y[lo:lo + 64, :], bank[s][lo:lo + 64, :], ACT.Exp))
                            act.sem_inc(bank_free[s], 1)
                            take(act, sem(f"d_args{s}"))
                            chain(act.activation(V, V, ACT.Exp))
                            chain(act.activation(X, X, ACT.Exp, scale=-1.0))
                            act.sem_inc(sem(f"d_full{s}"), 1)
                        invert(TA)
                        take(act, for_act[6])
                        u = bank[6][:, :].rearrange("p (s t n) -> p s t n", s=2, t=TT)
                        for s in range(2):
                            chain(act.activation(g_u0[:, :, 2 * ht + s, :], u[:, s], ACT.Copy))
                        act.sem_inc(bank_free[6], 1)
                        move(7, g_WT[:, ht, :], bank[7][:, :])
                        for s in range(2):
                            act.sem_inc(sem(f"R_free{s}"), 1)
                    act.sem_inc(sem("chunks_act"), 1)
                take(act, sem("norm_in_full"))
                roots(3, lambda i: mix[:, i, :], lambda i: g_TA[:, i, :], 1.0 / 64)
                meet()
                for i in range(7):
                    take(act, for_act[i % 2])
                    take(act, sem(f"pad_free{i % 2}"))
                    chain(act.activation(r_pads[i % 2][:, 1:1 + T], bank[i % 2][:, :], ACT.Copy))
                    act.sem_inc(bank_free[i % 2], 1)
                    act.sem_inc(sem(f"pad_full{i % 2}"), 1)
                    if i in (3, 6):
                        act.sem_inc(slot_free[(3 + i // 4) % 2], 1)
                take(act, sem("norm_in_full"))
                chain(act.activation(r_wa[0:64, 0, :], r_wa[0:64, 0, :], ACT.Tanh))
                act.sem_inc(sem("wa_full"), 1)
                roots(2, lambda i: r_kk[:, i, :], lambda i: r_TA[:, 8 + i, :], 1.0)
                for i in range(2):
                    act.sem_inc(sem("v_ch_full"), 1)
                    to_tokens(4 + i, r_vtok[:, :, i * P:(i + 1) * P])
                for e in range(2):
                    TA = r_TA
                    for ct in range(2):
                        take(act, sem("ta_free"))
                        move(0, TA[:, 0, :], bank[0][:, :], ACT.Sigmoid, bias=par2("w0", 2 * e + ct))
                        move(1, TA[:, 1, :], bank[1][:, :], ACT.Sigmoid, bias=par2("a0", 2 * e + ct))
                        act.sem_inc(sem("sig_full"), 1)
                        take(act, sem("args_full"))
                        A1, A2 = TA[:, 3, :], TA[:, 4, :]
                        for dst, src, sign in (((5, A1, -1), (6, A1, 1), (7, A2, -1)) if e == 0 else
                                               ((5, A2, 1), (6, A2, -1), (7, A1, 1))):
                            chain(act.activation(TA[:, dst, :], src, ACT.Exp, scale=sign * C_DECAY))
                        chain(act.activation(r_pm[:, ct, :], r_m[:, ct, :], ACT.Exp, scale=-C_DECAY))
                        chain(act.activation(r_pd[:, ct, :], r_d[:, ct, :], ACT.Exp, scale=-C_DECAY))
                        act.sem_inc(sem("func_full"), 1)
                        to_tokens(2 + ct, r_ktok[:, :, ct * P:(ct + 1) * P])
                    for ct in range(2):
                        take(act, for_act[7])
                        chain(act.activation(r_nBV.rearrange("p s t n -> p (s t n)"), bank[6][:, :], ACT.Copy, scale=-1.0))
                        act.sem_inc(bank_free[6], 1)
                        act.sem_inc(sem("nBV_full"), 1)
                        act.sem_inc(sem("direct_full"), 1)
                        invert(TA)
                        take(act, for_act[6])
                        u = bank[6][:, :].rearrange("p (s t n) -> p s t n", s=2, t=TT)
                        for s in range(2):
                            chain(act.activation(r_u0[:, :, 2 * ct + s, :], u[:, s], ACT.Copy))
                        act.sem_inc(bank_free[6], 1)
                        move(7, r_WT[:, ct, :], bank[7][:, :])
                    for ct in range(2):
                        to_tokens(2 + ct, r_btok[:, :, ct * P:(ct + 1) * P])
                        to_tokens(4 + ct, r_kmtok[:, :, ct * P:(ct + 1) * P])
                    act.sem_inc(sem("chunks_act"), 1)
                for i in range(2):
                    take(act, sem("norm_in_full"))
                    square(mix[:, 6 + i, :], 0)
                    root(6, 1.0 / 64, eps=const2("eps_ln"))
                meet()
                move(0, m_cq[:, 0, :], bank[0][:, :])
                move(1, m_cq[0:64, 1, :], bank[1][0:64, :])
                move(2, m_ckv[:, 0, :], bank[2][:, :])
                move(3, m_kr[64:96, 0, :], bank[3][64:96, :])
                act.sem_inc(slot_free[1], 1)
                act.sem_inc(sem("raw_full"), 1)
                square(m_cq[:, 0, :], 0)
                square(m_cq[0:64, 1, :], 1, 64)
                move(4, m_tmp[:, 0, :], bank[4][:, :], ACT.Ln, bias=eps_col, scale=1.0 / 192)
                act.sem_inc(sem("sq_free1"), 1)
                square(m_ckv[:, 0, :], 0)
                move(5, m_tmp[:, 1, :], bank[5][:, :], ACT.Ln, bias=eps_col, scale=1.0 / 128)
                act.sem_inc(sem("sq_free0"), 1)
                exponentials(2, lambda i: m_tmp[:, i, :])
                for h in range(MH):
                    b = h % 2
                    move(b, m_q[0:QK_M, h, :], bank[b][0:QK_M, :])
                    act.sem_inc(sem("raw_full"), 1)
                    move(4 + b, m_k[0:64, h, :], bank[4 + b][0:64, :])
                    act.sem_inc(sem("mla_k_full"), 1)
                for t in range(TT):
                    move(6 + t % 2, m_vtok[:, t, :], bank[6 + t % 2][:, 0:384])
                n = MH * TT
                for i in range(n + 4):
                    if i < n:
                        act.wait_ge(sem("maxima_ready"), i + 1)
                        chain(act.activation(m_pr[:, i % 4, :], bank[i % 4][:, :], ACT.Exp, bias=m_st[:, i % 4, 0:1],
                                             scale=QK_M ** -0.5, accum_out=m_st[:, i % 4, 1:2]))
                        act.sem_inc(bank_free[i % 4], 1)
                        act.sem_inc(sem("exps_ready"), 1)
                    if 2 <= i < n + 2:
                        j = i - 2
                        if j >= 4:
                            act.wait_ge(sem("turned_used"), j // 2 - 1)
                        move(4 + j % 2, m_wT[:, (j // 2) % 2, j % 2, :], bank[4 + j % 2][:, :])
                        act.sem_inc(sem("turned_ready"), 1)
                    if i >= 5 and (i - 5) % 2 == 0 and (i - 5) // 2 % TT == TT - 1:
                        hp = (i - 5) // 2 // TT
                        move(6 + hp % 2, mix[:, 3 + hp, :], bank[6 + hp % 2][:, :])
                        act.sem_inc(sem("turned_used"), 1)
                act.sem_clear(sem("maxima_ready"))
                take(act, sem("turned_used"), n // 2)
                for i in range(8):
                    take(act, sem(f"sg_free{i % 2}"))
                    move(i % 2, m_gate[:, i % 2, :], bank[i % 2][:, :], ACT.Silu)
                    act.sem_inc(sem(f"sg_full{i % 2}"), 1)
                    if i % 4 == 3:
                        act.sem_inc(slot_free[(6 + i // 4) % 2], 1)
                chain.reset()
            take(act, sem("norm_in_full"))
            for i in range(KD):
                square(xT[:, i, :], i % 2)
            root(1, 1.0 / D, last=1)

        def pool_second(pool):
            for name in ("par_free", "R_free0", "R_free1", "ta_free"):
                pool.sem_inc(sem(name), 1)
            chain = Chain(pool, sem("pool_chain"))
            def meet():
                pool.sem_inc(sem("pool_here"), 1)
                take(pool, sem("go_pool"))
            meet()
            with pool.Fori(0, LAYERS) as l:
                take(pool, sem("tok_full"), 2)
                for d in range(2):
                    if d == 1:
                        take(pool, sem("dir_done"))
                    for h in range(GH):
                        s = h % 2
                        c = 6 * d + h
                        def scaled(dst, src, col):
                            chain(pool.tensor_tensor(dst, src[:, :, h * 64:(h + 1) * 64],
                                                     col[:, :, c:c + 1].to_broadcast([P, TT, 64]), ALU.mult))
                        take(pool, sem(f"R_free{s}"))
                        scaled(R_v[s], g_vtok, g_beta)
                        scaled(R_k[s], g_ktok, g_bg)
                        pool.sem_inc(sem(f"R_full{s}"), 1)
                        scaled(g_kd[:, :, h, :], g_ktok, g_dec)
                    pool.sem_inc(sem("kd_full"), 1)
                meet()
                meet()
                take(pool, sem("kr_full"))
                for h in range(MH):
                    chain(pool.tensor_copy(m_k[64:96, h, :], m_kr[64:96, 0, :]))
                pool.sem_inc(sem("k_rot_full"), 1)
                chain.reset()

        def dve_second(dve, chain):
            def meet(sp=True):
                chain.wait()
                take(dve, sem("act_here"))
                take(dve, sem("pool_here"))
                for name in ("go_act", "go_pool") + (("go_sp",) if sp else ()):
                    dve.sem_inc(sem(name), 1)
            def times_rs(dst, src, col=None):
                take(dve, sem("rs_full"))
                if col is None:
                    chain(dve.tensor_tensor(dst, src, rs[:], ALU.mult))
                else:
                    chain(dve.scalar_tensor_tensor(dst, src, col, rs[:], ALU.mult, ALU.mult))
                dve.sem_inc(sem("rs_free"), 1)
            def times_roots(n, x, buf, col=None):
                for i in range(n):
                    dve.wait_ge(sem("rs_full"), i + 1)
                    if col is None:
                        chain(dve.tensor_tensor(x(i), x(i), buf(i), ALU.mult))
                    else:
                        chain(dve.scalar_tensor_tensor(x(i), x(i), col, buf(i), ALU.mult, ALU.mult))
                dve.sem_clear(sem("rs_full"))
            def start_inverse(TA, d, s):
                A, Tm, X = [tiles4(TA[:, i + s, :]) for i in (0, 2, 6)]
                chain(dve.tensor_tensor(X, A, level(d, 0), ALU.mult))
                dve.sem_inc(sem(f"xy_full{s}"), 1)
                chain(dve.tensor_tensor(Tm, over_tiles(ident), X, ALU.subtract))
                dve.sem_inc(sem(f"t_full{s}"), 1)
            def invert(TA, d):
                A, Tm, Y, X, _ = [[tiles4(TA[:, 2 * i + s, :]) for s in range(2)] for i in range(5)]
                I4 = over_tiles(ident)
                for s in range(2):
                    take(dve, for_dve[s])
                    chain.mark(dve.tensor_tensor(X[s], A[s], level(d, 1), ALU.mult))
                    chain(dve.tensor_tensor(Y[s], I4, tiles4(bank[s][:, :]), ALU.subtract))
                    dve.sem_inc(bank_free[s], 1)
                    dve.sem_inc(sem(f"xy_full{s}"), 1)
                for l in range(1, LEVELS):
                    for s in range(2):
                        take(dve, for_dve[2 + s])
                        if l < LEVELS - 1:
                            chain.mark(dve.tensor_tensor(X[s], A[s], level(d, l + 1), ALU.mult))
                        chain(dve.tensor_tensor(Y[s], Y[s], tiles4(bank[2 + s][:, :]), ALU.subtract))
                        dve.sem_inc(bank_free[2 + s], 1)
                        dve.sem_inc(sem(f"xy_full{s}"), 1)
                        if l < LEVELS - 1:
                            take(dve, for_dve[4 + s])
                            chain(dve.tensor_tensor(Tm[s], Tm[s], tiles4(bank[4 + s][:, :]), ALU.subtract))
                            dve.sem_inc(bank_free[4 + s], 1)
                            dve.sem_inc(sem(f"t_full{s}"), 1)
            def recurrence(d, n_heads, u0, U, S, next_state, first_tile, add):
                nt = n_heads // 2
                for n in range(TT):
                    t = n if d == 0 else TT - 1 - n
                    if n == 0:
                        chain(dve.tensor_copy(U, u0[:, t]))
                    else:
                        for s, b in ((0, 0), (1, 2)):
                            take(dve, for_dve[b])
                            chain(dve.tensor_tensor(U[:, s:n_heads:2], u0[:, t, s:n_heads:2],
                                                    bank[b][:, 0:nt * 64].rearrange("p (h n) -> p h n", h=nt), ALU.subtract))
                            dve.sem_inc(bank_free[b], 1)
                    dve.sem_inc(sem("u_full"), 1)
                    if n < TT - 1:
                        take(dve, for_dve[3])
                        next_state(n, t, bank[3][:, 0:nt * 64].rearrange("p (h n) -> p h n", h=nt))
                        dve.sem_inc(bank_free[3], 1)
                        dve.sem_inc(sem("state_full"), 1)
                    take(dve, for_dve[1])
                    dst = mix[:, first_tile:first_tile + nt, t * P:(t + 1) * P]
                    src = bank[1][:, 0:nt * P].rearrange("p (h n) -> p h n", h=nt)
                    if add:
                        chain(dve.tensor_tensor(dst, dst, src, ALU.add))
                    else:
                        chain(dve.tensor_copy(dst, src))
                    dve.sem_inc(bank_free[1], 1)
            meet()
            dve.sem_inc(sem("norm_in_full"), 1)
            chain.reset()
            with dve.Fori(0, LAYERS) as l:
                take(dve, sem("par_full"), 32)
                take(dve, sem("rs_full"))
                for k in range(KD):
                    dve.scalar_tensor_tensor(hT[:, k, :], xT[:, k, :], par2("norm_g", k), rs[:], ALU.mult,
                                             ALU.mult).then_inc(sem("tiles_full"), 1)
                for i in range(2):
                    chain(dve.memset(pads[i][:, 0:2], 0.0))
                    chain(dve.memset(pads[i][:, 2 + T:4 + T], 0.0))
                dve.sem_inc(sem("rs_free"), 1)
                for i in range(9):
                    if i == 6:
                        take(dve, for_dve[2])
                        ab = bank[2][:, 0:96].rearrange("p (t c) -> p t c", t=TT)
                        bias = row2[:, 12:24].rearrange("p (o c) -> p o c", o=1).to_broadcast([P, TT, 12])
                        chain(dve.tensor_tensor(g_y, ab[:, :, 0:12], bias, ALU.add))
                        chain(dve.tensor_copy(g_beta, ab[:, :, 12:24]))
                        dve.sem_inc(bank_free[2], 1)
                        chain(dve.scalar_tensor_tensor(g_neg, g_y, -1.0, g_y, ALU.mult, ALU.min))
                        dve.sem_inc(sem("args_full"), 1)
                    if i == 8:
                        take(dve, sem("func_full"))
                        chain(dve.scalar_tensor_tensor(g_g, g_y, 0.0, g_ln, ALU.max, ALU.add))
                        ea = g_ea.rearrange("p (o c) -> p o c", o=1).to_broadcast([P, TT, 12])
                        chain(dve.scalar_tensor_tensor(g_g, g_g, -1.0, ea, ALU.mult, ALU.mult))
                        dve.sem_inc(sem("g_full"), 1)
                    dst = g_qk[:, i, :] if i < 6 else g_v[:, i - 6, :]
                    pad = pads[i % 2]
                    take(dve, sem(f"pad_full{i % 2}"))
                    chain(dve.tensor_scalar(dst, pad[:, 0:T], par2("conv", 5 * i), None, ALU.mult))
                    for j in range(1, 5):
                        chain(dve.scalar_tensor_tensor(dst, pad[:, j:j + T], par2("conv", 5 * i + j), dst, ALU.mult, ALU.add))
                    dve.sem_inc(sem(f"pad_free{i % 2}"), 1)
                    dve.sem_inc(sem(f"conv_full{i % 2}"), 1)
                take(dve, for_dve[2])
                chain(dve.tensor_copy(g_cum, bank[2][:, 0:48].rearrange("p (t c) -> p t c", t=TT)))
                chain(dve.tensor_copy(g_ge, bank[2][:, 64:112].rearrange("p (t c) -> p t c", t=TT)))
                chain(dve.tensor_tensor(g_dec, g_ge, g_cum, ALU.subtract))
                dve.sem_inc(bank_free[2], 1)
                dve.sem_inc(sem("args_full"), 1)
                take(dve, sem("func_full"))
                chain(dve.tensor_tensor(g_bg, g_beta, g_gam, ALU.mult))
                for s in range(2):
                    for d in range(2):
                        chain(dve.tensor_copy(g_ge2[64 * s:64 * s + 64, d], g_ge[64 * s:64 * s + 64, :, 6 * d + s:6 * d + 6:2]
                                              .rearrange("p t h -> p h t")))
                dve.sem_inc(sem("tok_full"), 1)
                times_roots(6, lambda i: g_qk[:, i, :], lambda i: g_TA[:, i, :])
                dve.sem_inc(sem("k_ch_full"), 1)
                for d in range(2):
                    for ht in range(3):
                        TA = g_TA
                        for s in range(2):
                            c = 6 * d + 2 * ht + s
                            XD, X, V = TA[:, 2 + s, :], TA[:, 6 + s, :], TA[:, 8 + s, :]
                            take(dve, for_dve[s])
                            chain(dve.tensor_tensor(tiles4(XD), tiles4(bank[s][:, :]), along(g_cum[:, :, c]), ALU.subtract))
                            dve.sem_inc(sem(f"cb_full{s}"), 1)
                            keep1, keep2 = ("nLE", "nGT") if d == 0 else ("nGE", "nLT")
                            chain(dve.scalar_tensor_tensor(tiles4(V), tiles4(XD), 0.0, over_tiles(const2(keep1)), ALU.min, ALU.add))
                            chain(dve.scalar_tensor_tensor(tiles4(X), tiles4(XD), 0.0, over_tiles(const2(keep2)), ALU.max, ALU.subtract))
                            dve.sem_inc(sem(f"d_args{s}"), 1)
                        for s in range(2):
                            c = 6 * d + 2 * ht + s
                            lo = 64 * s
                            A, Y, X, V = [TA[:, i + s, :] for i in (0, 4, 6, 8)]
                            take(dve, sem(f"d_full{s}"))
                            take(dve, for_dve[4 + s])
                            chain(dve.tensor_tensor(g_PT[:, 2 * ht + s, :], bank[4 + s][:, :], V, ALU.mult))
                            dve.sem_inc(bank_free[4 + s], 1)
                            take(dve, for_dve[2 + s])
                            chain(dve.tensor_tensor(A, bank[2 + s][:, :], X, ALU.mult))
                            dve.sem_inc(bank_free[2 + s], 1)
                            chain(dve.tensor_tensor(tiles4(A), tiles4(A), along(g_beta[:, :, c]), ALU.mult))
                            chain(dve.tensor_tensor(g_qg[lo:lo + 64, ht, :], g_qk[lo:lo + 64, ht, :], Y[lo:lo + 64, :], ALU.mult))
                        for s in range(2):
                            start_inverse(TA, d, s)
                        invert(TA, d)
                    take(dve, sem("chunks_act"))
                    dve.sem_inc(sem("chunks_full"), 1)
                    def next_state(n, t, inc):
                        new, old = g_S[:, (n + 1) % 2], g_S[:, n % 2]
                        if n == 0:
                            chain(dve.tensor_copy(new, inc))
                        else:
                            ge = g_ge2[:, d, :, t:t + 1].to_broadcast([P, 3, 64])
                            chain(dve.tensor_tensor(new, old, ge, ALU.mult))
                            chain(dve.tensor_tensor(new, new, inc, ALU.add))
                    recurrence(d, GH, g_u0, g_U, g_S, next_state, 0, d == 1)
                    if d == 0:
                        dve.sem_inc(sem("dir_done"), 1)
                dve.sem_inc(sem("norm_in_full"), 1)
                times_roots(3, lambda i: mix[:, i, :], lambda i: g_TA[:, i, :], par2("gdn_g"))
                meet()
                for i in range(2):
                    chain(dve.memset(r_pads[i][:, 0:1], 0.0))
                    chain(dve.memset(r_pads[i][:, 1 + T:2 + T], 0.0))
                chain(dve.tensor_tensor(r_c0, par2("mu0", 0, 7), par2("mu1", 0, 7), ALU.add))
                chain(dve.tensor_scalar(r_c0, r_c0, -1.0, 1.0, ALU.mult, ALU.add))
                chain(dve.tensor_scalar(r_oka, par2("k_a", 0, 2), -1.0, 1.0, ALU.mult, ALU.add))
                for i in range(7):
                    dst = r_f[:, i, :] if i < 6 else r_wa[:, 0, :]
                    pad = r_pads[i % 2]
                    take(dve, sem(f"pad_full{i % 2}"))
                    chain(dve.tensor_scalar(dst, pad[:, 1:1 + T], r_c0[:, i:i + 1], None, ALU.mult))
                    chain(dve.scalar_tensor_tensor(dst, pad[:, 0:T], par2("mu0", i), dst, ALU.mult, ALU.add))
                    chain(dve.scalar_tensor_tensor(dst, pad[:, 2:2 + T], par2("mu1", i), dst, ALU.mult, ALU.add))
                    dve.sem_inc(sem(f"pad_free{i % 2}"), 1)
                for i in range(2):
                    chain(dve.tensor_scalar(r_kk[:, i, :], r_f[:, 2 + i, :], par2("k_k", i), None, ALU.mult))
                dve.sem_inc(sem("norm_in_full"), 1)
                times_roots(2, lambda i: r_kk[:, i, :], lambda i: r_TA[:, 8 + i, :])
                for e in range(2):
                    TA = r_TA
                    for ct in range(2):
                        SG, AV, L, A1, A2, E_up, E_dn, E_pr, KM = [TA[:, i, :] for i in range(9)]
                        take(dve, sem("sig_full"))
                        chain(dve.tensor_tensor_scan(L, const2("reset"), SG, 0.0, ALU.mult, ALU.add))
                        mid, tot = tiles4(L)[:, :, CHUNK // 2 - 1], tiles4(L)[:, :, CHUNK - 1]
                        chain(dve.tensor_copy(r_m[:, ct, :], mid))
                        chain(dve.tensor_tensor(r_d[:, ct, :], tot, r_m[:, ct, :], ALU.subtract))
                        chain(dve.tensor_tensor(tiles4(A1), tiles4(L), along(r_m[:, ct, :]), ALU.subtract))
                        chain(dve.tensor_tensor(A2, A1, SG, ALU.subtract))
                        dve.sem_inc(sem("args_full"), 1)
                        chain(dve.tensor_scalar(KM, AV, par2("k_a", ct), r_oka[:, ct:ct + 1], ALU.mult, ALU.add))
                        chain(dve.tensor_tensor(KM, KM, r_f[:, 2 + ct, :], ALU.mult))
                        if e == 0:
                            chain(dve.tensor_copy(r_bon[:, ct, :], KM))
                        else:
                            chain(dve.tensor_tensor(r_bon[:, ct, :], r_bon[:, ct, :], KM, ALU.add))
                        chain(dve.tensor_tensor(AV, AV, r_kk[:, ct, :], ALU.mult))
                        take(dve, sem("func_full"))
                        chain(dve.tensor_tensor(r_kt[:, ct, :], r_kk[:, ct, :], E_pr, ALU.mult))
                        dve.sem_inc(sem("kt_full"), 1)
                        chain(dve.tensor_tensor(r_bt[:, ct, :], AV, E_dn, ALU.mult))
                        chain(dve.tensor_tensor(r_kmt[:, ct, :], KM, E_dn, ALU.mult))
                        chain(dve.tensor_tensor(r_rt[:, ct, :], r_f[:, ct, :], E_up, ALU.mult))
                        if ct == 0:
                            dve.sem_inc(sem("ta_free"), 1)
                    pre, post = (r_pm, r_pd) if e == 0 else (r_pd, r_pm)
                    for t in range(TT):
                        nx = t + 1 if e == 0 else t - 1
                        if 0 <= nx < TT:
                            chain(dve.tensor_tensor(r_sc[:, :, t:t + 1], post[:, :, t:t + 1], pre[:, :, nx:nx + 1], ALU.mult))
                    for ct in range(2):
                        after, incl, A_keep = ("LT", "LE", "GT") if e == 0 else ("GT", "GE", "LT")
                        def masked(b, dst, m):
                            take(dve, for_dve[b])
                            chain(dve.tensor_tensor(tiles4(dst), tiles4(bank[b][:, :]), over_tiles(const2(m)), ALU.mult))
                            dve.sem_inc(bank_free[b], 1)
                        for s in range(2):
                            masked(2 + s, r_BT[s], after)
                            masked(6 + s, r_PkT[:, s, :], incl)
                        dve.sem_inc(sem("bp_full"), 1)
                        for s in range(2):
                            masked(s, TA[:, s, :], A_keep)
                            start_inverse(TA, e, s)
                        for s in range(2):
                            masked(4 + s, r_PbT[:, 2 * ct + s, :], incl)
                        take(dve, sem("direct_full"))
                        if e == 0:
                            chain(dve.tensor_copy(mix[:, 6 + ct, :], bank[7][:, :]))
                        else:
                            chain(dve.tensor_tensor(mix[:, 6 + ct, :], mix[:, 6 + ct, :], bank[7][:, :], ALU.add))
                        dve.sem_inc(bank_free[7], 1)
                        invert(TA, e)
                    take(dve, sem("chunks_act"))
                    dve.sem_inc(sem("chunks_full"), 1)
                    def next_state(n, t, inc):
                        new, old = r_S[:, (n + 1) % 2], r_S[:, n % 2]
                        sc = r_sc[:, :, t:t + 1].to_broadcast([P, 2, 64])
                        if n == 0:
                            chain(dve.tensor_tensor(new, inc, sc, ALU.mult))
                        else:
                            chain(dve.tensor_tensor(new, old, inc, ALU.add))
                            chain(dve.tensor_tensor(new, new, sc, ALU.mult))
                    recurrence(e, RH, r_u0, r_U, r_S, next_state, 6, True)
                    if e == 0:
                        dve.sem_inc(sem("ta_free"), 1)
                dve.sem_inc(sem("ta_free"), 1)
                for i in range(2):
                    y = mix[:, 6 + i, :]
                    dve.sem_inc(sem("y_full"), 1)
                    take(dve, for_dve[5])
                    chain(dve.scalar_tensor_tensor(y, bank[5][:, :], -1.0 / 64, y, ALU.mult, ALU.add))
                    dve.sem_inc(bank_free[5], 1)
                    dve.sem_inc(sem("norm_in_full"), 1)
                    chain(dve.scalar_tensor_tensor(r_bon[:, i, :], r_bon[:, i, :], par2("r_k", i), r_f[:, i, :], ALU.mult, ALU.mult))
                    dve.sem_inc(sem("bonus_full"), 1)
                    times_rs(y, y)
                    chain(dve.tensor_scalar(y, y, par2("ln_g", i), par2("ln_b", i), ALU.mult, ALU.add))
                    take(dve, for_dve[7])
                    chain(dve.tensor_tensor(r_kt[:, i, :], bank[7][:, :], r_f[:, 4 + i, :], ALU.mult))
                    dve.sem_inc(bank_free[7], 1)
                    chain(dve.scalar_tensor_tensor(y, r_kt[:, i, :], 0.5, y, ALU.mult, ALU.add))
                meet()
                dve.wait_ge(sem("rs_full"), 1)
                chain(dve.scalar_tensor_tensor(m_cq[:, 0, :], m_cq[:, 0, :], par2("qn_g"), m_tmp[:, 0, :], ALU.mult, ALU.mult))
                chain(dve.scalar_tensor_tensor(m_cq[0:64, 1, :], m_cq[0:64, 1, :], par2("qn_g", 1)[0:64], m_tmp[0:64, 0, :], ALU.mult, ALU.mult))
                dve.sem_inc(sem("latent_in_full"), 1)
                take(dve, sem("rs_full"), 2)
                chain(dve.scalar_tensor_tensor(m_ckv[:, 0, :], m_ckv[:, 0, :], par2("kvn_g"), m_tmp[:, 1, :], ALU.mult, ALU.mult))
                dve.sem_inc(sem("latent_in_full"), 1)
                rot = slice(64, 96)
                def rotate(x, b, j):
                    take(dve, for_dve[b])
                    chain(dve.tensor_tensor(m_tmp[rot, j, :], bank[b][rot, :], sinM[rot, :], ALU.mult))
                    dve.sem_inc(bank_free[b], 1)
                    chain(dve.tensor_tensor(x, x, cosM[rot, :], ALU.mult))
                    chain(dve.tensor_tensor(x, x, m_tmp[rot, j, :], ALU.add))
                rotate(m_kr[rot, 0, :], 3, 0)
                dve.sem_inc(sem("kr_full"), 1)
                for h in range(MH):
                    rotate(m_q[rot, h, :], 2 + h % 2, h % 2)
                    if h == MH - 1:
                        take(dve, sem("k_rot_full"))
                    dve.sem_inc(sem("mla_q_full"), 1)
                n = MH * TT
                for i in range(n + 1):
                    if i < n:
                        st = m_st[:, i % 4]
                        take(dve, for_dve[i % 4])
                        chain(dve.tensor_reduce(st[:, 2:3], bank[i % 4][:, :], AX.X, ALU.max))
                        chain(dve.tensor_scalar(st[:, 0:1], st[:, 2:3], -QK_M ** -0.5, None, ALU.mult))
                        dve.sem_inc(sem("maxima_ready"), 1)
                    if i >= 1:
                        j = (i - 1) % 4
                        st = m_st[:, j]
                        dve.wait_ge(sem("exps_ready"), i)
                        chain(dve.reciprocal(st[:, 3:4], st[:, 1:2]))
                        chain(dve.tensor_scalar(m_pr[:, j, :], m_pr[:, j, :], st[:, 3:4], None, ALU.mult))
                        dve.sem_inc(sem("probs_ready"), 1)
                dve.sem_clear(sem("exps_ready"))
                for i in range(8):
                    take(dve, sem(f"sg_full{i % 2}"))
                    chain(dve.tensor_tensor(mix[:, i, :], mix[:, i, :], m_gate[:, i % 2, :], ALU.mult))
                    dve.sem_inc(sem(f"sg_free{i % 2}"), 1)
                    dve.sem_inc(sem("tiles_full"), 1)
                for m_ in range(8):
                    b = 4 + m_ % 4
                    take(dve, for_dve[b])
                    chain(dve.tensor_tensor(xT[:, m_, :], xT[:, m_, :], bank[b][:, :], ALU.add))
                    dve.sem_inc(bank_free[b], 1)
                    if m_ % 4 == 3:
                        dve.sem_inc(slot_free[(8 + m_ // 4) % 2], 1)
                dve.sem_inc(sem("par_free"), 1)
                dve.sem_inc(sem("norm_in_full"), 1)
                chain.reset()
            take(dve, sem("rs_full"))
            for k in range(KD):
                chain(dve.scalar_tensor_tensor(hT[:, k, :], xT[:, k, :], par("final2_g", k), rs[:], ALU.mult, ALU.mult))
            dve.sem_inc(sem("done"), 1)

        block = ctx.enter_context(nc.Block())

        @block.sync
        def _(sp):
            for n, u in enumerate(units):
                take(sp, slot_free[n % SLOTS])
                sp.dma_start(slot(n), u).then_inc(slot_full[n % SLOTS], 16)
                if n == 0:
                    sp.dma_start(xT[:], xT_d.rearrange("(k p) t -> p k t", p=P)).then_inc(sem("x_loaded"), 16)
            def expert_weights(e_j, e, ring_at):
                for i, (w, k) in enumerate(((w_gate, 8), (w_up, 8), (w_down, 4))):
                    take(sp, slot_free[ring_at + i])
                    src = w[0].rearrange("(i j) d n -> i j d n", j=1 if e_j is None else 2)
                    src = src[bass.ds(e, 1), 0 if e_j is None else e_j].rearrange("a (k p) n -> p (a k) n", p=P)
                    sp.dma_start(slot(ring_at + i, k), src).then_inc(slot_full[ring_at + i], 16)
            with sp.Fori(0, N_EXP // 2) as pair:
                for j in range(2):
                    expert_weights(j, pair, 3 * j)
            sp.wait_ge(sem("routed"), 2)
            n_more = sp.value_load(meta[0:1, N_MORE:MORE], min_val=0, max_val=N_MORE)
            with sp.Fori(0, N_MORE) as m:
                with sp.If(m < n_more):
                    expert = sp.value_load(meta[0:1, bass.ds(m, 1)], min_val=0, max_val=N_EXP - 1)
                    expert_weights(None, expert, 0)
            sp.wait_ge(sem("y_stored"), 1)
            sp.dma_start(c2, w2["cn"]).then_inc(sem("const2_full"), 16)
            pos = w2["positions"].to_broadcast([P, T])
            sp.dma_start(hT[:, 7, :].bitcast(I32), pos).then_inc(sem("const2_full"), 16)
            for t in range(TT):
                sp.dma_start(y_tok[:, t], y_d[2 * t * P:2 * (t + 1) * P, :].rearrange("(p k) d -> p k d", k=2))\
                  .then_inc(sem("y_loaded"), 16)
            sp_second(sp)

        @block.gpsimd
        def _(pool):
            for b in range(8):
                pool.sem_inc(bank_free[b], 1)
            for s in range(SLOTS):
                pool.sem_inc(slot_free[s], 1)
            for name in ("rs_free",):
                pool.sem_inc(sem(name), 1)
            for j in range(2):
                pool.sem_inc(sem(f"sg_free{j}"), 1)
                pool.sem_inc(sem(f"x_free{j}"), 1)
                pool.sem_inc(sem(f"yb_free{j}"), 1)
                pool.sem_inc(sem(f"sq_free{j}"), 1)
                pool.sem_inc(sem(f"probs_free{j}"), 1)
                pool.sem_inc(sem(f"wgt_free{j}"), 1)
                pool.sem_inc(sem(f"wT_free{j}"), 1)
            pool.memset(u_pad, 0.0).then_inc(sem("pad_zero"), 1)
            pool.wait_ge(sem("scores_done"), 1)
            for g in range(4):
                pool.dma_start(inv_c[:, g, :], invcnt[g:g + 1, :].to_broadcast([P, T])).then_inc(sem("inv_loaded"), 16)
            pchain = Chain(pool, sem("pool_chain"))
            pool.wait_ge(sem("pooled"), 1)
            pchain(pool.memset(info, NO_SLOT))
            pool.dma_start(slot_d.rearrange("r c -> (r c)").rearrange("(s n) -> s n", s=P), info.rearrange("p b c -> p (b c)")).then_inc(sem("slot_table"), 16)
            pool.wait_ge(sem("slot_table"), 16)
            pool.wait_ge(sem("routed"), 1)
            for k in range(2):
                for t in range(TT):
                    pool.indirect_dma_start(
                        slot_d, bass.IndirectOffsetOnAxis(ap=dest[:, k, t:t + 1], axis=0), rows[:, k, t, :], None,
                        bounds_check=N_BLK * CAP - 1, oob_is_err=False).then_inc(sem("slot_table"), 16)
            pool.wait_ge(sem("slot_table"), 16 + 16 * 2 * TT)
            for c in range(2):
                pool.dma_start(info[c * CAP:(c + 1) * CAP], slot_d.rearrange("(b s) c -> s b c", s=CAP)[:, :, 4 * c:4 * c + 4])\
                    .then_inc(sem("slot_table"), 16)
            pool.wait_ge(sem("slot_table"), 48 + 16 * 2 * TT)
            pool.wait_ge(sem("h_stored"), 16 * TT)
            for j in range(2):
                pchain(pool.memset(X[j], 0.0))
            h_half = h_d.rearrange("t (c n) -> (t c) n", c=2)
            y_half = y_d.rearrange("t (c n) -> (t c) n", c=2)
            def info_of(block):
                return info[:, bass.ds(block, 1), :].rearrange("p a c -> p (a c)")
            def gather(j, block):
                take(pool, sem(f"x_free{j}"))
                pchain(pool.tensor_copy(cur[j], info_of(block)))
                pool.indirect_dma_start(
                    X[j], None, h_half, bass.IndirectOffsetOnAxis(ap=cur[j][:, 0:1].bitcast(U32), axis=0),
                    bounds_check=2 * T - 1, oob_is_err=False).then_inc(sem("rows_loaded"), 16)
            def gathered(j, number):
                pool.wait_ge(sem("rows_loaded"), number * 16)
                pool.sem_inc(sem(f"x_full{j}"), 1)
            def scatter(j, block):
                pchain(pool.tensor_copy(cur_y[j], info_of(block)))
                take(pool, sem(f"y_full{j}"))
                pool.indirect_dma_start(
                    y_half, bass.IndirectOffsetOnAxis(ap=cur_y[j][:, 1:2].bitcast(U32), axis=0), Yb[j], None,
                    bounds_check=4 * T - 1, oob_is_err=False).then_inc(sem("rows_stored"), 16)
            def scattered(j, number):
                pool.wait_ge(sem("rows_stored"), number * 16)
                pool.sem_inc(sem(f"yb_free{j}"), 1)
            for j in range(2):
                gather(j, j)
                gathered(j, j + 1)
            gather(0, 2)
            gathered(0, 3)
            gather(1, 3)
            scatter(0, 0)
            gathered(1, 4)
            pchain.reset()
            with pool.Fori(0, N_EXP // 2 - 2) as pair:
                for j in range(2):
                    gather(j, 2 * pair + 4 + j)
                    scattered(j, 2 * pair + 1 + j)
                    scatter(1 - j, 2 * pair + 1 + j)
                    gathered(j, 2 * pair + 5 + j)
                pchain.reset()
            for i in range(N_EXP - 3, N_EXP):
                scattered((i + 1) % 2, i)
                scatter(i % 2, i)
            scattered(1, N_EXP)
            pchain.reset()
            pool.wait_ge(sem("routed"), 2)
            n_more = pool.value_load(meta[0:1, N_MORE:MORE], min_val=0, max_val=N_MORE)
            with pool.Fori(0, N_MORE) as m:
                with pool.If(m < n_more):
                    gather(0, m + N_EXP)
                    gathered(0, m + N_EXP + 1)
                    scatter(0, m + N_EXP)
                    scattered(0, m + N_EXP + 1)
                    pchain.reset()
            pool.sem_inc(sem("y_stored"), 1)
            pool_second(pool)

        @block.tensor
        def _(pe):
            def sumsq(b, tiles, n0, mat=ones, rows=None):
                take(pe, bank_free[b])
                for i in range(tiles):
                    take(pe, sem(f"sq_full{(n0 + i) % 2}"))
                    r = P if rows is None else rows[i]
                    m = pe.matmul(bank[b][:, :], mat[0:r, :], sq[0:r, (n0 + i) % 2, :], start=(i == 0), stop=(i == tiles - 1))
                    if i < tiles - 1:
                        m.then_inc(sem(f"sq_free{(n0 + i) % 2}"), 1)
                m.then_inc(for_act[b], 1)

            pe.wait_ge(sem("params_loaded"), 16 * 3)
            pe.wait_ge(sem("silu_c"), 1)

            def mod_products(u):
                take(pe, slot_full[ada_at[u] % SLOTS], 16)
                b = 6 * (u % 2)
                take(pe, bank_free[b])
                for k in range(KD):
                    q = 32 * (k % 4)
                    mm = pe.matmul(bank[b][q:q + 32, :], small[:, k:k + 1].to_broadcast([P, 32]), slot(ada_at[u])[:, k, :],
                                   start=(k < 4), stop=(k >= 4))
                mm.then_inc(for_act[b], 1)
            def mod_columns(u):
                take(pe, sem(f"wT_full{u % 2}"))
                if u % 4 == 0:
                    take(pe, bank_free[7])
                for m in range(4):
                    col = 4 * (u % 4) + m
                    mm = pe.matmul(bank[7][:, col:col + 1], mod_rows[:, u % 2, m * P:(m + 1) * P], quarters, start=True, stop=True)
                if u % 4 == 3:
                    mm.then_inc(for_dve[7], 1)
            def mod_pair(n):
                for u in (4 + 2 * n, 5 + 2 * n):
                    mod_products(u)
                    if u > 4:
                        mod_columns(u - 1)

            for u in range(4):
                mod_products(u)
                if u > 0:
                    mod_columns(u - 1)
            mod_columns(3)
            sumsq(1, KD, 0)
            for n in range(2):
                s = in_at[n] % SLOTS
                take(pe, slot_full[s], 16)
                for m in range(4):
                    i = n * 4 + m
                    b = 2 + i % 2
                    take(pe, bank_free[b])
                    for k in range(KD):
                        if n == 0 and m == 0:
                            pe.wait_ge(sem("h_ready"), k + 1)
                        mm = pe.matmul(bank[b][:, :], slot(s)[:, k, m * P:(m + 1) * P], hT[:, k, :],
                                       start=(k == 0), stop=(k == KD - 1))
                    mm.then_inc(for_act[b], 1)
                    if i > 0:
                        j = i - 1
                        pe.wait_ge(sem("raw_ready"), j + 1)
                        take(pe, bank_free[4 + j % 2])
                        pe.matmul(bank[4 + j % 2][:, :], const("rotA"), raw[:, j % 2, :], start=True,
                                  stop=True).then_inc(for_dve[4 + j % 2], 1)
                pe.wait_ge(sem("raw_ready"), n * 4 + 4)
                pe.sem_inc(slot_free[s], 1)
                mod_pair(n)
            take(pe, bank_free[5])
            pe.matmul(bank[5][:, :], const("rotA"), raw[:, 1, :], start=True, stop=True).then_inc(for_dve[5], 1)
            s = in_at[2] % SLOTS
            take(pe, slot_full[s], 16)
            for t in range(TT):
                b = 2 + t % 2
                take(pe, bank_free[b])
                for k in range(KD):
                    mm = pe.matmul(bank[b][:, :], hT[:, k, t * P:(t + 1) * P], slot(s)[:, k, :],
                                   start=(k == 0), stop=(k == KD - 1))
                mm.then_inc(for_act[b], 1)
            pe.wait_ge(sem("v_ready"), TT)
            pe.sem_inc(slot_free[s], 1)
            mod_pair(2)
            s = in_at[3] % SLOTS
            take(pe, slot_full[s], 16)
            for m in range(4):
                b = 2 + m % 2
                take(pe, bank_free[b])
                for k in range(KD):
                    mm = pe.matmul(bank[b][:, :], slot(s)[:, k, m * P:(m + 1) * P], hT[:, k, :],
                                   start=(k == 0), stop=(k == KD - 1))
                mm.then_inc(for_act[b], 1)
            pe.wait_ge(sem("u_ready"), 4)
            pe.sem_inc(slot_free[s], 1)
            mod_pair(3)
            mod_columns(11)

            steps = [(h, q) for h in range(HEADS) for q in range(TT)]
            def scores(i):
                h, q = steps[i]
                for c in range(2):
                    b = 2 * (i % 2) + c
                    take(pe, bank_free[b])
                    lo = c * HD
                    pe.matmul(bank[b][:, :], qkT[lo:lo + HD, h, q * P:(q + 1) * P], qkT[lo:lo + HD, 4 + h, :],
                              start=True, stop=True).then_inc(for_dve[b], 1)
            def weights(i):
                h, q = steps[i]
                take(pe, sem(f"wgt_full{i % 2}"))
                b = 4 + i % 2
                take(pe, bank_free[b])
                for kt in range(TT):
                    mm = pe.transpose(bank[b][:, kt * P:(kt + 1) * P], wgt[:, i % 2, kt * P:(kt + 1) * P], ident)
                mm.then_inc(for_act[b], 1)
            def values(i):
                h, q = steps[i]
                take(pe, sem(f"wT_full{i % 2}"))
                b = 6 + h % 2
                if q == 0:
                    take(pe, bank_free[b])
                for kt in range(TT):
                    mm = pe.matmul(bank[b][:, q * P:(q + 1) * P], v_tok[:, kt, h * P:(h + 1) * P],
                                   wTq[:, i % 2, kt * P:(kt + 1) * P], start=(kt == 0), stop=(kt == TT - 1))
                if q == TT - 1:
                    mm.then_inc(for_act[b], 1)
                else:
                    mm.then_inc(sem(f"wT_free{i % 2}"), 1)
            pe.wait_ge(sem("qk_ready"), 8)
            for i in range(len(steps) + 3):
                if i < len(steps):
                    scores(i)
                if 2 <= i < len(steps) + 2:
                    weights(i - 2)
                if i >= 3:
                    values(i - 3)
            for h in range(HEADS):
                sumsq(h % 2, 1, h)
            pe.wait_ge(sem("pool_w_loaded"), 16)
            for g in range(4):
                b = 2 + g % 2
                take(pe, bank_free[b])
                pe.wait_ge(sem("pooled"), g + 1)
                pe.matmul(bank[b][:, :], pool_w[:, g, :], u_pad[:, g, 0:T], start=True,
                          stop=True).then_inc(for_act[b], 1)
            pe.wait_ge(sem("mix_ready"), 8)
            for n in range(2):
                s = (out_at + n) % SLOTS
                take(pe, slot_full[s], 16)
                for m in range(4):
                    b = 4 + m
                    take(pe, bank_free[b])
                    for k in range(KD):
                        mm = pe.matmul(bank[b][:, :], slot(s)[:, k, m * P:(m + 1) * P], mixT[:, k, :],
                                       start=(k == 0), stop=(k == KD - 1))
                    mm.then_inc(for_dve[b], 1)
                pe.wait_ge(sem("x_mixed"), 4 * n + 4)
                pe.sem_inc(slot_free[s], 1)
            sumsq(1, KD, 0)
            pe.wait_ge(sem("router_loaded"), 32)
            pe.wait_ge(sem("h_ready"), 2 * KD)
            take(pe, bank_free[0])
            for t in range(TT):
                for k in range(KD):
                    mm = pe.matmul(bank[0][:, t * 36:(t + 1) * 36], hT[:, k, t * P:(t + 1) * P], w_router[:, k, :],
                                   start=(k == 0), stop=(k == KD - 1))
            mm.then_inc(for_dve[0], 1)
            for t in range(TT):
                for c in range(2):
                    b = 1 + c
                    take(pe, bank_free[b])
                    for k in range(4):
                        mm = pe.transpose(bank[b][:, k * P:(k + 1) * P], hT[:, 4 * c + k, t * P:(t + 1) * P], ident)
                    mm.then_inc(for_act[b], 1)
            pe.wait_ge(sem("choices_full"), 1)
            take(pe, bank_free[0])
            for t in range(TT):
                for i in range(t):
                    pe.matmul(bank[0][:, t * N_EXP:(t + 1) * N_EXP], ones, Ms[:, i, :], start=(i == 0), stop=False)
                pe.matmul(bank[0][:, t * N_EXP:(t + 1) * N_EXP], const("lt"), Ms[:, t, :], start=(t == 0), stop=True)
            for t in range(TT):
                mm = pe.matmul(bank[0][:, TT * N_EXP:(TT + 1) * N_EXP], ones, Ms[:, t, :], start=(t == 0), stop=(t == TT - 1))
            mm.then_inc(for_dve[0], 1)

            def turn_inputs(j):
                take(pe, sem(f"x_full{j}"))
                take(pe, bank_free[0])
                for k in range(4):
                    mm = pe.transpose(bank[0][:, k * P:(k + 1) * P], X[j][:, k * P:(k + 1) * P], ident)
                mm.then_inc(for_dve[0], 1)
            def gate_up(j, ring_at):
                take(pe, sem(f"xt_full{j}"))
                for i, reader in ((0, for_act), (1, for_dve)):
                    b = 2 + 2 * j + i
                    take(pe, slot_full[ring_at + i], 16)
                    take(pe, bank_free[b])
                    for k in range(KD):
                        for c in range(2):
                            mm = pe.matmul(bank[b][c * CAP:(c + 1) * CAP, 0:FE // 2], XT[j][:, k % 4, k // 4, :],
                                           slot(ring_at + i)[:, k, c * (FE // 2):(c + 1) * (FE // 2)], start=(k == 0),
                                           stop=(k == KD - 1))
                    mm.then_inc(reader[b], 1)
            def turn_hidden(j):
                take(pe, sem(f"hid_full{j}"))
                take(pe, bank_free[1])
                for f in range(2):
                    mm = pe.transpose(bank[1][:, f * P:(f + 1) * P], hid[:, j, f * P:(f + 1) * P], ident)
                mm.then_inc(for_dve[1], 1)
            def down(j, ring_at):
                take(pe, slot_full[ring_at + 2], 16)
                take(pe, sem(f"hidT_full{j}"))
                take(pe, bank_free[6 + j])
                for f in range(4):
                    for c in range(2):
                        mm = pe.matmul(bank[6 + j][c * CAP:(c + 1) * CAP, :], hidT[:, j, f % 2, f // 2, :],
                                       slot(ring_at + 2, 4)[:, f, c * HALF:(c + 1) * HALF], start=(f == 0), stop=(f == 3))
                mm.then_inc(for_act[6 + j], 1)
            turn_inputs(0)
            turn_inputs(1)
            gate_up(0, 0)
            with pe.Fori(0, N_EXP // 2 - 1) as pair:
                for j in range(2):
                    gate_up(1 - j, 3 * (1 - j))
                    turn_hidden(j)
                    turn_inputs(j)
                    down(j, 3 * j)
            gate_up(1, 3)
            for j in range(2):
                turn_hidden(j)
                down(j, 3 * j)
            pe.wait_ge(sem("routed"), 2)
            n_more = pe.value_load(meta[0:1, N_MORE:MORE], min_val=0, max_val=N_MORE)
            with pe.Fori(0, N_MORE) as m:
                with pe.If(m < n_more):
                    turn_inputs(0)
                    gate_up(0, 0)
                    turn_hidden(0)
                    down(0, 0)
            pe.wait_ge(sem("y_summed"), TT)
            for d in range(KD):
                b = d % 4
                take(pe, bank_free[b])
                for t in range(TT):
                    mm = pe.transpose(bank[b][:, t * P:(t + 1) * P], y_tok[:, t, 0, d * P:(d + 1) * P], ident)
                mm.then_inc(for_dve[b], 1)
            sumsq(1, KD, 0)
            pe_second(pe, sumsq)

        @block.scalar
        def _(act):
            chain = Chain(act, sem("act_chain"))
            act.dma_start(p1[:], par1).then_inc(sem("params_loaded"), 16)
            act.dma_start(c_sb[:], cn).then_inc(sem("params_loaded"), 16)
            act.dma_start(r1[:], row1.to_broadcast([P, N_R1])).then_inc(sem("params_loaded"), 16)
            act.dma_start(pool_w[:], w_pool[0].rearrange("g c d -> c g d")).then_inc(sem("pool_w_loaded"), 16)
            act.dma_start(w_router[:, :, 0:4], w_rg[0].rearrange("(k p) n -> p k n", p=P)).then_inc(sem("router_loaded"), 16)
            act.dma_start(w_router[:, :, 4:36], w_re[0].rearrange("(k p) n -> p k n", p=P)).then_inc(sem("router_loaded"), 16)
            act.wait_ge(sem("params_loaded"), 48)
            act.activation(small[:, 0:8], par("c", 0, 8), ACT.Silu).then_inc(sem("silu_c"), 1)
            take(act, sem("args_full"))
            act.activation(small[:, 18:20], small[:, 16:18], ACT.Exp).then_inc(sem("func_full"), 1)

            def squares(src, tiles, n0=0):
                for i in range(tiles):
                    j = (n0 + i) % 2
                    take(act, sem(f"sq_free{j}"))
                    act.activation(sq[:, j, :], src(i), ACT.Square).then_inc(sem(f"sq_full{j}"), 1)

            def inverse_root(b, scale, last=1):
                take(act, for_act[b])
                chain(act.activation(rs[:], bank[b][:, :], ACT.Ln, bias=eps_col, scale=scale))
                act.sem_inc(bank_free[b], 1)
                act.sem_inc(sem(f"sq_free{last}"), 1)
                act.activation(rs[:], rs[:], ACT.Exp, scale=-0.5).then_inc(sem("rs_ready"), 1)

            def mod_moved(u):
                b = 6 * (u % 2)
                take(act, for_act[b])
                chain(act.activation(mod_rows[:, u % 2, :], bank[b][:, :], ACT.Copy))
                act.sem_inc(bank_free[b], 1)
                act.sem_inc(slot_free[ada_at[u] % SLOTS], 1)
                act.sem_inc(sem(f"wT_full{u % 2}"), 1)

            for u in range(4):
                mod_moved(u)
            act.wait_ge(sem("x_loaded"), 16)
            squares(lambda i: xT[:, i, :], KD)
            inverse_root(1, 1.0 / D)
            act.wait_ge(sem("mod_ready"), 1)
            for k in range(KD):
                act.wait_ge(sem("scaled"), k + 1)
                act.activation(hT[:, k, :], hT[:, k, :], ACT.Identity, bias=mod[:, k:k + 1]).then_inc(sem("h_ready"), 1)
            for i in range(8):
                b = 2 + i % 2
                take(act, for_act[b])
                if i >= 2:
                    act.wait_ge(sem("qk_ready"), i - 1)
                chain(act.activation(raw[:, i % 2, :], bank[b][:, :], ACT.Copy))
                act.sem_inc(bank_free[b], 1)
                act.sem_inc(sem("raw_ready"), 1)
                if i % 4 == 3:
                    mod_moved(4 + i // 2 - 1)
                    mod_moved(5 + i // 2 - 1)
            for t in range(TT):
                b = 2 + t % 2
                take(act, for_act[b])
                chain(act.activation(v_tok[:, t, :], bank[b][:, :], ACT.Copy))
                act.sem_inc(bank_free[b], 1)
                act.sem_inc(sem("v_ready"), 1)
            mod_moved(8)
            mod_moved(9)
            act.wait_ge(sem("pad_zero"), 1)
            for m in range(4):
                b = 2 + m % 2
                take(act, for_act[b])
                chain(act.activation(u_pad[:, m, POOL_PAD:POOL_PAD + T], bank[b][:, :], ACT.Copy))
                act.sem_inc(bank_free[b], 1)
                act.sem_inc(sem("u_ready"), 1)
            mod_moved(10)
            mod_moved(11)

            steps = [(h, q) for h in range(HEADS) for q in range(TT)]
            def exps(i):
                take(act, sem(f"probs_free{i % 2}"))
                for c in range(2):
                    b = 2 * (i % 2) + c
                    take(act, sem(f"max_full{i % 2}{c}"))
                    chain(act.activation(probs[:, i % 2, c, :], bank[b][:, :], ACT.Exp,
                                         bias=stat[:, i % 2, c:c + 1], scale=HD ** -0.5,
                                         accum_out=stat[:, i % 2, 2 + c:3 + c]))
                    act.sem_inc(bank_free[b], 1)
                act.sem_inc(sem(f"probs_full{i % 2}"), 1)
            def move(i):
                h, q = steps[i]
                b = 4 + i % 2
                take(act, for_act[b])
                act.sem_inc(sem(f"wgt_free{i % 2}"), 1)
                take(act, sem(f"wT_free{i % 2}"))
                chain(act.activation(wTq[:, i % 2, :], bank[b][:, :], ACT.Copy))
                act.sem_inc(bank_free[b], 1)
                act.sem_inc(sem(f"wT_full{i % 2}"), 1)
            def head_out(h):
                b = 6 + h % 2
                take(act, for_act[b])
                chain(act.activation(mixT[:, h, :], bank[b][:, :], ACT.Copy))
                act.sem_inc(bank_free[b], 1)
                act.sem_inc(sem("wT_free1"), 1)
            for i in range(len(steps) + 4):
                if i < len(steps):
                    exps(i)
                if i >= 4 and steps[i - 4][1] == TT - 1:
                    head_out(steps[i - 4][0])
                if 2 <= i < len(steps) + 2:
                    move(i - 2)
                if i == len(steps):
                    act.sem_inc(sem("scores_done"), 1)
            rs_head = lambda h: probs[:, h // 2, h % 2, :]
            for h in range(HEADS + 1):
                if h < HEADS:
                    take(act, sem(f"sq_free{h % 2}"))
                    act.activation(sq[:, h % 2, :], mixT[:, h, :], ACT.Square).then_inc(sem(f"sq_full{h % 2}"), 1)
                if h > 0:
                    j = (h - 1) % 2
                    take(act, for_act[j])
                    chain(act.activation(rs_head(h - 1), bank[j][:, :], ACT.Ln, bias=eps_col, scale=1.0 / P))
                    act.sem_inc(bank_free[j], 1)
                    act.sem_inc(sem(f"sq_free{j}"), 1)
            for h in range(HEADS):
                act.activation(rs_head(h), rs_head(h), ACT.Exp, scale=-0.5).then_inc(sem("rs_ready"), 1)
            for g in range(4):
                take(act, for_act[2 + g % 2])
                chain(act.activation(mixT[:, 4 + g, :], bank[2 + g % 2][:, :], ACT.Copy, scale=par("pool_scale", g)))
                act.sem_inc(bank_free[2 + g % 2], 1)
                act.sem_inc(sem("mix_ready"), 1)
            act.wait_ge(sem("x_mixed"), 8)
            squares(lambda i: xT[:, i, :], KD)
            inverse_root(1, 1.0 / D)
            for k in range(KD):
                act.wait_ge(sem("scaled"), KD + k + 1)
                act.activation(hT[:, k, :], hT[:, k, :], ACT.Identity, bias=mod[:, 24 + k:25 + k]).then_inc(sem("h_ready"), 1)
            take(act, sem("args_full"))
            act.activation(rt_exp, rt_arg, ACT.Exp).then_inc(sem("func_full"), 1)
            for t in range(TT):
                for c in range(2):
                    b = 1 + c
                    take(act, for_act[b])
                    chain(act.activation(h_tok[:, t, c * 512:(c + 1) * 512], bank[b][:, :], ACT.Copy))
                    act.sem_inc(bank_free[b], 1)
                act.dma_start(h_d[t * P:(t + 1) * P, :], h_tok[:, t, :]).then_inc(sem("h_stored"), 16)
            act.wait_ge(sem("h_stored"), 16 * TT)

            def gated(j, ring_at):
                take(act, for_act[2 + 2 * j])
                take(act, sem(f"sg_free{j}"))
                chain(act.activation(sg[:, j, :], bank[2 + 2 * j][:, 0:FE // 2], ACT.Silu))
                act.sem_inc(bank_free[2 + 2 * j], 1)
                act.sem_inc(slot_free[ring_at], 1)
                act.sem_inc(sem(f"sg_full{j}"), 1)
            def downed(j, ring_at):
                take(act, sem(f"yb_free{j}"))
                take(act, for_act[6 + j])
                chain(act.activation(Yb[j], bank[6 + j][:, :], ACT.Copy))
                act.sem_inc(bank_free[6 + j], 1)
                act.sem_inc(slot_free[ring_at + 2], 1)
                act.sem_inc(sem(f"y_full{j}"), 1)
            gated(0, 0)
            chain.reset()
            with act.Fori(0, N_EXP // 2 - 1) as pair:
                for j in range(2):
                    gated(1 - j, 3 * (1 - j))
                    downed(j, 3 * j)
                chain.reset()
            gated(1, 3)
            downed(0, 0)
            downed(1, 3)
            chain.reset()
            act.wait_ge(sem("routed"), 2)
            n_more = act.value_load(meta[0:1, N_MORE:MORE], min_val=0, max_val=N_MORE)
            with act.Fori(0, N_MORE) as m:
                with act.If(m < n_more):
                    gated(0, 0)
                    downed(0, 0)
                    chain.reset()
            take(act, sem("args_full"))
            chain(act.activation(sinM[0:QK_M], sinM[0:QK_M], ACT.Sin))
            chain(act.activation(cosM[0:QK_M], cosM[0:QK_M], ACT.Sin))
            act.sem_inc(sem("func_full"), 1)
            act.wait_ge(sem("x_moe"), 8)
            squares(lambda i: xT[:, i, :], KD)
            inverse_root(1, 1.0 / D)
            act_second(act, chain)

        @block.vector
        def _(dve):
            chain = Chain(dve, sem("dve_chain"))
            dve.wait_ge(sem("params_loaded"), 48)
            lam = r1[:, 0:256].rearrange("p (a b c) -> p a b c", a=2, b=2)
            lam_p = small[:, 128:256].rearrange("p (a c) -> p a c", a=2)
            chain(dve.tensor_tensor(lam_p, lam[:, :, 0, :], lam[:, :, 1, :], ALU.mult))
            dve.tensor_reduce(small[:, 16:18], lam_p, AX.X, ALU.add).then_inc(sem("args_full"), 1)
            take(dve, sem("func_full"))
            chain(dve.tensor_tensor(small[:, 20:21], small[:, 18:19], small[:, 19:20], ALU.subtract))
            chain(dve.tensor_scalar(small[:, 21:22], small[:, 20:21], 0.2, None, ALU.add))
            chain(dve.tensor_scalar(subln, par("subln_g"), 0.8, None, ALU.mult))

            def modulation(first, b):
                take(dve, for_dve[b])
                c0 = first
                chain(dve.tensor_tensor(mod[:, c0:c0 + 16], bank[b][:, 0:16], par("b_ada", c0, 16), ALU.add))
                dve.sem_inc(bank_free[b], 1)
                dve.sem_inc(sem("mod_ready"), 1)

            def gains(which, g):
                sc = mod[:, 24 * which + 8:24 * which + 16]
                chain(dve.tensor_scalar(gs[:, which, :], sc, 1.0, None, ALU.add))
                chain(dve.tensor_tensor(gs[:, which, :], gs[:, which, :], g, ALU.mult))

            def normed(which, n):
                dve.wait_ge(sem("rs_ready"), n)
                for k in range(KD):
                    dve.scalar_tensor_tensor(hT[:, k, :], xT[:, k, :], gs[:, which, k:k + 1], rs[:],
                                             ALU.mult, ALU.mult).then_inc(sem("scaled"), 1)

            modulation(0, 7)
            gains(0, par("norm1_g", 0, 8))
            normed(0, 1)
            for i in range(8):
                b = 4 + i % 2
                dve.wait_ge(sem("raw_ready"), i + 1)
                chain(dve.tensor_tensor(qkT[:, i, :], raw[:, i % 2, :], const("cosA"), ALU.mult))
                take(dve, for_dve[b])
                chain(dve.tensor_tensor(rtmp[:, i % 2, :], bank[b][:, :], const("sinA"), ALU.mult))
                dve.sem_inc(bank_free[b], 1)
                dve.tensor_tensor(qkT[:, i, :], qkT[:, i, :], rtmp[:, i % 2, :], ALU.add).then_inc(sem("qk_ready"), 1)
            modulation(16, 7)
            modulation(32, 7)
            gains(1, par("norm2_g", 0, 8))
            dve.wait_ge(sem("qk_ready"), 8)
            steps = [(h, q) for h in range(HEADS) for q in range(TT)]
            def maxima(i):
                for c in range(2):
                    b = 2 * (i % 2) + c
                    take(dve, for_dve[b])
                    st = stat[:, i % 2, :]
                    chain(dve.tensor_reduce(st[:, 4 + c:5 + c], bank[b][:, :], AX.X, ALU.max))
                    dve.tensor_scalar(st[:, c:c + 1], st[:, 4 + c:5 + c], -HD ** -0.5, None,
                                      ALU.mult).then_inc(sem(f"max_full{i % 2}{c}"), 1)
            def combine(i):
                take(dve, sem(f"probs_full{i % 2}"))
                st = stat[:, i % 2, :]
                pr = probs[:, i % 2]
                chain(dve.reciprocal(st[:, 6:8], st[:, 2:4]))
                chain(dve.tensor_tensor(st[:, 7:8], st[:, 7:8], small[:, 21:22], ALU.mult))
                chain(dve.tensor_scalar(pr[:, 1, :], pr[:, 1, :], st[:, 7:8], None, ALU.mult))
                take(dve, sem(f"wgt_free{i % 2}"))
                chain(dve.scalar_tensor_tensor(wgt[:, i % 2, :], pr[:, 0, :], st[:, 6:7], pr[:, 1, :],
                                               ALU.mult, ALU.subtract))
                dve.sem_inc(sem(f"wgt_full{i % 2}"), 1)
                dve.sem_inc(sem(f"probs_free{i % 2}"), 1)
            for i in range(len(steps) + 1):
                if i < len(steps):
                    maxima(i)
                if i >= 1:
                    combine(i - 1)
            for h in range(HEADS):
                dve.wait_ge(sem("rs_ready"), 2 + h)
                dve.scalar_tensor_tensor(mixT[:, h, :], mixT[:, h, :], subln, probs[:, h // 2, h % 2, :], ALU.mult,
                                         ALU.mult).then_inc(sem("mix_ready"), 1)
            dve.wait_ge(sem("inv_loaded"), 64)
            for g, w in enumerate(POOL_W):
                n = T + 2 * POOL_PAD
                src, k, into = u_pad[:, g, :], 1, 0
                while k < w:
                    n -= k
                    chain(dve.tensor_tensor(pool_a[:, into, 0:n], src[:, 0:n], src[:, k:k + n], ALU.add))
                    src, k, into = pool_a[:, into, :], 2 * k, 1 - into
                lo = POOL_PAD - w // 2
                chain(dve.tensor_tensor(pool_a[:, into, 0:T], src[:, lo:lo + T], inv_c[:, g, :], ALU.mult))
                chain(dve.tensor_tensor(pool_a[:, into, 0:T], pool_a[:, into, 0:T],
                                        u_pad[:, g, POOL_PAD:POOL_PAD + T], ALU.subtract))
                dve.tensor_copy(u_pad[:, g, 0:T], pool_a[:, into, 0:T]).then_inc(sem("pooled"), 1)
                dve.wait_ge(sem("pooled"), g + 1)
            for m in range(8):
                take(dve, for_dve[4 + m % 4])
                chain(dve.scalar_tensor_tensor(xT[:, m, :], bank[4 + m % 4][:, :], mod[:, 16 + m:17 + m], xT[:, m, :],
                                               ALU.mult, ALU.add))
                dve.sem_inc(bank_free[4 + m % 4], 1)
                dve.sem_inc(sem("x_mixed"), 1)
            normed(1, 6)
            take(dve, for_dve[0])
            bias = r1[:, 256:292].rearrange("p (a b) -> p a b", a=1).to_broadcast([P, TT, 36])
            chain(dve.tensor_tensor(lg, bank[0][:, 0:TT * 36].rearrange("p (a b) -> p a b", a=TT), bias, ALU.add))
            dve.sem_inc(bank_free[0], 1)
            iota = const("iota").rearrange("p (a b) -> p a b", a=1)

            def first_max(vals, n, hot, mx):
                chain(dve.tensor_reduce(mx, vals, AX.X, ALU.max))
                chain(dve.tensor_tensor(rt_t[:, :, 0:n], vals, mx.to_broadcast([P, TT, n]), ALU.is_lt))
                chain(dve.scalar_tensor_tensor(rt_t[:, :, 0:n], rt_t[:, :, 0:n], 100.0,
                                               iota[:, :, 0:n].to_broadcast([P, TT, n]), ALU.mult, ALU.add))
                chain(dve.tensor_reduce(rt_i, rt_t[:, :, 0:n], AX.X, ALU.min))
                chain(dve.tensor_tensor(hot, iota[:, :, 0:n].to_broadcast([P, TT, n]),
                                        rt_i.to_broadcast([P, TT, n]), ALU.is_equal))
            gl = lg[:, :, 0:4]
            first_max(gl, 4, ohg, m_g)
            el = lg[:, :, 4:36].rearrange("p t (g e) -> p t g e", g=4)
            for t in range(TT):
                chain(dve.tensor_tensor(rt_big, el[:, t], ohg[:, t, :].rearrange("p (g o) -> p g o", o=1).to_broadcast([P, 4, 8]), ALU.mult))
                chain(dve.tensor_reduce(e_in[:, t, :], rt_big.rearrange("p g e -> p e g"), AX.X, ALU.add))
            first_max(e_in, 8, oh1, m_1)
            chain(dve.scalar_tensor_tensor(e_in2, oh1, -1e30, e_in, ALU.mult, ALU.add))
            first_max(e_in2, 8, oh2, m_2)
            chain(dve.tensor_tensor(rt_arg.rearrange("p (t n) -> p t n", t=TT)[:, :, 0:4], gl, m_g.to_broadcast([P, TT, 4]), ALU.subtract))
            dve.tensor_tensor(rt_arg.rearrange("p (t n) -> p t n", t=TT)[:, :, 4:5], m_2, m_1, ALU.subtract).then_inc(sem("args_full"), 1)
            take(dve, sem("func_full"))
            ex = rt_exp.rearrange("p (t n) -> p t n", t=TT)
            den, w1, w2_ = rt_s[:, 0], rt_s[:, 1], rt_s[:, 2]
            chain(dve.tensor_reduce(den, ex[:, :, 0:4], AX.X, ALU.add))
            chain(dve.tensor_scalar(w1, ex[:, :, 4:5], 1.0, None, ALU.add))
            chain(dve.tensor_tensor(w1, w1, den, ALU.mult))
            chain(dve.reciprocal(w1, w1))
            chain(dve.tensor_tensor(w2_, w1, ex[:, :, 4:5], ALU.mult))
            for M, oh in ((M1, oh1), (M2, oh2)):
                for g in range(4):
                    chain(dve.tensor_tensor(M[:, :, 8 * g:8 * g + 8], oh, ohg[:, :, g:g + 1].to_broadcast([P, TT, 8]), ALU.mult))
            chain(dve.tensor_tensor(Ms, M1, M2, ALU.add))
            dve.sem_inc(sem("choices_full"), 1)
            take(dve, for_dve[0])
            chain(dve.tensor_copy(posn, bank[0][:, 0:TT * N_EXP].rearrange("p (t e) -> p t e", t=TT)))
            chain(dve.tensor_copy(cnt, bank[0][:, TT * N_EXP:(TT + 1) * N_EXP]))
            dve.sem_inc(bank_free[0], 1)
            chain(dve.tensor_scalar(nblk, cnt, float(CAP), None, ALU.is_gt))
            for full in range(2 * CAP, T, CAP):
                chain(dve.scalar_tensor_tensor(nblk, cnt, float(full), nblk, ALU.is_gt, ALU.add))
            chain(dve.tensor_tensor_scan(ends, ones[:, 0:N_EXP], nblk, 0.0, ALU.mult, ALU.add))
            ex32 = const("iota")
            chain(dve.tensor_tensor(base, ends, nblk, ALU.subtract))
            chain(dve.tensor_tensor(base, base, ex32, ALU.subtract))
            chain(dve.tensor_scalar(base, base, float(CAP), float((N_EXP - 1) * CAP), ALU.mult, ALU.add))
            over_t = lambda v: v.rearrange("p (o e) -> p o e", o=1).to_broadcast([P, TT, N_EXP])
            chain(dve.scalar_tensor_tensor(prod, posn, float(CAP), over_t(base), ALU.is_ge, ALU.mult))
            chain(dve.tensor_tensor(prod, prod, posn, ALU.add))
            chain(dve.scalar_tensor_tensor(posn, over_t(ex32), float(CAP), prod, ALU.mult, ALU.add))
            tok0 = CN["tok"][0]
            for k, (M, w) in enumerate(((M1, w1), (M2, w2_))):
                chain(dve.tensor_tensor(prod, M, posn, ALU.mult))
                chain(dve.tensor_reduce(dst_f[:, k, :].rearrange("p (t o) -> p t o", o=1), prod, AX.X, ALU.add))
                for c in range(2):
                    for field, value in ((0, c), (1, 2 + 2 * k + c)):
                        chain(dve.tensor_copy(rows[:, k, :, 4 * c + field], c_sb[:, tok0 + value * TT:tok0 + (value + 1) * TT]))
                    for field in (2, 3):
                        chain(dve.tensor_copy(rows[:, k, :, 4 * c + field:4 * c + field + 1].bitcast(F32), w))
            chain(dve.tensor_copy(dest.rearrange("p k t -> p (k t)"), dst_f.rearrange("p k t -> p (k t)")))
            dve.sem_inc(sem("routed"), 1)
            m_iota = const("iota")[:, 0:N_MORE].rearrange("p (m o) -> p m o", o=1).to_broadcast([P, N_MORE, N_EXP])
            m_ends = ends.rearrange("p (o e) -> p o e", o=1).to_broadcast([P, N_MORE, N_EXP])
            chain(dve.tensor_tensor(more_t, m_ends, m_iota, ALU.is_le))
            chain(dve.tensor_reduce(more_f[:, 0:N_MORE].rearrange("p (m o) -> p m o", o=1), more_t, AX.X, ALU.add))
            chain(dve.tensor_scalar(more_f[:, 0:N_MORE], more_f[:, 0:N_MORE], float(N_EXP - 1), None, ALU.min))
            chain(dve.tensor_copy(more_f[:, N_MORE:MORE], ends[:, N_EXP - 1:N_EXP]))
            chain(dve.tensor_copy(meta, more_f))
            dve.sem_inc(sem("routed"), 1)
            dve.wait_ge(sem("h_stored"), 16 * TT)

            def turned(j):
                take(dve, for_dve[0])
                chain(dve.tensor_copy(XT[j].rearrange("p k c n -> p (k c n)"), bank[0][:, :]))
                dve.sem_inc(bank_free[0], 1)
                dve.sem_inc(sem(f"xt_full{j}"), 1)
                dve.sem_inc(sem(f"x_free{j}"), 1)
            def hidden(j, block, ring_at):
                chain(dve.tensor_copy(cur_w, info[:, bass.ds(block, 1), :].rearrange("p a c -> p (a c)")))
                take(dve, sem(f"sg_full{j}"))
                take(dve, for_dve[3 + 2 * j])
                chain(dve.scalar_tensor_tensor(hid[:, j, :], bank[3 + 2 * j][:, 0:FE // 2], cur_w[:, 2:3].bitcast(F32),
                                               sg[:, j, :], ALU.mult, ALU.mult))
                dve.sem_inc(bank_free[3 + 2 * j], 1)
                dve.sem_inc(slot_free[ring_at + 1], 1)
                dve.sem_inc(sem(f"sg_free{j}"), 1)
                dve.sem_inc(sem(f"hid_full{j}"), 1)
            def hidden_turned(j):
                take(dve, for_dve[1])
                chain(dve.tensor_copy(hidT[:, j].rearrange("p f c n -> p (f c n)"), bank[1][:, 0:FE // 2]))
                dve.sem_inc(bank_free[1], 1)
                dve.sem_inc(sem(f"hidT_full{j}"), 1)
            turned(0)
            turned(1)
            hidden(0, 0, 0)
            chain.reset()
            with dve.Fori(0, N_EXP // 2 - 1) as pair:
                for j in range(2):
                    hidden_turned(j)
                    hidden(1 - j, 2 * pair + j + 1, 3 * (1 - j))
                    turned(j)
                chain.reset()
            hidden_turned(0)
            hidden(1, N_EXP - 1, 3)
            hidden_turned(1)
            chain.reset()
            n_more = dve.value_load(meta[0:1, N_MORE:MORE], min_val=0, max_val=N_MORE)
            with dve.Fori(0, N_MORE) as m:
                with dve.If(m < n_more):
                    turned(0)
                    hidden(0, m + N_EXP, 0)
                    hidden_turned(0)
                    chain.reset()
            dve.wait_ge(sem("const2_full"), 32)
            R96 = slice(0, QK_M)
            ang, turns = hT[R96, 0, :], hT[R96, 1, :]
            chain(dve.tensor_copy(ang, hT[R96, 7, :].bitcast(I32)))
            chain(dve.tensor_scalar(ang, ang, const2("invf")[R96], None, ALU.mult))
            MAGIC = 1.5 * 2.0 ** 23
            for dst, shift in ((sinM, 0.0), (cosM, 0.25)):
                chain(dve.tensor_scalar(turns, ang, float(1 / (2 * np.pi)), shift, ALU.mult, ALU.add))
                chain(dve.tensor_scalar(turns, turns, MAGIC, None, ALU.add))
                chain(dve.tensor_scalar(turns, turns, MAGIC, None, ALU.subtract))
                chain(dve.scalar_tensor_tensor(dst[R96], turns, -6.28125, ang, ALU.mult, ALU.add))
                chain(dve.scalar_tensor_tensor(dst[R96], turns, -0.00193500518798828125, dst[R96], ALU.mult, ALU.add))
                chain(dve.scalar_tensor_tensor(dst[R96], turns, -float(2 * np.pi - 6.28125 - 0.00193500518798828125), dst[R96], ALU.mult, ALU.add))
                if shift:
                    chain(dve.tensor_scalar(dst[R96], dst[R96], float(np.pi / 2), None, ALU.add))
                chain(dve.tensor_scalar(dst[R96], dst[R96], 3.1415925, -3.1415925, ALU.min, ALU.max))
            dve.sem_inc(sem("args_full"), 1)
            take(dve, sem("func_full"))
            for t in range(TT):
                if t == 0:
                    dve.wait_ge(sem("y_loaded"), 16 * TT)
                chain(dve.tensor_tensor(y_tok[:, t, 0, :], y_tok[:, t, 0, :], y_tok[:, t, 1, :], ALU.add))
                dve.sem_inc(sem("y_summed"), 1)
            for m in range(8):
                take(dve, for_dve[m % 4])
                chain(dve.scalar_tensor_tensor(xT[:, m, :], bank[m % 4][:, :], mod[:, 40 + m:41 + m], xT[:, m, :],
                                               ALU.mult, ALU.add))
                dve.sem_inc(bank_free[m % 4], 1)
                dve.sem_inc(sem("x_moe"), 1)
            dve.wait_ge(sem("rs_ready"), 7)
            for k in range(KD):
                chain(dve.scalar_tensor_tensor(xT[:, k, :], xT[:, k, :], par("final_g", k), rs[:], ALU.mult, ALU.mult))
            dve_second(dve, chain)


def constants():
    c = np.zeros((P, N_CN), np.float32)
    def put(name, a):
        c[:a.shape[0], CN[name][0]:CN[name][0] + a.shape[1]] = a
    put("ident", np.eye(P, dtype=np.float32))
    put("ones", np.ones((P, P), np.float32))
    b = np.zeros((P, P), np.float32); b[:64, :64] = 1; b[64:, 64:] = 1
    put("blk", b)
    rot = HD // 4
    half = rot // 2
    inv = np.float32(500000.0) ** (-np.arange(0, rot, 2, dtype=np.float32) / np.float32(rot))
    ang = np.arange(T, dtype=np.float32)[:, None] * inv[None]
    cos, sin = np.ones((P, T), np.float32), np.zeros((P, T), np.float32)
    R = np.zeros((P, P), np.float32)
    for o in (0, 64):
        cos[o:o + half] = np.cos(ang).T; cos[o + half:o + rot] = np.cos(ang).T
        sin[o:o + half] = np.sin(ang).T; sin[o + half:o + rot] = np.sin(ang).T
        for i in range(half):
            R[o + half + i, o + i] = -1.0
            R[o + i, o + half + i] = 1.0
    put("cosA", cos); put("sinA", sin); put("rotA", R)
    put("iota", np.tile(np.arange(32, dtype=np.float32), (P, 1)))
    put("lt", (np.arange(P)[:, None] < np.arange(P)[None]).astype(np.float32))
    tok = np.arange(P)[:, None] + P * np.arange(TT)[None]
    put("tok", np.concatenate([2 * tok, 2 * tok + 1] + [4 * tok + i for i in range(4)], axis=1).astype(np.float32))
    s = np.zeros((P, 8), np.float32); s[:, 0] = EPS; s[::32, 1] = 1.0
    put("scal", s)
    pos = np.arange(T)
    ic = np.stack([1.0 / (np.clip(pos + w - 1 - w // 2 + 1, 0, T) - np.clip(pos - w // 2, 0, T)) for w in POOL_W])
    return c, ic.astype(np.float32)


def constants2():
    c = np.zeros((P, N_C2), np.float32)
    def put(name, a):
        c[:a.shape[0], C2[name][0]:C2[name][0] + a.shape[1]] = a
    p, f = np.arange(P)[:, None], np.arange(P)[None]
    for name, m in (("LE", p <= f), ("LT", p < f), ("GE", p >= f), ("GT", p > f)):
        put(name, m.astype(np.float32))
        put("n" + name, np.where(m, 0.0, -30000.0).astype(np.float32))
    lev = []
    for l in range(LEVELS):
        s = 1 << l
        lev.append((p // (2 * s) == f // (2 * s)) & ((p // s) % 2 == 1) & ((f // s) % 2 == 0))
    put("lev0", np.concatenate([m.astype(np.float32) for m in lev], axis=1))
    put("lev1", np.concatenate([m.T.astype(np.float32) for m in lev], axis=1))
    put("reset", np.tile((np.arange(T) % CHUNK != 0).astype(np.float32), (P, 1)))
    half = ROPE // 2
    R = np.zeros((QK_M, QK_M), np.float32)
    for i in range(half):
        R[NOPE + half + i, NOPE + i] = -1.0
        R[NOPE + i, NOPE + half + i] = 1.0
    put("rotM", R)
    inv = np.float32(10000.0) ** (-np.arange(half, dtype=np.float32) / np.float32(half))
    put("invf", np.concatenate([np.zeros(NOPE, np.float32), inv, inv])[:, None])
    put("ln8", np.full((P, 1), np.log(GD ** -0.5), np.float32))
    put("eps_ln", np.full((P, 1), 64e-5, np.float32))
    return c


def second_inputs(a, put):
    def col(v, n):
        v = np.asarray(v).reshape(-1)
        if v.size < n * P:
            v = np.concatenate([v, np.zeros(n * P - v.size, v.dtype)])
        return v.reshape(n, P).T
    par, row = [], []
    for l in range(LAYERS):
        g = lambda n: np.asarray(a[n + "_2"])[l]
        conv = g("gdn_conv").reshape(5, 9, P).transpose(2, 1, 0).reshape(P, 45)
        par.append(np.concatenate([
            col(g("norm_g"), 8), conv, col(np.tile(g("gdn_norm_g"), 2), 1), col(g("mla_q_norm_g"), 2),
            col(g("mla_kv_norm_g"), 1), col(g("rwkv_mu")[0], 7), col(g("rwkv_mu")[1], 7), col(g("rwkv_k_k"), 2),
            col(g("rwkv_k_a"), 2), col(g("rwkv_r_k"), 2), col(g("rwkv_ln_g"), 2), col(g("rwkv_ln_b"), 2),
            col(g("rwkv_w0"), 4), col(g("rwkv_a0"), 4)], axis=1))
        row.append(np.concatenate([g("gdn_a_log").reshape(-1), g("gdn_dt_bias").reshape(-1)]))
    w = {n: put(n + "_2", a[n + "_2"]) for n in ("w_in", "w_out", "mla_w_uq", "mla_w_ukv", "rwkv_w2", "rwkv_a2", "positions")}
    w["par"] = put("par2", np.stack(par))
    w["row"] = put("row2", np.stack(row))
    w["cn"] = put("cn2", constants2())
    return w


def kernel(x, c, w_ada, b_ada, norm1_g, w_in, lambda_q1, lambda_k1, lambda_q2, lambda_k2, subln_g, w_pool,
           pool_scale, w_out, norm2_g, w_router_group, b_router_group, w_router_expert, b_router_expert,
           w_gate, w_up, w_down, final_g, final_norm_g_2, **rest):
    import concourse.bacc as bacc
    from concourse.bass_utils import run_bass_kernel_spmd
    nc = bacc.Bacc("TRN2", target_bir_lowering=False, num_devices=1)
    arrays = {}
    def put(name, a):
        a = np.ascontiguousarray(a)
        arrays[name] = a
        return nc.dram_tensor(name, a.shape, mybir.dt.from_np(a.dtype), kind="ExternalInput").ap()
    def col(a):
        return np.asarray(a).reshape(-1, P).T
    par1 = np.concatenate([col(norm1_g), col(b_ada), col(norm2_g), col(final_g), col(pool_scale), col(subln_g), col(c),
                           col(final_norm_g_2)], axis=1)
    row1 = np.concatenate([np.asarray(a).reshape(1, -1) for a in (lambda_q1, lambda_k1, lambda_q2, lambda_k2,
                           b_router_group, b_router_expert)], axis=1)
    cn, ic = constants()
    out = nc.dram_tensor("out", (D, T), F32, kind="ExternalOutput").ap()
    build(nc, put("xT_in", np.asarray(x)[0].T), put("par1", par1), put("row1", row1), put("cn", cn), put("invcnt", ic),
          put("w_ada", w_ada), put("w_in", w_in), put("w_pool", w_pool), put("w_out", w_out), put("w_rg", w_router_group),
          put("w_re", w_router_expert), put("w_gate", w_gate), put("w_up", w_up), put("w_down", w_down), second_inputs(rest, put), out)
    r = run_bass_kernel_spmd(nc, [arrays], core_ids=[0])
    return np.ascontiguousarray(np.asarray(r.results[0]["out"]).T)[None]
```
